# Optimizing a Trainium2 kernel written in Bass

```python
import jax, jax.numpy as jnp
from jax import lax
import numpy as np

D_MODEL = 2048
BATCH = 1
SEQ = 256
DEPTH = 2
DEC_BATCH = 8
DEC_SEQ = 1
PAST_LEN = 2048
PAGE_SIZE = 128

N_EVEN = (DEPTH + 1) // 2
N_ODD = DEPTH // 2
EPS = 1e-6
NEG_INF = -1e30
A_HEADS = 16
A_KV_HEADS = 4
A_GROUP = A_HEADS // A_KV_HEADS
HEAD_DIM = 64
A_WIDTH = A_HEADS * HEAD_DIM
A_KV_WIDTH = A_KV_HEADS * HEAD_DIM
WINDOW = 128
SWA_BLOCK = 128
ROPE_THETA = 10000.0
CONV_DIM = D_MODEL // 2
CONV_W = 3
GLA_HEADS = 4
GLA_WIDTH = D_MODEL // 2
GLA_DV = GLA_WIDTH // GLA_HEADS
GLA_DK = GLA_DV // 2
GLA_K_WIDTH = GLA_HEADS * GLA_DK
GLA_RANK = 16
GLA_TAU = 16.0
GLA_CHUNK = 64
POOL_DIM = D_MODEL // 2
POOL_WINDOWS = (2, 4, 8, 16)
POOL_GROUPS = 4
POOL_GDIM = POOL_DIM // POOL_GROUPS
POOL_BUF = 15
D_FF = -(-8 * D_MODEL // (3 * 256)) * 256
EVEN_IN = A_WIDTH + 2 * A_KV_WIDTH + 3 * CONV_DIM
EVEN_OUT = A_WIDTH + CONV_DIM
ODD_IN = 2 * GLA_K_WIDTH + 2 * GLA_WIDTH + GLA_RANK + POOL_DIM
ODD_OUT = GLA_WIDTH + POOL_DIM

kernel_name = 'hybrid_swa_conv_gla_pool_decode_step'

def rms_norm(x, g):
    x32 = x.astype(jnp.float32)
    y = x32 * lax.rsqrt(jnp.mean(x32 * x32, axis=-1, keepdims=True) + EPS)
    return (y * g.astype(jnp.float32)).astype(x.dtype)

def rope(x, pos):
    half = HEAD_DIM // 2
    inv = jnp.power(ROPE_THETA, -jnp.arange(half, dtype=jnp.float32) / half)
    ang = pos.astype(jnp.float32)[:, None] * inv[None, :]
    cos = jnp.cos(ang)[:, None, :]
    sin = jnp.sin(ang)[:, None, :]
    x32 = x.astype(jnp.float32)
    x1, x2 = x32[..., :half], x32[..., half:]
    return jnp.concatenate([x1 * cos - x2 * sin, x2 * cos + x1 * sin], axis=-1).astype(x.dtype)

def sink_attention(q, k, v, mask, sinks):
    s = jnp.einsum('...qhgd,...khd->...hgqk', q, k).astype(jnp.float32) * (HEAD_DIM ** -0.5)
    s = jnp.where(mask[..., None, None, :, :], s, NEG_INF)
    sink = sinks.astype(jnp.float32).reshape(A_KV_HEADS, A_GROUP, 1, 1)
    m = jnp.maximum(jnp.max(s, axis=-1, keepdims=True), sink)
    p = jnp.exp(s - m)
    p = p / (jnp.sum(p, axis=-1, keepdims=True) + jnp.exp(sink - m))
    return jnp.einsum('...hgqk,...khd->...qhgd', p.astype(v.dtype), v)

def swa_prompt(q, k, v, sinks):
    B, T = q.shape[:2]
    nb = T // SWA_BLOCK
    qb = q.reshape(B, nb, SWA_BLOCK, A_KV_HEADS, A_GROUP, HEAD_DIM)

    def band(a):
        ab = a.reshape(B, nb, SWA_BLOCK, A_KV_HEADS, HEAD_DIM)
        prev = jnp.concatenate([jnp.zeros_like(ab[:, :1]), ab[:, :-1]], axis=1)
        return jnp.concatenate([prev, ab], axis=2)

    kb, vb = band(k), band(v)
    qpos = jnp.arange(nb)[:, None] * SWA_BLOCK + jnp.arange(SWA_BLOCK)[None, :]
    kpos = (jnp.arange(nb)[:, None] - 1) * SWA_BLOCK + jnp.arange(2 * SWA_BLOCK)[None, :]
    diff = qpos[:, :, None] - kpos[:, None, :]
    mask = (diff >= 0) & (diff <= WINDOW) & (kpos[:, None, :] >= 0)
    o = sink_attention(qb, kb, vb, mask, sinks)
    return o.reshape(B, T, A_WIDTH)

def swa_sample(q, k_new, v_new, k_cache, v_cache, sinks):
    B, Ts = q.shape[:2]
    Lc = k_cache.shape[1]
    keys = jnp.concatenate([k_cache.astype(k_new.dtype), k_new], axis=1)
    vals = jnp.concatenate([v_cache.astype(v_new.dtype), v_new], axis=1)
    qpos = PAST_LEN + jnp.arange(Ts)
    kpos = jnp.concatenate([PAST_LEN - Lc + jnp.arange(Lc), qpos])
    diff = qpos[:, None] - kpos[None, :]
    mask = (diff >= 0) & (diff <= WINDOW)
    qg = q.reshape(B, Ts, A_KV_HEADS, A_GROUP, HEAD_DIM)
    o = sink_attention(qg, keys, vals, mask, sinks)
    return o.reshape(B, Ts, A_WIDTH), keys[:, -Lc:], vals[:, -Lc:]

def short_conv(u, prev, w):
    T = u.shape[1]
    ext = jnp.concatenate([prev.astype(u.dtype), u], axis=1)
    y = ext[:, 0:T] * w[0]
    for j in range(1, CONV_W):
        y = y + ext[:, j:j + T] * w[j]
    return y, ext[:, -(CONV_W - 1):]

def pool_mix(u, prev, n_prev, w_pool, scale):
    B, T, _ = u.shape
    ext_raw = jnp.concatenate([prev.astype(u.dtype), u], axis=1)
    ext = ext_raw.astype(jnp.float32)
    cs = jnp.concatenate([jnp.zeros((B, 1, POOL_DIM), jnp.float32), jnp.cumsum(ext, axis=1)], axis=1)
    t_idx = jnp.arange(T)
    outs = []
    for g, w in enumerate(POOL_WINDOWS):
        lo, hi = g * POOL_GDIM, (g + 1) * POOL_GDIM
        s = cs[:, POOL_BUF + 1:POOL_BUF + 1 + T, lo:hi] - cs[:, POOL_BUF + 1 - w:POOL_BUF + 1 - w + T, lo:hi]
        cnt = jnp.minimum(w, n_prev + t_idx + 1).astype(jnp.float32)
        outs.append(s / cnt[None, :, None] - ext[:, POOL_BUF:, lo:hi])
    d = jnp.stack(outs, axis=2).astype(u.dtype)
    y = jnp.einsum('btgc,gcd->btgd', d, w_pool).reshape(B, T, POOL_DIM) * scale
    return y, ext_raw[:, -POOL_BUF:]

def gla_chunked(q, k, v, gk, s0):
    B, T, H, DK = q.shape
    DV = v.shape[-1]
    C = GLA_CHUNK
    N = T // C
    q, k, gk = (a.reshape(B, N, C, H, DK) for a in (q, k, gk))
    v = v.reshape(B, N, C, H, DV)
    b = jnp.cumsum(gk, axis=2)
    b_last = b[:, :, -1:]
    qd = q * jnp.exp(b)
    kd = k * jnp.exp(-b)
    att = jnp.einsum('bnchd,bnjhd->bnhcj', qd, kd)
    att = jnp.where(jnp.tril(jnp.ones((C, C), dtype=bool)), att, 0.0)
    o_intra = jnp.einsum('bnhcj,bnjhe->bnche', att, v)
    delta = jnp.einsum('bnjhd,bnjhe->bnhde', k * jnp.exp(b_last - b), v)
    decay = jnp.exp(b_last[:, :, 0])

    def step(S, xs):
        dec, dl = xs
        return dec[..., None] * S + dl, S

    s_final, s_starts = lax.scan(step, s0, (decay.swapaxes(0, 1), delta.swapaxes(0, 1)))
    o_inter = jnp.einsum('bnchd,bnhde->bnche', qd, s_starts.swapaxes(0, 1))
    return (o_intra + o_inter).reshape(B, T, H, DV), s_final

def gla_recurrent(q, k, v, gk, s0):
    def step(S, xs):
        qt, kt, vt, gt = xs
        S = jnp.exp(gt)[..., None] * S + kt[..., :, None] * vt[..., None, :]
        return S, jnp.einsum('bhd,bhde->bhe', qt, S)

    s_final, o = lax.scan(step, s0, tuple(a.swapaxes(0, 1) for a in (q, k, v, gk)))
    return o.swapaxes(0, 1), s_final

def gla_mixer(zq, zk, zv, zg, zr, s0, w_alpha_up, b_alpha, out_gain, chunked):
    B, T, _ = zq.shape
    q = zq.reshape(B, T, GLA_HEADS, GLA_DK).astype(jnp.float32) * (GLA_DK ** -0.5)
    k = zk.reshape(B, T, GLA_HEADS, GLA_DK).astype(jnp.float32)
    v = zv.reshape(B, T, GLA_HEADS, GLA_DV).astype(jnp.float32)
    gk = jax.nn.log_sigmoid((zr @ w_alpha_up + b_alpha).astype(jnp.float32)) / GLA_TAU
    gk = gk.reshape(B, T, GLA_HEADS, GLA_DK)
    fn = gla_chunked if chunked else gla_recurrent
    o, s = fn(q, k, v, gk, s0.astype(jnp.float32))
    o = rms_norm(o, out_gain).reshape(B, T, GLA_WIDTH).astype(zv.dtype) * jax.nn.silu(zg)
    return o, s.astype(s0.dtype)

def mixer_even(h, pos, k_cache, v_cache, conv_prev, cache_len, w_in, w_out, q_gain, k_gain, sinks, conv_w, is_prompt):
    B, T, _ = h.shape
    z = h @ w_in
    zq, zk, zv, zb, zc, zh = jnp.split(z, [A_WIDTH, A_WIDTH + A_KV_WIDTH, A_WIDTH + 2 * A_KV_WIDTH,
                                          A_WIDTH + 2 * A_KV_WIDTH + CONV_DIM,
                                          A_WIDTH + 2 * A_KV_WIDTH + 2 * CONV_DIM], axis=-1)
    q = rope(rms_norm(zq.reshape(B, T, A_HEADS, HEAD_DIM), q_gain), pos)
    k = rope(rms_norm(zk.reshape(B, T, A_KV_HEADS, HEAD_DIM), k_gain), pos)
    v = zv.reshape(B, T, A_KV_HEADS, HEAD_DIM)
    if is_prompt:
        attn = swa_prompt(q, k, v, sinks)
        new_k, new_v = k[:, -cache_len:], v[:, -cache_len:]
    else:
        attn, new_k, new_v = swa_sample(q, k, v, k_cache, v_cache, sinks)
    conv_y, new_conv = short_conv(zc * zh, conv_prev, conv_w)
    y = jnp.concatenate([attn, zb * conv_y], axis=-1) @ w_out
    return y, new_k, new_v, new_conv

def mixer_odd(h, gla_s0, pool_prev, pool_prev_valid, w_in, w_out, w_alpha_up, b_alpha, gla_gain, w_pool, pool_scale, is_prompt):
    z = h @ w_in
    o1 = GLA_K_WIDTH
    o2 = o1 + GLA_K_WIDTH
    o3 = o2 + GLA_WIDTH
    o4 = o3 + GLA_WIDTH
    o5 = o4 + GLA_RANK
    zq, zk, zv, zg, zr, zp = jnp.split(z, [o1, o2, o3, o4, o5], axis=-1)
    oc, new_s = gla_mixer(zq, zk, zv, zg, zr, gla_s0, w_alpha_up, b_alpha, gla_gain, is_prompt)
    od, new_pool = pool_mix(zp, pool_prev, pool_prev_valid, w_pool, pool_scale)
    y = jnp.concatenate([oc, od], axis=-1) @ w_out
    return y, new_s, new_pool

def swiglu(x, wg, wu, wd):
    return (jax.nn.silu(x @ wg) * (x @ wu)) @ wd

def run_trunk(x, pos, k_cache, v_cache, conv_st, gla_st, pool_st, pool_prev_valid, cache_len, prm, is_prompt):
    nk_l, nv_l, nc_l, ng_l, np_l = [], [], [], [], []
    for layer in range(DEPTH):
        i = layer // 2
        h = rms_norm(x, prm['norm_mix'][layer])
        if layer % 2 == 0:
            kc = None if is_prompt else k_cache[i]
            vc = None if is_prompt else v_cache[i]
            y, nk, nv, nc = mixer_even(h, pos, kc, vc, conv_st[i], cache_len,
                                       prm['w_in_even'][i], prm['w_out_even'][i], prm['q_norm'][i],
                                       prm['k_norm'][i], prm['attn_sinks'][i], prm['conv_w'][i], is_prompt)
            nk_l.append(nk)
            nv_l.append(nv)
            nc_l.append(nc)
        else:
            y, ns, npool = mixer_odd(h, gla_st[i], pool_st[i], pool_prev_valid,
                                     prm['w_in_odd'][i], prm['w_out_odd'][i], prm['w_alpha_up'][i],
                                     prm['b_alpha'][i], prm['gla_out_norm'][i], prm['w_pool'][i],
                                     prm['pool_scale'][i], is_prompt)
            ng_l.append(ns)
            np_l.append(npool)
        x = x + y
        x = x + swiglu(rms_norm(x, prm['norm_ffn'][layer]), prm['w_gate'][layer], prm['w_up'][layer], prm['w_down'][layer])
    return x, jnp.stack(nk_l), jnp.stack(nv_l), jnp.stack(nc_l), jnp.stack(ng_l), jnp.stack(np_l)

def setup_inputs(seed: int = 0) -> dict:
    key = jax.random.key(seed)
    ks = jax.random.split(key, 26)
    f32 = jnp.float32

    def nrm(k, shape, scale):
        return jax.random.normal(k, shape, f32) * scale

    lc = min(WINDOW, PAST_LEN)
    return {
        'x_prompt': nrm(ks[0], (BATCH, SEQ, D_MODEL), 1.0),
        'x_sample': nrm(ks[1], (DEC_BATCH, DEC_SEQ, D_MODEL), 1.0),
        'cache_swa_k': nrm(ks[2], (N_EVEN, DEC_BATCH, lc, A_KV_HEADS, HEAD_DIM), 1.0),
        'cache_swa_v': nrm(ks[3], (N_EVEN, DEC_BATCH, lc, A_KV_HEADS, HEAD_DIM), 1.0),
        'state_conv': nrm(ks[4], (N_EVEN, DEC_BATCH, CONV_W - 1, CONV_DIM), 1.0),
        'state_gla': nrm(ks[5], (N_ODD, DEC_BATCH, GLA_HEADS, GLA_DK, GLA_DV), 2.0),
        'state_pool': nrm(ks[6], (N_ODD, DEC_BATCH, POOL_BUF, POOL_DIM), 1.0),
        'norm_mix': 1.0 + nrm(ks[7], (DEPTH, D_MODEL), 0.05),
        'norm_ffn': 1.0 + nrm(ks[8], (DEPTH, D_MODEL), 0.05),
        'w_in_even': nrm(ks[9], (N_EVEN, D_MODEL, EVEN_IN), D_MODEL ** -0.5),
        'w_out_even': nrm(ks[10], (N_EVEN, EVEN_OUT, D_MODEL), EVEN_OUT ** -0.5),
        'q_norm': 1.0 + nrm(ks[11], (N_EVEN, HEAD_DIM), 0.05),
        'k_norm': 1.0 + nrm(ks[12], (N_EVEN, HEAD_DIM), 0.05),
        'attn_sinks': nrm(ks[13], (N_EVEN, A_HEADS), 0.5),
        'conv_w': nrm(ks[14], (N_EVEN, CONV_W, CONV_DIM), CONV_W ** -0.5),
        'w_in_odd': nrm(ks[15], (N_ODD, D_MODEL, ODD_IN), D_MODEL ** -0.5),
        'w_out_odd': nrm(ks[16], (N_ODD, ODD_OUT, D_MODEL), ODD_OUT ** -0.5),
        'w_alpha_up': nrm(ks[17], (N_ODD, GLA_RANK, GLA_K_WIDTH), GLA_RANK ** -0.5),
        'b_alpha': nrm(ks[18], (N_ODD, GLA_K_WIDTH), 0.1),
        'gla_out_norm': 1.0 + nrm(ks[19], (N_ODD, GLA_DV), 0.05),
        'w_pool': nrm(ks[20], (N_ODD, POOL_GROUPS, POOL_GDIM, POOL_GDIM), POOL_GDIM ** -0.5),
        'pool_scale': 1.0 + nrm(ks[21], (N_ODD, POOL_DIM), 0.1),
        'w_gate': nrm(ks[22], (DEPTH, D_MODEL, D_FF), D_MODEL ** -0.5),
        'w_up': nrm(ks[23], (DEPTH, D_MODEL, D_FF), D_MODEL ** -0.5),
        'w_down': nrm(ks[24], (DEPTH, D_FF, D_MODEL), D_FF ** -0.5),
    }

def reference(x_prompt, x_sample, cache_swa_k, cache_swa_v, state_conv, state_gla, state_pool,
              norm_mix, norm_ffn, w_in_even, w_out_even, q_norm, k_norm, attn_sinks, conv_w,
              w_in_odd, w_out_odd, w_alpha_up, b_alpha, gla_out_norm, w_pool, pool_scale,
              w_gate, w_up, w_down):
    prm = {'norm_mix': norm_mix, 'norm_ffn': norm_ffn, 'w_in_even': w_in_even, 'w_out_even': w_out_even,
           'q_norm': q_norm, 'k_norm': k_norm, 'attn_sinks': attn_sinks, 'conv_w': conv_w,
           'w_in_odd': w_in_odd, 'w_out_odd': w_out_odd, 'w_alpha_up': w_alpha_up, 'b_alpha': b_alpha,
           'gla_out_norm': gla_out_norm, 'w_pool': w_pool, 'pool_scale': pool_scale,
           'w_gate': w_gate, 'w_up': w_up, 'w_down': w_down}
    cache_len = cache_swa_k.shape[2]
    B, T = x_prompt.shape[:2]
    dt = x_prompt.dtype
    zero_conv = jnp.zeros((N_EVEN, B, CONV_W - 1, CONV_DIM), dt)
    zero_gla = jnp.zeros((N_ODD, B, GLA_HEADS, GLA_DK, GLA_DV), dt)
    zero_pool = jnp.zeros((N_ODD, B, POOL_BUF, POOL_DIM), dt)
    y_prompt, pk, pv, pc, pg, pp = run_trunk(x_prompt, jnp.arange(T), None, None, zero_conv, zero_gla, zero_pool,
                                             0, cache_len, prm, True)
    y_sample, sk, sv, sc, sg, sp = run_trunk(x_sample, PAST_LEN + jnp.arange(x_sample.shape[1]),
                                             cache_swa_k, cache_swa_v, state_conv, state_gla, state_pool,
                                             min(POOL_BUF, PAST_LEN), cache_len, prm, False)
    return (y_prompt, y_sample, pk, pv, pc, pg, pp, sk, sv, sc, sg, sp)


_drawn_inputs = setup_inputs


def setup_inputs(seed=0):
    import zlib

    import numpy as np

    out = dict(_drawn_inputs(seed))
    spreads = {}
    factors = {'q_norm': 8.0, 'attn_sinks': 8.0, 'gla_out_norm': 3.978}
    for name, (base, spread) in spreads.items():
        noise = np.random.default_rng([zlib.crc32(name.encode()), seed]).standard_normal(out[name].shape)
        drawn = base * np.exp(spread * noise) if base else spread * noise
        out[name] = __import__('jax').numpy.asarray(drawn.astype(out[name].dtype))
    for name, factor in factors.items():
        out[name] = (out[name] * factor).astype(out[name].dtype)
    return out
```

```python
from contextlib import ExitStack

import numpy as np

import concourse.bass as bass
from concourse import mybir

F32 = mybir.dt.float32
F32R = mybir.dt.float32r
BF16 = mybir.dt.bfloat16
I32 = mybir.dt.int32
ALU = mybir.AluOpType
ACT = mybir.ActivationFunctionType
AX = mybir.AxisListType.X

P = 128
D = 2048
TP, NB = 256, 8
T = TP + NB
KC = D // P
FF = 5632
FC = FF // P
HD, NH, NKV, GRP = 64, 16, 4, 4
PAST = 2048
EPS = 1e-6
GH, GDK, GDV = 4, 128, 256
CH = 64
NCH = TP // CH
WIN = (2, 4, 8, 16)
PB = 15
COLS = 512
RING = 4
AHEAD = 3

IN_UNITS = KC // 2
EVEN_GROUPS = 9
U_EVEN = 0
U_OUT_E = U_EVEN + EVEN_GROUPS * IN_UNITS
U_FFN0 = U_OUT_E + 4 * IN_UNITS
GU_ITERS = FF // COLS
DN_UNITS = FC // 2
U_DN0 = U_FFN0 + GU_ITERS * 2 * IN_UNITS
U_ODD = U_DN0 + 4 * DN_UNITS
U_OUT_O = U_ODD + 8 * IN_UNITS + 2
U_FFN1 = U_OUT_O + 4 * IN_UNITS
U_DN1 = U_FFN1 + GU_ITERS * 2 * IN_UNITS
U_END = U_DN1 + 4 * DN_UNITS

G_EVEN = 4
G_OUT_E = G_EVEN + EVEN_GROUPS
G_FFN0 = G_OUT_E + 4
G_DN0 = G_FFN0 + 2 * GU_ITERS
G_ODD = G_DN0 + 4
G_OUT_O = G_ODD + 9
G_FFN1 = G_OUT_O + 4
G_DN1 = G_FFN1 + 2 * GU_ITERS

V_MIX, V_FFN, V_CONV, V_PSC, V_BAL, V_GLA, V_Q, V_K = 0, 32, 64, 88, 96, 100, 102, 103
NVEC = 104

C_ID, C_BLK, C_ROT, C_COS, C_SIN, C_MASK, C_TRI, C_CNT = 0, 128, 256, 384, 648, 912, 1168, 1232
C_ALL = C_CNT + 4 * 16

OUT_E_ORDER = (4, 5, 6, 0, 1, 2, 3, 7)
ATTN_UNITS = (3, 4, 5, 6)
OUT_O_ORDER = (4, 5, 6, 7, 0, 1, 2, 3)
ZR = 3072
ODD_COLS = (0, None, 512, 1024, 1536, 3088, 3600, 2048, 2560)
ODD_FIRST = (0, 8, 10, 18, 26, 34, 42, 50, 58)


def constants():
    c = np.zeros((P, C_ALL), np.float32)
    r = np.arange(P)
    c[:, C_ID:C_ID + P] = np.eye(P)
    c[:, C_BLK:C_BLK + P] = (r[:, None] // HD) == (r[None, :] // HD)
    half = HD // 2
    for m in range(P):
        if m % HD < half:
            c[m + half, C_ROT + m] = -1.0
        else:
            c[m - half, C_ROT + m] = 1.0
    inv = np.power(np.float32(10000.0), -np.arange(half, dtype=np.float32) / np.float32(half))
    pos = np.concatenate([np.arange(TP), np.full(NB, PAST)]).astype(np.float32)
    ang = (pos[None, :] * inv[r % half][:, None]).astype(np.float32)
    c[:, C_COS:C_COS + T] = np.cos(ang)
    c[:, C_SIN:C_SIN + T] = np.sin(ang)
    k = np.arange(P)
    c[:, C_MASK:C_MASK + P] = np.where(k[None, :] >= r[:, None], 0.0, -1e30)
    c[:, C_MASK + P:C_MASK + 2 * P] = np.where(k[None, :] <= r[:, None], 0.0, -1e30)
    c[:, C_TRI:C_TRI + CH] = (r % CH)[:, None] <= np.arange(CH)[None, :]
    for g, w in enumerate(WIN):
        c[:, C_CNT + 16 * g:C_CNT + 16 * g + 16] = np.float32(1.0) / np.minimum(w, np.arange(16) + 1).astype(np.float32)
    return c


def decoder_step(nc, a, o):
    (y_prompt, y_sample, o_kp, o_vp, o_cp, o_gp, o_pp, o_ks, o_vs, o_cs, o_gs, o_ps) = o
    w_even, w_out_e = a["w_in_even"][0], a["w_out_even"][0]
    w_odd, w_out_o = a["w_in_odd"][0], a["w_out_odd"][0]

    ctx = ExitStack()
    with ctx:
        def sem(name):
            return ctx.enter_context(nc.semaphore(name))

        used = {}

        def put(name, shape, at, dt=F32):
            size = 1
            for s in shape[1:]:
                size *= s
            size *= 2 if dt == BF16 else 4
            used[name] = (at, at + size)
            return nc.alloc_sbuf_tensor_at(name, shape, dt, offset=at)

        def after(name):
            return (used[name][1] + 31) // 32 * 32

        x = put("x", [P, KC, T], 1024)
        xh = put("xh", [P, KC, T], after("x"), F32R)
        xl = put("xl", [P, KC, T], after("xh"), F32R)
        raw = put("raw", [P, RING, 2 * COLS], after("xl"))
        whi = put("whi", [P, RING, 2 * COLS], after("raw"), F32R)
        wlo = put("wlo", [P, RING, 2 * COLS], after("whi"), F32R)
        hh = put("hh", [P, FC, T], after("wlo"), F32R)
        hl = put("hl", [P, FC, T], after("hh"), F32R)
        acc4 = put("acc4", [P, 4, T], after("hl"))
        sq4 = put("sq4", [P, 4, T], after("acc4"))
        gbuf = put("gbuf", [P, 4, T], after("sq4"))
        ubuf = put("ubuf", [P, 4, T], after("gbuf"))
        rstd = put("rstd", [P, T], after("ubuf"))
        std = put("std", [P, T], after("rstd"))
        ones = put("ones", [P, P], after("std"))
        cst = put("cst", [P, C_ALL], after("ones"))
        vec = put("vec", [P, NVEC], after("cst"))
        maskb = put("maskb", [P, 2 * P], after("vec"), BF16)
        identb = put("identb", [P, P], after("maskb"), BF16)
        eps = put("eps", [P, 1], after("identb"))
        small = put("small", [P, 64], after("eps"))
        spare = after("small")
        assert spare <= 229344
        ident = cst[:, C_ID:C_ID + P]
        blk = cst[:, C_BLK:C_BLK + P]
        rot = cst[:, C_ROT:C_ROT + P]
        ya, yb = used["hh"][0], used["hl"][0]
        reg_a, end_a = ya + KC * T * 4, used["hh"][1]
        reg_b, end_b = yb + KC * T * 4, used["hl"][1]

        xtok = put("xtok", [P, 2, D], reg_a)
        xtok_s = put("xtok_s", [NB, D], after("xtok"))
        vrow = put("vrow", [NVEC, P], after("xtok_s"))
        assert after("vrow") <= end_a

        kc = put("kc", [P, NB, 256], reg_b)
        prob = put("prob", [P, 2, 4, 256], reg_b)
        vc = put("vc", [P, NB, 256], after("kc"))
        kcT = put("kcT", [P, 2 * NB, P], after("vc"))
        cst_rows = put("cst_rows", [16, 1024], after("kcT"))
        assert after("cst_rows") <= end_b
        qk = put("qk", [P, 10, T], reg_a)
        vF = put("vF", [P, 2, T], after("qk"))
        kT1 = put("kT1", [P, 256], after("vF"))
        vT = put("vT", [P, 2, 256], after("kT1"))
        kvS = put("kvS", [NB, 512], after("vT"))
        pT = put("pT", [P, 2, 512], after("kvS"))
        conv_in = put("conv_in", [P, 4, 282], after("pT"))
        assert after("conv_in") <= end_a
        conv_tok = put("conv_tok", [NB, 2, COLS], spare)
        conv_st = put("conv_st", [P, 8, 16], after("conv_tok"))
        sT = put("sT", [P, P], after("conv_st"))
        pS = put("pS", [P, 132], after("sT"))
        pTS = put("pTS", [P, 192], after("pS"))
        prod = put("prod", [P, 64], after("pTS"))
        dg = put("dg", [P, 64], after("prod"))
        sink_row = put("sink_row", [P, 16], after("dg"))
        sink_col = put("sink_col", [P, 1], after("sink_row"))
        nsink_row = put("nsink_row", [P, 16], after("sink_col"))
        nsink_col = put("nsink_col", [P, 1], after("nsink_row"))
        assert after("nsink_col") <= 229344, after("nsink_col")

        yh, yl = hh, hl

        vtok = put("vtok", [P, 2, 1024], ya)
        oF = put("oF", [P, 8, T], yb)
        qg = put("qg", [P, 4, T], reg_a)
        kg = put("kg", [P, 4, T], after("qg"))
        vf = put("vf", [P, 4, T], after("kg"))
        ext = put("ext", [P, 4, 399], used["kg"][0])
        assert after("ext") <= after("vf")
        vS = put("vS", [NB, 1024], after("vf"))
        ktS = put("ktS", [NB, 512], after("vS"))
        kdiag = put("kdiag", [NB, 2, 512], after("ktS"))
        attS = put("attS", [P, 8, CH], after("kdiag"))
        zr = put("zr", [16, T], after("attS"))
        qsamp = put("qsamp", [P, 4, NB], after("zr"))
        rst2 = put("rst2", [P, 2, T], after("qsamp"))
        assert after("rst2") <= end_a, (after("rst2"), end_a)
        k2t = put("k2t", [P, 2, 512], reg_b)
        st = put("st", [P, 2, 4, 256], after("k2t"))
        wpool = put("wpool", [P, 8, 256], after("k2t"))
        sgl = put("sgl", [P, 4, 2, 256], after("st"))
        d0 = put("d0", [P, 4, T], after("sgl"))
        tree = put("tree", [P, 2, 2, 272], after("sgl"))
        dmix = put("dmix", [P, 2, T], after("tree"))
        wup = put("wup", [16, 512], after("dmix"))
        assert after("wup") <= end_b, (after("wup"), end_b)
        prow = put("prow", [120, 1024], spare)
        ptok = put("ptok", [16, 2, COLS], after("prow"))
        assert after("ptok") <= 229344, after("ptok")

        ps = ctx.enter_context(nc.psum_tensor("ps", [P, 8, 512], F32))
        psf = ps[:, :, :].rearrange("p b n -> p (b n)")

        raw_full = [sem(f"raw_full{s}") for s in range(RING)]
        raw_up = [sem(f"raw_up{s}") for s in range(RING)]
        hi_done = sem("hi_done")
        lo_done = sem("lo_done")
        units_done = sem("units_done")
        tile_done = sem("tile_done")
        evac_t = sem("evac_t")
        evac_g = sem("evac_g")
        head_done = sem("head_done")
        xh_done = sem("xh_done")
        xl_done = sem("xl_done")
        sq_done = sem("sq_done")
        acc_done = sem("acc_done")
        ss_done = sem("ss_done")
        std_done = sem("std_done")
        rstd_done = sem("rstd_done")
        gate_half = sem("gate_half")
        silu_done = sem("silu_done")
        up_scaled = sem("up_scaled")
        h_ready = sem("h_ready")
        hh_done = sem("hh_done")
        hid_done = sem("hid_done")
        d_x = sem("d_x")
        d_cst = sem("d_cst")
        d_vec = sem("d_vec")
        d_even = sem("d_even")
        d_odd = sem("d_odd")
        d_out = sem("d_out")
        ms_done = sem("ms_done")
        vecT = sem("vecT")
        vec_ok = sem("vec_ok")
        maskb_ok = sem("maskb_ok")
        dv = sem("dv")
        kcT_ps = sem("kcT_ps")
        kcT_ok = sem("kcT_ok")
        cst_ps = sem("cst_ps")
        cst_ok = sem("cst_ok")
        qsq = sem("qsq")
        qss = sem("qss")
        qstd = sem("qstd")
        qnorm = sem("qnorm")
        qrot = sem("qrot")
        qk_ready = sem("qk_ready")
        kv_ps = sem("kv_ps")
        kv_tok = sem("kv_tok")
        sc_done = sem("sc_done")
        negm_done = sem("negm_done")
        exp_done = sem("exp_done")
        rec_done = sem("rec_done")
        pn_done = sem("pn_done")
        pt_done = sem("pt_done")
        pT_ok = sem("pT_ok")
        pv_done = sem("pv_done")
        oh_done = sem("oh_done")
        o_done = sem("o_done")
        sS_done = sem("sS_done")
        sT_ok = sem("sT_ok")
        sR_done = sem("sR_done")
        nS_done = sem("nS_done")
        eS_done = sem("eS_done")
        pS_ok = sem("pS_ok")
        pTS_ps = sem("pTS_ps")
        pTS_ok = sem("pTS_ok")
        pvS = sem("pvS")
        prod_ok = sem("prod_ok")
        oS_ok = sem("oS_ok")
        conv_u = sem("conv_u")
        conv_y = sem("conv_y")
        conv_h = sem("conv_h")
        conv_l = sem("conv_l")
        ct_ps = sem("ct_ps")
        ct_ok = sem("ct_ok")
        zr_ok = sem("zr_ok")
        gk_ps = sem("gk_ps")
        zb_ok = sem("zb_ok")
        ln_ok = sem("ln_ok")
        b_ok = sem("b_ok")
        eb_ok = sem("eb_ok")
        kd_ok = sem("kd_ok")
        df_ok = sem("df_ok")
        edf_ok = sem("edf_ok")
        k2_ok = sem("k2_ok")
        att_ps = sem("att_ps")
        att_ok = sem("att_ok")
        k2t_ps = sem("k2t_ps")
        k2t_ok = sem("k2t_ok")
        vf_ok = sem("vf_ok")
        vt_ps = sem("vt_ps")
        vt_ok = sem("vt_ok")
        dl_ps = sem("dl_ps")
        st_ok = sem("st_ok")
        go_ps = sem("go_ps")
        go_ok = sem("go_ok")
        d_gs = [sem(f"d_gs{k}") for k in range(4)]
        d_gso = [sem(f"d_gso{k}") for k in range(4)]
        d_go = [sem("d_go0"), sem("d_go1")]
        kdg = sem("kdg")
        kv_o = sem("kv_o")
        sg_ok = sem("sg_ok")
        so_ps = sem("so_ps")
        osq = sem("osq")
        oss = sem("oss")
        ostd = sem("ostd")
        zg_ok = sem("zg_ok")
        sg_silu = sem("sg_silu")
        oc_ok = sem("oc_ok")
        och = sem("och")
        ocl = sem("ocl")
        pst_ps = sem("pst_ps")
        pst_ok = sem("pst_ok")
        ext_ok = sem("ext_ok")
        tree_ok = sem("tree_ok")
        dmix_ok = sem("dmix_ok")
        pm_ps = sem("pm_ps")
        pmh = sem("pmh")
        pml = sem("pml")
        po_ps = sem("po_ps")
        po_ok = sem("po_ok")
        d_wp = sem("d_wp")
        d_prow = sem("d_prow")
        d_pt = [sem("d_pt0"), sem("d_pt1")]
        d_ct = sem("d_ct")
        d_kc = sem("d_kc")
        ac = sem("ac")
        pl = sem("pl")
        padc = sem("padc")
        d0_ok = sem("d0_ok")
        pad_ok = sem("pad_ok")
        y_ps = sem("y_ps")
        y_ok = sem("y_ok")
        d_y = sem("d_y")

        def at_turn(eng, i, step, first):
            if i is None:
                return first
            return i * step + first if isinstance(i, int) else eng.snap(i * step + first)

        def pieces(buf, n, split=False):
            slot = buf[:, n % RING, :]
            if n >= U_EVEN + 2 * IN_UNITS:
                return [slot]
            order = "p (q h d) -> p h q d" if split else "p (h q d) -> p h q d"
            return [slot[:, k * COLS:(k + 1) * COLS].rearrange(order, h=2, q=4) for k in range(2)]

        def beyond(n, i, step):
            return n + (i * step if isinstance(i, int) else 0) >= U_END

        def split_hi(act, n, i=None, step=0, up=None):
            if beyond(n, i, step):
                return
            landed = at_turn(act, i, 16 * step // RING, 16 * (n // RING + 1))
            if up is not None:
                up = at_turn(act, i, up[1], up[0])
            free = at_turn(act, i, step, n - RING + 1)
            act.wait_ge(raw_full[n % RING], landed)
            if up is not None:
                act.wait_ge(raw_up[n % RING], up)
            if n >= RING:
                act.wait_ge(units_done, free)
            for dst, src in zip(pieces(whi, n, True), pieces(raw, n)):
                ins = act.activation(dst, src, ACT.Copy)
            ins.then_inc(hi_done, 1)

        def split_lo(dve, n, i=None, step=0):
            if beyond(n, i, step):
                return
            dve.wait_ge(hi_done, at_turn(dve, i, step, n + 1))
            for dst, src, hi in zip(pieces(wlo, n, True), pieces(raw, n), pieces(whi, n, True)):
                ins = dve.tensor_tensor(dst, src, hi.bitcast(F32), ALU.subtract)
            ins.then_inc(lo_done, 1)

        block = ctx.enter_context(nc.Block())

        @block.sync
        def _(sp):
            def load(n, w, row, col, i=None, step=0, up=None):
                p = P if up is None else HD
                src = [w[r:r + 2 * p, :].rearrange("(k p) n -> p k n", p=p)[:, :, bass.ds(col, COLS)] for r in (row, up or row)]
                if n >= RING:
                    sp.wait_ge(lo_done, at_turn(sp, i, step, n - RING + 1))
                dst = raw[:, n % RING, :].rearrange("p (k n) -> p k n", k=2)
                sp.dma_start(dst[0:p], src[0]).then_inc(raw_full[n % RING], 16)
                if up is not None:
                    sp.dma_start(dst[p:P], src[1]).then_inc(raw_up[n % RING], 16)

            for g in range(3):
                for j in range(IN_UNITS):
                    load(U_EVEN + IN_UNITS * g + j, w_even, 2 * P * j, COLS * g)
            n0 = U_EVEN + 3 * IN_UNITS
            with sp.Fori(0, 2, 1) as i:
                for g, base in enumerate((2560, 3584, 1536)):
                    col = sp.snap(i * COLS + base)
                    for j in range(IN_UNITS):
                        load(n0 + IN_UNITS * g + j, w_even, 2 * P * j, col, i=i, step=3 * IN_UNITS)
            with sp.Fori(0, 2, 1) as i:
                for h in range(2):
                    col = i * (2 * COLS) + COLS * h
                    for j in range(IN_UNITS):
                        n = U_OUT_E + IN_UNITS * h + j
                        if j not in ATTN_UNITS:
                            load(n, w_out_e, 2 * P * OUT_E_ORDER[j], col, i=i, step=2 * IN_UNITS)
                            continue
                        c = 2 * OUT_E_ORDER[j]
                        lower = (8 * (c // 4) + c % 4) * HD
                        load(n, w_out_e, lower, col if lower else (i * 2 + h) * COLS, i=i, step=2 * IN_UNITS, up=lower + 4 * HD)

            def ffn(layer, n_gu, n_dn):
                with sp.Fori(0, GU_ITERS, 1) as i:
                    col = sp.snap(i * COLS)
                    for h, w in enumerate((a["w_gate"][layer], a["w_up"][layer])):
                        for j in range(IN_UNITS):
                            load(n_gu + IN_UNITS * h + j, w, 2 * P * j, col, i=i, step=2 * IN_UNITS)
                with sp.Fori(0, 2, 1) as i:
                    for h in range(2):
                        col = i * (2 * COLS) + COLS * h
                        for j in range(DN_UNITS):
                            load(n_dn + DN_UNITS * h + j, a["w_down"][layer], 2 * P * j, col, i=i, step=2 * DN_UNITS)

            ffn(0, U_FFN0, U_DN0)
            n = U_ODD
            for base in ODD_COLS:
                if base is None:
                    for j in range(2):
                        sp.wait_ge(lo_done, n - RING + 1)
                        sp.dma_start(raw[:, n % RING, :].rearrange("p (k n) -> p k n", k=8),
                                     w_odd[8 * P * j:8 * P * (j + 1), ZR:ZR + P].rearrange("(k p) n -> p k n", p=P)
                                     ).then_inc(raw_full[n % RING], 16)
                        n += 1
                else:
                    for j in range(IN_UNITS):
                        load(n, w_odd, 2 * P * j, base)
                        n += 1
            assert n == U_OUT_O
            with sp.Fori(0, 2, 1) as i:
                for h in range(2):
                    col = i * (2 * COLS) + COLS * h
                    for j in range(IN_UNITS):
                        row = 2 * P * OUT_O_ORDER[j]
                        load(U_OUT_O + IN_UNITS * h + j, w_out_o, row, col if row else (i * 2 + h) * COLS, i=i, step=2 * IN_UNITS)
            ffn(1, U_FFN1, U_DN1)

        @block.tensor
        def _(pe):
            def unit(n, yhi, ylo, k0, bank, first, last, i=None, step=0, taken=None, single=False):
                pe.wait_ge(lo_done, at_turn(pe, i, step, n + 1))
                s = n % RING
                for t in range(4):
                    if taken is not None and t < 3:
                        pe.wait_ge(evac_t, taken[0] + t)
                    if taken is not None and t == 3:
                        pe.wait_ge(evac_g, taken[1])
                    for kk in range(2):
                        c = kk * COLS + t * P
                        for m, (w, r) in enumerate(((whi, yhi), (whi, ylo), (wlo, yhi))):
                            mm = pe.matmul(ps[:, bank + t, 0:T], w[:, s, c:c + P], r[:, k0 + kk, :],
                                           start=first and kk == 0 and m == 0, stop=last and kk == 1 and m == 2)
                    if single and last and t < 3:
                        mm.then_inc(tile_done, 1)
                mm.then_inc(units_done, 1)

            def norm_sum(m):
                pe.wait_ge(acc_done, 4 * m + 4)
                for t in range(4):
                    mm = pe.matmul(ps[:, 4, 0:T], ones[:, :], acc4[:, t, :], start=t == 0, stop=t == 3)
                mm.then_inc(ss_done, 1)

            pe.wait_ge(d_cst, 16)
            pe.wait_ge(d_vec, 16 * 8)
            pe.transpose(ps[:, 7, 0:NVEC], vrow[:, :], ident[0:NVEC, 0:NVEC]).then_inc(vecT, 1)
            pe.wait_ge(d_x, 48)
            for g in range(4):
                if g == 1:
                    pe.wait_ge(vec_ok, 1)
                if g >= 2:
                    pe.wait_ge(evac_g, g - 1)
                for t in range(4):
                    c, b = 4 * g + t, 4 * (g % 2) + t
                    for q in range(2):
                        pe.transpose(ps[:, b, q * P:(q + 1) * P], xtok[:, q, c * P:(c + 1) * P], ident)
                    mm = pe.transpose(ps[:, b, TP:T], xtok_s[:, c * P:(c + 1) * P], ident[0:NB, 0:NB])
                mm.then_inc(head_done, 1)

            def cache_T():
                pe.wait_ge(d_kc, 16)
                pe.wait_ge(evac_g, 4)
                for b in range(NB):
                    for p in range(2):
                        q = 2 * b + p
                        mm = pe.transpose(psf[:, 4 * 512 + q * P:4 * 512 + (q + 1) * P], kc[:, b, p * P:(p + 1) * P], ident)
                mm.then_inc(kcT_ps, 1)

            def conv_state_T():
                pe.wait_ge(d_even, 16 * 2)
                pe.wait_ge(kcT_ok, 1)
                for c in range(8):
                    mm = pe.transpose(ps[:, 4, c * 16:(c + 1) * 16], cst_rows[:, c * P:(c + 1) * P], ident[0:16, 0:16])
                mm.then_inc(cst_ps, 1)

            def qk_sum(q, n):
                pe.wait_ge(qsq, q + 1)
                if q:
                    pe.wait_ge(qk_ready, q)
                else:
                    pe.wait_ge(std_done, 1)
                for t in range(n):
                    mm = pe.matmul(ps[:, 4 + t, 0:T], blk, sq4[:, t, :], start=True, stop=True)
                mm.then_inc(qss, 1)

            def qk_rot(q, c0, n):
                pe.wait_ge(qnorm, q + 1)
                for t in range(n):
                    mm = pe.matmul(ps[:, 4 + t, 0:T], rot, qk[:, c0 + t, :], start=True, stop=True)
                mm.then_inc(qrot, 1)

            def kv_T():
                pe.wait_ge(qk_ready, 3)
                for p in range(2):
                    cs = slice(p * P, (p + 1) * P)
                    cs2 = slice(256 + p * P, 256 + (p + 1) * P)
                    pe.transpose(ps[:, 4, cs], qk[:, 8 + p, P:2 * P], ident)
                    pe.transpose(ps[:, 4, cs2], vF[:, p, 0:P], ident)
                    pe.transpose(ps[:, 5, cs], vF[:, p, P:2 * P], ident)
                    pe.matmul(ps[0:NB, 6, cs], qk[:, 8 + p, TP:T], ident, start=True, stop=True)
                    mm = pe.matmul(ps[0:NB, 6, cs2], vF[:, p, TP:T], ident, start=True, stop=True)
                mm.then_inc(kv_ps, 1)

            def item(i):
                q, kv = divmod(i, NKV)
                return q, kv, kv // 2, HD * (kv % 2), P * (q + 1)

            def scores(i):
                q, kv, p, r, nk = item(i)
                pe.wait_ge(kv_tok, 1)
                pe.wait_ge(maskb_ok, 2)
                if i:
                    pe.wait_ge(exp_done, i)
                if i == NKV:
                    pe.wait_ge(ct_ok, 1)
                for g in range(GRP):
                    out = psf[:, 4 * 512 + g * nk:4 * 512 + (g + 1) * nk]
                    pe.matmul(out, qk[r:r + HD, 4 * p + g, q * P:(q + 1) * P], qk[r:r + HD, 8 + p, 0:nk],
                              start=True, stop=False)
                    mm = pe.matmul(out, identb[:, :], maskb[:, 2 * P - nk:2 * P], start=False, stop=True)
                mm.then_inc(sc_done, 1)

            def probs_T(i):
                q, kv, p, r, nk = item(i)
                pe.wait_ge(pn_done, i + 1)
                if i:
                    pe.wait_ge(o_done, i)
                for kb in range(nk // P):
                    for g in range(GRP):
                        mm = pe.transpose(ps[:, 6 + kb, g * P:(g + 1) * P], prob[:, i % 2, g, kb * P:(kb + 1) * P], ident)
                mm.then_inc(pt_done, 1)

            def attend(i):
                q, kv, p, r, nk = item(i)
                pe.wait_ge(pT_ok, i + 1)
                for kb in range(nk // P):
                    mm = pe.matmul(ps[r:r + HD, 6, :], vT[:, kb, kv * HD:(kv + 1) * HD], pT[:, kb, :],
                                   start=kb == 0, stop=kb == nk // P - 1)
                mm.then_inc(pv_done, 1)

            def by_bc(flat):
                return flat.rearrange("p (r c b) -> p r c b", r=2, c=8)

            def dec_scores():
                pe.wait_ge(exp_done, 8)
                pe.wait_ge(kcT_ok, 1)
                for b in range(NB):
                    for kv in range(NKV):
                        p, r = kv // 2, HD * (kv % 2)
                        mm = pe.matmul(by_bc(ps[:, 4 + kv % 2, 0:P])[:, kv % 2, 4 * p:4 * p + 4, b],
                                       kcT[r:r + HD, 2 * b + p, :], qk[r:r + HD, 4 * p:4 * p + 4, TP + b],
                                       start=True, stop=True)
                mm.then_inc(sS_done, 1)

            def dec_rows():
                pe.wait_ge(sT_ok, 1)
                pe.wait_ge(prod_ok, 1)
                pe.transpose(ps[:, 5, 0:P], sT[:, :], ident)
                for r in (0, HD):
                    mm = pe.matmul(ps[r:r + HD, 5, P:P + 1], prod[r:r + HD, :], ones[r:r + HD, 0:1], start=True, stop=True)
                mm.then_inc(sR_done, 1)

            def dec_probs_T():
                pe.wait_ge(pS_ok, 1)
                pe.wait_ge(o_done, 8)
                pe.transpose(ps[:, 6, 0:P], pS[:, 0:P], ident)
                pe.matmul(ps[:, 6, P:P + HD], blk, dg[:, :], start=True, stop=True).then_inc(pTS_ps, 1)

            def dec_attend():
                pe.wait_ge(pTS_ok, 1)
                pe.wait_ge(d_even, 16 * 2)
                for b in range(NB):
                    for kv in range(NKV):
                        p, r = kv // 2, HD * (kv % 2)
                        mm = pe.matmul(ps[r:r + HD, 7, 0:64].rearrange("p (c b) -> p c b", c=8)[:, 4 * p:4 * p + 4, b],
                                       vc[:, b, kv * HD:(kv + 1) * HD], by_bc(pTS[:, 0:P])[:, kv % 2, 4 * p:4 * p + 4, b],
                                       start=True, stop=True)
                mm.then_inc(pvS, 1)

            def conv_T(h, b0, b1):
                pe.wait_ge(conv_u, h + 1)
                for t in range(4):
                    cs = slice(t * P, (t + 1) * P)
                    pe.matmul(ps[0:2, b0, cs], conv_in[:, t, TP:TP + 2], ident, start=True, stop=True)
                    mm = pe.matmul(ps[0:NB, b1, cs], conv_in[:, t, 274:282], ident, start=True, stop=True)
                mm.then_inc(ct_ps, 1)

            for u in range(EVEN_GROUPS * IN_UNITS):
                g, j = divmod(u, IN_UNITS)
                if g == 0:
                    pe.wait_ge(xl_done, j // 2 + 1)
                if u == 0:
                    pe.wait_ge(evac_g, G_EVEN - 1)
                unit(U_EVEN + u, xh, xl, 2 * j, 0, j == 0, j == IN_UNITS - 1, single=True,
                     taken=(3 * g - 2, G_EVEN + g) if g and j == 0 else None)
                if u == 1:
                    cache_T()
                if u == 2:
                    conv_state_T()
                if u == 4:
                    pe.wait_ge(cst_ok, 1)
                    norm_sum(0)
                for q, (c0, n) in enumerate(((0, 4), (4, 4), (8, 2))):
                    if u == IN_UNITS * q + 8:
                        qk_sum(q, n)
                    if u == IN_UNITS * q + 10:
                        qk_rot(q, c0, n)
                if u == 27:
                    kv_T()
                at, i = (u - 28) % 4, (u - 28) // 4
                if 0 <= i < 8:
                    if at == 0:
                        scores(i)
                    if at == 2:
                        probs_T(i)
                    if at == 3:
                        attend(i)
                if u == 41:
                    conv_T(0, 5, 7)
                if u == 60:
                    dec_scores()
                if u == 61:
                    dec_rows()
                if u == 63:
                    dec_probs_T()
                if u == 64:
                    dec_attend()
                if u == 67:
                    pe.wait_ge(eS_done, 1)
                    conv_T(1, 4, 5)

            def out_proj(U, G, order, even):
                with pe.Fori(0, 2, 1) as i:
                    for h in range(2):
                        for j in range(IN_UNITS):
                            if j == 0:
                                pe.wait_ge(evac_g, at_turn(pe, i, 1 + h, G))
                            if h == 1 and j == 0:
                                if even:
                                    pe.wait_ge(ct_ok, 2)
                                else:
                                    pe.wait_ge(ostd, 2)
                            if even and h == 0 and j in (0, 2):
                                pe.wait_ge(conv_l, 1 + j // 2)
                            if even and h == 0 and j == 3:
                                pe.wait_ge(o_done, 9)
                            if not even and h == 0 and j in (0, 2):
                                pe.wait_ge(pml, 4 + 2 * j)
                            if not even and h == 0 and j in (4, 6):
                                pe.wait_ge(ocl, j // 2 - 1)
                            unit(U + IN_UNITS * h + j, yh, yl, 2 * order[j], 4 * h, j == 0, j == IN_UNITS - 1,
                                 i=i, step=2 * IN_UNITS)

            def ffn(layer, U, G, m):
                def gate_up(i, peeled):
                    for h in range(2):
                        for j in range(IN_UNITS):
                            if j == 0:
                                pe.wait_ge(evac_g, at_turn(pe, i, 2, G - 1 + h))
                            if peeled and h == 0:
                                pe.wait_ge(xl_done, 4 * m + j // 2 + 1)
                            if peeled and h == 1 and j == 0:
                                pe.wait_ge(rstd_done, m + 1)
                            unit(U + IN_UNITS * h + j, xh, xl, 2 * j, 4 * h, j == 0, j == IN_UNITS - 1,
                                 i=i, step=2 * IN_UNITS)
                            if peeled and h == 0 and j == 5:
                                pe.wait_ge(evac_g, G)
                                norm_sum(m)

                gate_up(None, True)
                with pe.Fori(1, GU_ITERS, 1) as i:
                    gate_up(i, False)
                U2, G2 = U + 2 * IN_UNITS * GU_ITERS, G + 2 * GU_ITERS
                hid = GU_ITERS * (layer + 1)
                with pe.Fori(0, 2, 1) as i:
                    for h in range(2):
                        for j in range(DN_UNITS):
                            if j == 0:
                                pe.wait_ge(evac_g, at_turn(pe, i, 2, G2 - 1 + h))
                            if h == 0 and j == 0:
                                pe.wait_ge(hid_done, hid - 1)
                            if h == 0 and j == 20:
                                pe.wait_ge(hid_done, hid)
                            if layer == 1 and j == 0:
                                pe.wait_ge(y_ok, at_turn(pe, i, 2, 2))
                            unit(U2 + DN_UNITS * h + j, hh, hl, 2 * j, 4 * h, j == 0, j == DN_UNITS - 1,
                                 i=i, step=2 * DN_UNITS)
                            if layer == 1 and (h, j) in ((1, 2), (1, DN_UNITS - 1)):
                                k = 0 if j == 2 else 1
                                stage = (gbuf, ubuf)[k]
                                pe.wait_ge(evac_g, at_turn(pe, i, 2, G2 + k + 1))
                                for t in range(4):
                                    cs = slice(t * P, (t + 1) * P)
                                    for q in range(2):
                                        pe.transpose(ps[:, 4 * k + q, cs], stage[:, t, q * P:(q + 1) * P], ident)
                                    mm = pe.matmul(ps[0:NB, 4 * k + 2, cs], stage[:, t, TP:T], ident, start=True, stop=True)
                                mm.then_inc(y_ps, 1)

            out_proj(U_OUT_E, G_OUT_E, OUT_E_ORDER, True)
            ffn(0, U_FFN0, G_FFN0, 1)

            def gate_rank():
                pe.wait_ge(evac_g, G_ODD + 2)
                pe.wait_ge(d_odd, 16)
                for h in range(GH):
                    mm = pe.matmul(ps[:, 4 + h, 0:T], wup[:, h * P:(h + 1) * P], zr[:, :], start=True, stop=True)
                mm.then_inc(gk_ps, 1)

            def att():
                pe.wait_ge(kd_ok, 1)
                pe.wait_ge(zb_ok, 1)
                for h in range(GH):
                    for n in range(NCH):
                        r = CH * (n % 2)
                        q = 2 * h + n // 2
                        mm = pe.matmul(ps[r:r + CH, 4, q * CH:(q + 1) * CH], sq4[:, h, n * CH:(n + 1) * CH],
                                       qg[:, h, n * CH:(n + 1) * CH], start=True, stop=True)
                mm.then_inc(att_ps, 1)

            def k2_T():
                pe.wait_ge(k2_ok, 1)
                for h in range(GH):
                    cs = slice(h * P, (h + 1) * P)
                    for q in range(2):
                        pe.transpose(ps[:, 5 + q, cs], ubuf[:, h, q * P:(q + 1) * P], ident)
                    mm = pe.matmul(ps[0:NB, 7, cs], kg[:, h, TP:T], ident, start=True, stop=True)
                mm.then_inc(k2t_ps, 1)

            def v_T(half):
                pe.wait_ge(evac_g, G_ODD + 4 + half)
                pe.wait_ge(k2t_ok, 1)
                if half:
                    pe.wait_ge(st_ok, 2)
                    pe.wait_ge(go_ok, 2)
                for t in range(4):
                    cs = slice(t * P, (t + 1) * P)
                    for q in range(2):
                        pe.transpose(ps[:, 5 + q, cs], vf[:, t, q * P:(q + 1) * P], ident)
                    mm = pe.matmul(ps[0:NB, 7, cs], vf[:, t, TP:T], ident, start=True, stop=True)
                mm.then_inc(vt_ps, 1)

            def gla_delta(h):
                pe.wait_ge(vt_ok, h // 2 + 1)
                if h:
                    pe.wait_ge(st_ok, h)
                for n in range(NCH):
                    r, q = CH * (n % 2), n // 2
                    mm = pe.matmul(ps[:, 5 + n % 2, q * GDV:(q + 1) * GDV], k2t[r:r + CH, q, h * P:(h + 1) * P],
                                   vtok[r:r + CH, q, h * GDV:(h + 1) * GDV], start=True, stop=True)
                mm.then_inc(dl_ps, 1)

            def gla_out(h):
                pe.wait_ge(st_ok, h + 1)
                pe.wait_ge(att_ok, 1)
                if h:
                    pe.wait_ge(go_ok, h)
                for e in range(2):
                    for n in range(NCH):
                        r, q = CH * (n % 2), n // 2
                        out = ps[:, 4 if n % 2 == 0 else 7, e * P + q * CH:e * P + (q + 1) * CH]
                        c0 = h * GDV + e * P
                        mm = pe.matmul(out, vtok[r:r + CH, q, c0:c0 + P], attS[r:r + CH, 2 * h + q, :],
                                       start=True, stop=n == 0)
                        if n:
                            mm = pe.matmul(out, st[:, h % 2, n - 1, e * P:(e + 1) * P], qg[:, h, n * CH:(n + 1) * CH],
                                           start=False, stop=True)
                mm.then_inc(go_ps, 1)

            def dec_outer(q):
                b, hp = divmod(q, 2)
                pe.wait_ge(kdg, b + 1)
                pe.wait_ge(vt_ok, 2)
                pe.wait_ge(st_ok, 4)
                if q >= 2:
                    pe.wait_ge(sg_ok, q - 1)
                for k in range(2):
                    h = 2 * hp + k
                    mm = pe.matmul(ps[:, 5 + q % 2, k * GDV:(k + 1) * GDV], kdiag[:, b % 2, h * P:(h + 1) * P],
                                   vS[:, h * GDV:(h + 1) * GDV], start=True, stop=True)
                mm.then_inc(kv_o, 1)

            def dec_out(q):
                b, hp = divmod(q, 2)
                pe.wait_ge(sg_ok, q + 1)
                if q == 0:
                    pe.wait_ge(go_ok, 4)
                for k in range(2):
                    for e in range(2):
                        h = 2 * hp + k
                        c = (2 * h + e) * NB + b
                        mm = pe.matmul(ps[:, 7, c:c + 1], sgl[:, q % 4, k, e * P:(e + 1) * P], qsamp[:, h, b:b + 1],
                                       start=True, stop=True)
                mm.then_inc(so_ps, 1)

            def pool_state_T(half):
                pe.wait_ge(d_prow, 16)
                pe.wait_ge(go_ok, 4)
                if half:
                    pe.wait_ge(pml, 4)
                for t in range(4):
                    c = 4 * half + t
                    mm = pe.transpose(ps[:, 4, t * 120:(t + 1) * 120], prow[:, c * P:(c + 1) * P], ident[0:120, 0:120])
                mm.then_inc(pst_ps, 1)

            def pool_T(half, part):
                pe.wait_ge(evac_g, G_ODD + 6 + half)
                pe.wait_ge(pst_ok, half + 1)
                if half + part:
                    pe.wait_ge(po_ok, 2 * half + part)
                for t in range(4):
                    cs = slice(t * P, (t + 1) * P)
                    if part == 0:
                        mm = pe.matmul(ps[0:PB, 4, cs], ext[:, t, TP:TP + PB], ident, start=True, stop=True)
                    else:
                        mm = pe.matmul(ps[0:NB, 4, cs], ext[:, t, 286:399:16], ident, start=True, stop=True)
                mm.then_inc(po_ps, 1)

            def pool_mix(c):
                g, m = divmod(c, 2)
                pe.wait_ge(dmix_ok, g + 1)
                pe.wait_ge(d_wp, 16)
                pe.wait_ge(po_ok, 2 * (g // 2) + 2)
                if c:
                    pe.wait_ge(pml, c)
                for k in range(2):
                    mm = pe.matmul(ps[:, 4, 0:T], wpool[:, 2 * g + k, m * P:(m + 1) * P], dmix[:, k, :],
                                   start=k == 0, stop=k == 1)
                mm.then_inc(pm_ps, 1)

            def out_sum(half):
                pe.wait_ge(osq, half + 1)
                pe.wait_ge(sg_ok, 16)
                if half:
                    pe.wait_ge(ostd, 1)
                for k in range(2):
                    for e in range(2):
                        mm = pe.matmul(ps[:, 5 + k, 0:T], ones[:, :], sq4[:, 2 * k + e, :], start=e == 0, stop=e == 1)
                mm.then_inc(oss, 1)

            tiles_before = 3 * EVEN_GROUPS
            for q, (col, s0) in enumerate(zip(ODD_COLS, ODD_FIRST)):
                G = G_ODD + q
                units = IN_UNITS if col is not None else 2
                for j in range(units):
                    s = s0 + j
                    n = U_ODD + s
                    if col is None:
                        pe.wait_ge(lo_done, n + 1)
                        if j == 0:
                            pe.wait_ge(evac_t, tiles_before - 2)
                        for k in range(8):
                            for m, (w, r) in enumerate(((whi, xh), (whi, xl), (wlo, xh))):
                                mm = pe.matmul(ps[:, 0, 0:T], w[:, n % RING, k * P:(k + 1) * P], r[:, 8 * j + k, :],
                                               start=j == k == m == 0, stop=j == 1 and k == 7 and m == 2)
                        mm.then_inc(units_done, 1)
                    else:
                        if q == 0:
                            pe.wait_ge(xl_done, 8 + j // 2 + 1)
                        if q == 0 and j == 0:
                            pe.wait_ge(evac_g, G - 1)
                        if q == 2 and j == 0:
                            pe.wait_ge(evac_g, G)
                        unit(n, xh, xl, 2 * j, 0, j == 0, j == IN_UNITS - 1, single=True,
                             taken=(tiles_before - 2, G) if q > 2 and j == 0 else None)
                    if s == 5:
                        pe.wait_ge(evac_g, G_ODD)
                        norm_sum(2)
                    if s == 10:
                        pe.wait_ge(std_done, 3)
                        gate_rank()
                    if s == 19:
                        att()
                    if s == 20:
                        k2_T()
                    if s == 27:
                        v_T(0)
                    if s == 35:
                        v_T(1)
                    for k, h in ((28, 0), (30, 1), (36, 2), (38, 3)):
                        if s == k:
                            gla_delta(h)
                        if s == k + 1:
                            gla_out(h)
                    if 0 <= s - 40 < 16:
                        dec_outer(s - 40)
                    if 0 <= s - 41 < 16:
                        dec_out(s - 41)
                    for half in range(2):
                        if s == 40 + 8 * half:
                            pool_state_T(half)
                        if s == 42 + 8 * half:
                            pool_T(half, 0)
                        if s == 43 + 8 * half:
                            pool_T(half, 1)
                        if 44 + 8 * half <= s < 48 + 8 * half:
                            pool_mix(4 * half + s - 44 - 8 * half)
                        if s == 57 + 2 * half:
                            out_sum(half)
                if col is not None:
                    tiles_before += 3

            out_proj(U_OUT_O, G_OUT_O, OUT_O_ORDER, False)
            ffn(1, U_FFN1, G_FFN1, 3)

        @block.scalar
        def _(act):
            steps = [0]

            def own(ins):
                steps[0] += 1
                ins.then_inc(ac, 1)
                act.wait_ge(ac, steps[0])

            act.dma_start(cst[:, :], a["consts"]).then_inc(d_cst, 16)
            for r, n, src in ((V_MIX, 32, a["norm_mix"].rearrange("l (c p) -> (l c) p", p=P)),
                              (V_FFN, 32, a["norm_ffn"].rearrange("l (c p) -> (l c) p", p=P)),
                              (V_CONV, 24, a["conv_w"][0].rearrange("j (c p) -> (j c) p", p=P)),
                              (V_PSC, 8, a["pool_scale"].rearrange("l (c p) -> (l c) p", p=P)),
                              (V_BAL, 4, a["b_alpha"].rearrange("l (c p) -> (l c) p", p=P)),
                              (V_GLA, 2, a["gla_out_norm"].rearrange("l (c p) -> (l c) p", p=P))):
                act.dma_start(vrow[r:r + n, :], src).then_inc(d_vec, 16)
            for r, src in ((V_Q, a["q_norm"]), (V_K, a["k_norm"])):
                act.dma_start(vrow[r:r + 1, :].rearrange("o (h d) -> o h d", h=2),
                              src.unsqueeze(1).broadcast_to([1, 2, HD])).then_inc(d_vec, 16)
            for q in range(2):
                act.dma_start(xtok[:, q, :], a["x_prompt"][0, q * P:(q + 1) * P, :]).then_inc(d_x, 16)
            act.dma_start(xtok_s[:, :], a["x_sample"].rearrange("b s d -> (b s) d")).then_inc(d_x, 16)
            act.dma_start(kc[:, :, :], a["cache_swa_k"][0].rearrange("b k h d -> k b (h d)")).then_inc(d_kc, 16)
            act.dma_start(vc[:, :, :], a["cache_swa_v"][0].rearrange("b k h d -> k b (h d)")).then_inc(d_even, 16)
            act.dma_start(cst_rows[:, :], a["state_conv"][0].rearrange("b j d -> (b j) d")).then_inc(d_even, 16)

            def norm_prep(r, G, c0, base, i=None):
                evac_g_then = at_turn(act, i, 2, G + 1)
                acc_done_then = at_turn(act, i, 2, r)
                act.wait_ge(evac_g, evac_g_then)
                if r:
                    act.wait_ge(acc_done, acc_done_then)
                c = c0 if i is None else act.snap(i * 8 + c0)
                for t in range(4):
                    ins = act.activation(xh[:, c0 + t, :] if i is None else xh[:, bass.ds(c + t, 1), :],
                                         x[:, c0 + t, :] if i is None else x[:, bass.ds(c + t, 1), :], ACT.Copy,
                                         scale=vec[:, base + c0 + t:base + c0 + t + 1] if i is None
                                         else vec[:, bass.ds(c + base + t, 1)])
                ins.then_inc(xh_done, 1)
                act.activation(sq4[:, :, :], x[:, c0:c0 + 4, :] if i is None else x[:, bass.ds(c, 4), :],
                               ACT.Square).then_inc(sq_done, 1)

            def root(m):
                act.wait_ge(ss_done, m + 1)
                act.activation(std[:, :], ps[:, 4, 0:T], ACT.Sqrt, scale=1.0 / D, bias=eps[:, :]).then_inc(std_done, 1)

            act.wait_ge(vecT, 1)
            act.wait_ge(ms_done, 2)
            act.activation(vec[:, :], ps[:, 7, 0:NVEC], ACT.Copy).then_inc(vec_ok, 1)
            act.wait_ge(d_cst, 16)
            act.activation(maskb[:, :], cst[:, C_MASK:C_MASK + 2 * P], ACT.Copy).then_inc(maskb_ok, 1)
            act.activation(identb[:, :], ident, ACT.Copy).then_inc(maskb_ok, 1)
            for n in range(AHEAD):
                split_hi(act, n)
            act.wait_ge(vec_ok, 1)
            for g in range(4):
                norm_prep(g, g, 4 * g, V_MIX)

            def item(i):
                q, kv = divmod(i, NKV)
                return q, kv, kv // 2, HD * (kv % 2), P * (q + 1)

            def exps(i):
                q, kv, p, r, nk = item(i)
                b = 24 * (i % 2)
                act.wait_ge(negm_done, i + 1)
                if i >= 2:
                    act.wait_ge(pt_done, i - 1)
                act.wait_ge(kcT_ps, 1)
                for g in range(GRP):
                    act.activation(prob[:, i % 2, g, 0:nk], psf[:, 4 * 512 + g * nk:4 * 512 + (g + 1) * nk], ACT.Exp,
                                   scale=HD ** -0.5, bias=small[:, b + 4 + g:b + 5 + g],
                                   accum_out=small[:, b + 12 + g:b + 13 + g])
                act.activation(small[:, b + 16:b + 20], small[:, b + 8:b + 12], ACT.Exp).then_inc(exp_done, 1)

            def take_pT(i):
                nkb = item(i)[4] // P
                act.wait_ge(pt_done, i + 1)
                if i:
                    act.wait_ge(pv_done, i)
                act.activation(pT[:, 0:nkb, :], ps[:, 6:6 + nkb, :], ACT.Copy).then_inc(pT_ok, 1)

            def out_hi(i):
                q, kv, p, r, nk = item(i)
                act.wait_ge(pv_done, i + 1)
                act.activation(yh[r:r + HD, 4 * p:4 * p + 4, q * P:(q + 1) * P],
                               ps[r:r + HD, 6, :].rearrange("p (g t) -> p g t", g=4), ACT.Copy).then_inc(oh_done, 1)

            def conv_rows(h):
                b0, b1 = ((5, 7), (4, 5))[h]
                act.wait_ge(ct_ps, h + 1)
                if h:
                    act.wait_ge(d_ct, 32)
                act.activation(conv_tok[0:2, 0, :], ps[0:2, b0, :], ACT.Copy)
                act.activation(conv_tok[:, 1, :], ps[0:NB, b1, :], ACT.Copy).then_inc(ct_ok, 1)
                act.wait_ge(ct_ok, h + 1)
                cs = slice(h * COLS, (h + 1) * COLS)
                act.dma_start(o_cp[0, 0, :, cs], conv_tok[0:2, 0, :]).then_inc(d_ct, 16)
                act.dma_start(o_cs[0, :, 1, cs], conv_tok[:, 1, :]).then_inc(d_ct, 16)

            for u in range(EVEN_GROUPS * IN_UNITS):
                n = U_EVEN + u + AHEAD
                split_hi(act, n)
                if u == 1:
                    act.wait_ge(kcT_ps, 1)
                    act.activation(kcT[:, :, :].rearrange("p q k -> p (q k)"), psf[:, 4 * 512:8 * 512], ACT.Copy).then_inc(kcT_ok, 1)
                if u == 2:
                    act.wait_ge(cst_ps, 1)
                    act.activation(conv_st[:, :, :].rearrange("p c r -> p (c r)"), ps[:, 4, 0:P], ACT.Copy).then_inc(cst_ok, 1)
                if u == 4:
                    root(0)
                if u == 5:
                    for k, (s, t) in enumerate(((a["cache_swa_k"], o_ks), (a["cache_swa_v"], o_vs))):
                        act.dma_start(t[0, :, 0:P - 1], s[0, :, 1:P]).then_inc(d_out, 16)
                    act.dma_start(o_cs[0, :, 0, :], a["state_conv"][0, :, 1, :]).then_inc(d_out, 16)
                    act.dma_start(o_ps[0, :, 0:PB - 1, :], a["state_pool"][0, :, 1:PB, :]).then_inc(d_out, 16)
                    act.dma_start(sink_row[:, :], a["attn_sinks"].broadcast_to([P, NH])).then_inc(d_even, 16)
                    for r in range(2):
                        for p in range(2):
                            src = a["attn_sinks"][0, 8 * p + 4 * r:8 * p + 4 * r + 4].unsqueeze(1).unsqueeze(2)
                            lo_p = HD * r + 32 * p
                            act.dma_start(sink_col[lo_p:lo_p + 32, :], src.broadcast_to([4, NB, 1])).then_inc(d_even, 16)
                for q, (c0, nq) in enumerate(((0, 4), (4, 4), (8, 2))):
                    if u == IN_UNITS * q + 7:
                        act.wait_ge(evac_g, G_EVEN + q + 1)
                        if q:
                            act.wait_ge(qss, q)
                        act.activation(sq4[:, 0:nq, :], qk[:, c0:c0 + nq, :], ACT.Square).then_inc(qsq, 1)
                    if u == IN_UNITS * q + 9:
                        act.wait_ge(qss, q + 1)
                        if q:
                            act.wait_ge(qnorm, q)
                        act.activation(ubuf[:, 0:nq, :], ps[:, 4:4 + nq, 0:T], ACT.Sqrt, scale=1.0 / HD,
                                       bias=eps[:, :]).then_inc(qstd, 1)
                if u == 27:
                    act.wait_ge(kv_ps, 1)
                    act.activation(vT[:, 0, :], ps[:, 4, 256:512], ACT.Copy)
                    act.activation(vT[:, 1, :], ps[:, 5, 0:256], ACT.Copy)
                    act.activation(kT1[:, :], ps[:, 4, 0:256], ACT.Copy)
                    act.activation(kvS[:, :], ps[0:NB, 6, :], ACT.Copy).then_inc(kv_tok, 1)
                if u == 29:
                    act.wait_ge(kv_tok, 1)
                    act.dma_start(o_kp[0, 0].rearrange("k h d -> k (h d)"), kT1[:, :]).then_inc(d_out, 16)
                    act.dma_start(o_vp[0, 0].rearrange("k h d -> k (h d)"), vT[:, 1, :]).then_inc(d_out, 16)
                    act.dma_start(o_ks[0, :, P - 1].rearrange("b h d -> b (h d)"), kvS[:, 0:256]).then_inc(d_out, 16)
                    act.dma_start(o_vs[0, :, P - 1].rearrange("b h d -> b (h d)"), kvS[:, 256:512]).then_inc(d_out, 16)
                at, i = (u - 28) % 4, (u - 28) // 4
                if 0 <= i < 8:
                    if at == 0:
                        exps(i)
                    if at == 2:
                        take_pT(i)
                    if at == 3:
                        out_hi(i)
                if u == 41:
                    conv_rows(0)
                for h in range(2):
                    if u == 47 + 24 * h:
                        act.wait_ge(conv_y, h + 1)
                        act.activation(yh[:, 8 + 4 * h:12 + 4 * h, :], gbuf[:, :, :], ACT.Copy).then_inc(conv_h, 1)
                if u == 60:
                    act.wait_ge(sS_done, 1)
                    act.activation(sT[:, 0:HD], ps[:, 4, 0:HD], ACT.Copy)
                    act.activation(sT[:, HD:P], ps[:, 5, HD:P], ACT.Copy).then_inc(sT_ok, 1)
                if u == 61:
                    act.wait_ge(nS_done, 1)
                    act.activation(pS[:, 0:P + 1], ps[:, 5, 0:P + 1], ACT.Exp, scale=HD ** -0.5,
                                   bias=small[:, 49:50], accum_out=small[:, 51:52])
                    act.activation(small[:, 52:53], small[:, 50:51], ACT.Exp).then_inc(eS_done, 1)
                if u == 63:
                    act.wait_ge(pTS_ps, 1)
                    act.activation(pTS[:, :], ps[:, 6, 0:192], ACT.Copy).then_inc(pTS_ok, 1)
                if u == 65:
                    act.wait_ge(oS_ok, 1)
                    act.activation(yh[:, 0:8, TP:T], prod[:, :].rearrange("p (c b) -> p c b", c=8), ACT.Copy).then_inc(oh_done, 1)
                if u == 67:
                    conv_rows(1)

            def out_proj(U, G, r0, base, split_rows):
                with act.Fori(0, 2, 1) as i:
                    for h in range(2):
                        for j in range(IN_UNITS):
                            n = U + IN_UNITS * h + j + AHEAD
                            up = (16 * (h + 1), 32) if split_rows and (j + AHEAD) in ATTN_UNITS else None
                            split_hi(act, n, i=i, step=2 * IN_UNITS, up=up)
                        norm_prep(r0 + h, G + h, 4 * h, base, i=i)

            def ffn(layer, U, G, m):
                def gate_up(i, peeled):
                    for k in range(2 * IN_UNITS):
                        split_hi(act, U + k + AHEAD, i=i, step=2 * IN_UNITS)
                        if peeled and k == 5:
                            root(m)
                        if k == IN_UNITS - 1:
                            act.wait_ge(evac_g, at_turn(act, i, 2, G + 1))
                            act.activation(gbuf[:, :, :], gbuf[:, :, :], ACT.Silu).then_inc(silu_done, 1)
                    act.wait_ge(h_ready, at_turn(act, i, 1, 11 * layer + 1))
                    dst = hh[:, 0:4, :] if i is None else hh[:, bass.ds(act.snap(i * 4), 4), :]
                    act.activation(dst, ubuf[:, :, :], ACT.Copy).then_inc(hh_done, 1)

                gate_up(None, True)
                with act.Fori(1, GU_ITERS, 1) as i:
                    gate_up(i, False)
                U2, G2 = U + 2 * IN_UNITS * GU_ITERS, G + 2 * GU_ITERS
                if layer == 0:
                    with act.Fori(0, 2, 1) as i:
                        for h in range(2):
                            for j in range(DN_UNITS):
                                split_hi(act, U2 + DN_UNITS * h + j + AHEAD, i=i, step=2 * DN_UNITS)
                            norm_prep(8 + h, G2 + h, 4 * h, V_MIX + KC, i=i)
                    return

                def rows_out(i, k):
                    col = at_turn(act, i, 2 * COLS, COLS * k)
                    act.wait_ge(y_ps, 2 * i + k + 1)
                    if i or k:
                        act.wait_ge(d_y, 64 * i + 32 * k)
                    act.activation(sq4[:, :, :].rearrange("p a t -> p (a t)")[:, 0:2 * COLS], psf[:, 2048 * k:2048 * k + 2 * COLS], ACT.Copy)
                    act.activation(acc4[0:NB, :, :].rearrange("p a t -> p (a t)")[:, 0:COLS], ps[0:NB, 4 * k + 2, :], ACT.Copy).then_inc(y_ok, 1)
                    act.wait_ge(y_ok, 2 * i + k + 3)
                    act.dma_start(y_prompt[0].rearrange("(q p) d -> p q d", q=2)[:, :, bass.ds(col, COLS)],
                                  sq4[:, :, :].rearrange("p a t -> p (a t)")[:, 0:2 * COLS].rearrange("p (q d) -> p q d", q=2)
                                  ).then_inc(d_y, 16)
                    act.dma_start(y_sample.rearrange("b s d -> (b s) d")[:, bass.ds(col, COLS)],
                                  acc4[0:NB, :, :].rearrange("p a t -> p (a t)")[:, 0:COLS]).then_inc(d_y, 16)

                for i in range(2):
                    for k in range(2 * DN_UNITS):
                        split_hi(act, U2 + k + AHEAD, i=i, step=2 * DN_UNITS)
                        if k == DN_UNITS + 2:
                            rows_out(i, 0)
                    rows_out(i, 1)

            out_proj(U_OUT_E, G_OUT_E, 4, V_FFN, True)
            act.wait_ge(d_out, 16 * 8)
            act.wait_ge(d_ct, 64)
            ffn(0, U_FFN0, G_FFN0, 1)

            act.wait_ge(evac_g, G_ODD)
            act.wait_ge(units_done, U_ODD)
            act.wait_ge(d_ct, 64)
            act.dma_start(prow[:, :], a["state_pool"][0].rearrange("b j d -> (b j) d")).then_inc(d_prow, 16)
            act.dma_start(wup[:, :], a["w_alpha_up"][0]).then_inc(d_odd, 16)
            gla_in = a["state_gla"][0].rearrange("b h k v -> k b h v")
            gla_o = o_gs[0].rearrange("b h k v -> k b h v")

            def dec_load(q):
                b, hp = divmod(q, 2)
                if q >= 4:
                    act.wait_ge(d_gso[q % 4], 16 * (q // 4))
                    act.wait_ge(so_ps, q - 3)
                act.dma_start(sgl[:, q % 4, :, :], gla_in[:, b, 2 * hp:2 * hp + 2, :]).then_inc(d_gs[q % 4], 16)

            for q in range(4):
                dec_load(q)

            def pool_rows(half, part):
                n = PB if part == 0 else NB
                act.wait_ge(po_ps, 2 * half + part + 1)
                if half:
                    act.wait_ge(d_pt[part], 16)
                act.activation(ptok[0:n, part, :], ps[0:n, 4, :], ACT.Copy).then_inc(po_ok, 1)
                act.wait_ge(po_ok, 2 * half + part + 1)
                cs = slice(half * COLS, (half + 1) * COLS)
                dst = o_pp[0, 0, :, cs] if part == 0 else o_ps[0, :, PB - 1, cs]
                act.dma_start(dst, ptok[0:n, part, :]).then_inc(d_pt[part], 16)

            for s in range(U_OUT_O - U_ODD):
                split_hi(act, U_ODD + s + AHEAD)
                if s == 5:
                    root(2)
                if s == 10:
                    act.wait_ge(zb_ok, 1)
                    own(act.activation(sq4[:, :, :], acc4[:, :, :], ACT.Abs))
                    own(act.activation(sq4[:, :, :], sq4[:, :, :], ACT.Exp, scale=-1.0))
                    act.activation(sq4[:, :, :], sq4[:, :, :], ACT.Ln, bias=ones[:, 0:1]).then_inc(ln_ok, 1)
                if s == 12:
                    act.wait_ge(b_ok, 1)
                    act.activation(acc4[:, :, :], gbuf[:, :, :], ACT.Exp, scale=1.0 / 16)
                    act.activation(sq4[:, :, :], gbuf[:, :, :], ACT.Exp, scale=-1.0 / 16).then_inc(eb_ok, 1)
                if s == 17:
                    act.wait_ge(df_ok, 1)
                    act.activation(ubuf[:, :, 0:TP], ubuf[:, :, 0:TP], ACT.Exp, scale=1.0 / 16).then_inc(edf_ok, 1)
                if s == 20:
                    act.wait_ge(k2t_ps, 1)
                    act.activation(k2t[:, :, :], ps[:, 5:7, :], ACT.Copy)
                    act.activation(ktS[:, :], ps[0:NB, 7, :], ACT.Copy).then_inc(k2t_ok, 1)
                for half in range(2):
                    if s == 27 + 8 * half:
                        act.wait_ge(vt_ps, half + 1)
                        cs = slice(half * COLS, (half + 1) * COLS)
                        act.activation(vtok[:, :, cs], ps[:, 5:7, :], ACT.Copy)
                        act.activation(vS[:, cs], ps[0:NB, 7, :], ACT.Copy).then_inc(vt_ok, 1)
                for k, h in ((29, 0), (31, 1), (37, 2), (39, 3)):
                    if s == k:
                        act.wait_ge(go_ps, h + 1)
                        to = oF[:, 2 * h:2 * h + 2, 0:TP].rearrange("p e (q r c) -> p e q r c", q=2, r=2)
                        for r, bank in ((0, 4), (1, 7)):
                            ins = act.activation(to[:, :, :, r, :], ps[:, bank, 0:TP].rearrange("p (e q c) -> p e q c", e=2, q=2), ACT.Copy)
                        ins.then_inc(go_ok, 1)
                        act.wait_ge(st_ok, h + 1)
                        act.dma_start(o_gp[0, 0, h], st[:, h % 2, 3, :]).then_inc(d_go[h % 2], 16)
                if s == 40:
                    act.wait_ge(d_go[0], 32)
                    act.wait_ge(d_go[1], 32)
                    act.wait_ge(go_ps, 4)
                    act.dma_start(wpool[:, :, :], a["w_pool"][0].rearrange("g (k p) n -> p (g k) n", p=P)).then_inc(d_wp, 16)
                if 0 <= s - 41 < 16:
                    q = s - 41
                    act.wait_ge(sg_ok, q + 1)
                    act.dma_start(gla_o[:, q // 2, 2 * (q % 2):2 * (q % 2) + 2, :], sgl[:, q % 4, :, :]).then_inc(d_gso[q % 4], 16)
                if 0 <= s - 42 < 12:
                    dec_load(s - 42 + 4)
                for half in range(2):
                    if s == 40 + 8 * half:
                        act.wait_ge(pst_ps, half + 1)
                        act.wait_ge(pad_ok, 1)
                        if half:
                            act.wait_ge(dmix_ok, 2)
                            act.wait_ge(po_ps, 2)
                        act.activation(ext[:, :, 271:399].rearrange("p t (b j) -> p t b j", b=NB)[:, :, :, 0:PB],
                                       ps[:, 4, 0:480].rearrange("p (t b j) -> p t b j", t=4, b=NB), ACT.Copy).then_inc(pst_ok, 1)
                    if s == 42 + 8 * half:
                        pool_rows(half, 0)
                    if s == 43 + 8 * half:
                        pool_rows(half, 1)
                    if 44 + 8 * half <= s < 48 + 8 * half:
                        c = 4 * half + s - 44 - 8 * half
                        act.wait_ge(pm_ps, c + 1)
                        act.activation(yh[:, 8 + c, :], ps[:, 4, 0:T], ACT.Copy,
                                       scale=vec[:, V_PSC + c:V_PSC + c + 1]).then_inc(pmh, 1)
                    if s == 57 + 2 * half:
                        act.wait_ge(oss, half + 1)
                        act.activation(rst2[:, :, :], ps[:, 5:7, 0:T], ACT.Sqrt, scale=1.0 / GDV, bias=eps[:, :]).then_inc(ostd, 1)
                    if s == 57 + 8 * half:
                        act.wait_ge(evac_g, G_ODD + 8 + half)
                        act.activation(gbuf[:, :, :], gbuf[:, :, :], ACT.Silu).then_inc(sg_silu, 1)
                        act.wait_ge(oc_ok, half + 1)
                        act.activation(yh[:, 4 * half:4 * half + 4, :], oF[:, 4 * half:4 * half + 4, :], ACT.Copy).then_inc(och, 1)
                if s == 56:
                    act.wait_ge(so_ps, 16)
                    own(act.activation(oF[:, :, TP:T], ps[:, 7, 0:64].rearrange("p (c b) -> p c b", c=8), ACT.Copy))
                for half in range(2):
                    if s == 56 + 2 * half:
                        act.wait_ge(kd_ok, 1)
                        if half:
                            act.wait_ge(oss, 1)
                        ins = act.activation(sq4[:, :, :], oF[:, 4 * half:4 * half + 4, :], ACT.Square)
                        ins.then_inc(osq, 1)

            out_proj(U_OUT_O, G_OUT_O, 12, V_FFN + KC, False)
            act.wait_ge(d_go[0], 32)
            act.wait_ge(d_go[1], 32)
            act.wait_ge(d_gso[0], 64)
            act.wait_ge(d_gso[1], 64)
            act.wait_ge(d_gso[2], 64)
            act.wait_ge(d_gso[3], 64)
            ffn(1, U_FFN1, G_FFN1, 3)
            act.wait_ge(d_out, 16 * 8)
            act.wait_ge(d_ct, 64)
            act.wait_ge(d_go[0], 32)
            act.wait_ge(d_go[1], 32)
            act.wait_ge(d_pt[0], 32)
            act.wait_ge(d_pt[1], 32)
            act.wait_ge(d_y, 128)
            act.wait_ge(d_gso[0], 64)
            act.wait_ge(d_gso[1], 64)
            act.wait_ge(d_gso[2], 64)
            act.wait_ge(d_gso[3], 64)

        @block.vector
        def _(dve):
            steps = [0]

            def own(ins):
                steps[0] += 1
                ins.then_inc(dv, 1)
                dve.wait_ge(dv, steps[0])

            def norm_rest(r, c0, base, i=None):
                dve.wait_ge(xh_done, at_turn(dve, i, 2, r + 1))
                c = c0 if i is None else dve.snap(i * 8 + c0)
                for t in range(4):
                    at = slice(c0 + t, c0 + t + 1) if i is None else bass.ds(c + t, 1)
                    g = vec[:, base + c0 + t:base + c0 + t + 1] if i is None else vec[:, bass.ds(c + base + t, 1)]
                    ins = dve.scalar_tensor_tensor(xl[:, at, :], x[:, at, :], g, xh[:, at, :].bitcast(F32), ALU.mult, ALU.subtract)
                ins.then_inc(xl_done, 1)

            def reciprocal_std(m):
                dve.wait_ge(std_done, m + 1)
                dve.reciprocal(rstd[:, :], std[:, :]).then_inc(rstd_done, 1)
                dve.wait_ge(rstd_done, m + 1)

            def take(G, dst, scale, tiles=4, done=None):
                for t in range(tiles):
                    if t == 3:
                        dve.wait_ge(units_done, done)
                    else:
                        dve.wait_ge(tile_done, take.tiles + t + 1)
                    ins = dve.tensor_tensor(dst(t), ps[:, t, 0:T], scale, ALU.mult)
                    ins.then_inc(evac_g if t == tiles - 1 else evac_t, 1)
                if tiles == 4:
                    take.tiles += 3

            take.tiles = 0

            for n in range(AHEAD):
                split_lo(dve, n)
            for g in range(4):
                dve.wait_ge(head_done, g + 1)
                dve.tensor_copy(x[:, 4 * g:4 * g + 4, :], ps[:, 4 * (g % 2):4 * (g % 2) + 4, 0:T]).then_inc(evac_g, 1)
                if g:
                    norm_rest(g - 1, 4 * (g - 1), V_MIX)
            norm_rest(3, 12, V_MIX)

            def item(i):
                q, kv = divmod(i, NKV)
                return q, kv, kv // 2, HD * (kv % 2), P * (q + 1)

            def row_max(i):
                q, kv, p, r, nk = item(i)
                b = 24 * (i % 2)
                dve.wait_ge(sc_done, i + 1)
                own(dve.reduce_max(small[:, b:b + 4], psf[:, 4 * 512:4 * 512 + 4 * nk].rearrange("p (g k) -> p g k", g=4), AX))
                own(dve.scalar_tensor_tensor(small[:, b + 4:b + 8], small[:, b:b + 4], -HD ** -0.5,
                                             nsink_row[:, 4 * kv:4 * kv + 4], ALU.mult, ALU.min))
                dve.tensor_tensor(small[:, b + 8:b + 12], small[:, b + 4:b + 8], sink_row[:, 4 * kv:4 * kv + 4],
                                  ALU.add).then_inc(negm_done, 1)

            def denominators(i):
                b = 24 * (i % 2)
                dve.wait_ge(exp_done, i + 1)
                own(dve.tensor_tensor(small[:, b + 12:b + 16], small[:, b + 12:b + 16], small[:, b + 16:b + 20], ALU.add))
                dve.reciprocal(small[:, b + 20:b + 24], small[:, b + 12:b + 16]).then_inc(rec_done, 1)

            def out_lo(i):
                q, kv, p, r, nk = item(i)
                dve.wait_ge(oh_done, i + 1)
                at = (slice(r, r + HD), slice(4 * p, 4 * p + 4), slice(q * P, (q + 1) * P))
                dve.tensor_tensor(yl[at], ps[r:r + HD, 6, :].rearrange("p (g t) -> p g t", g=4), yh[at].bitcast(F32),
                                  ALU.subtract).then_inc(o_done, 1)

            def conv(h):
                for j in range(3):
                    for t in range(4):
                        w = vec[:, V_CONV + 8 * j + 4 * h + t:V_CONV + 8 * j + 4 * h + t + 1]
                        for dst, src in ((gbuf[:, t, 0:TP], conv_in[:, t, j:j + TP]),
                                         (gbuf[:, t, TP:T], conv_in[:, t, 258 + NB * j:266 + NB * j])):
                            if j == 0:
                                ins = dve.tensor_scalar(dst, src, w, None, ALU.mult)
                            else:
                                ins = dve.scalar_tensor_tensor(dst, src, w, dst, ALU.mult, ALU.add)
                    own(ins)

            for u in range(EVEN_GROUPS * IN_UNITS):
                split_lo(dve, U_EVEN + u + AHEAD)
                done = U_EVEN + u + 1
                g, j = divmod(u, IN_UNITS)
                if u == 4:
                    reciprocal_std(0)
                if u == 6:
                    dve.wait_ge(d_even, 16 * 7)
                    dve.wait_ge(vec_ok, 1)
                    dve.wait_ge(evac_g, 4)
                    dve.wait_ge(cst_ok, 1)
                    dve.tensor_scalar(nsink_row[:, :], sink_row[:, :], -1.0, None, ALU.mult)
                    dve.tensor_scalar(nsink_col[:, :], sink_col[:, :], -1.0, None, ALU.mult)
                    dve.tensor_tensor(dg[:, :], ident[:, 0:HD], ident[:, HD:P], ALU.add)
                    own(dve.memset(conv_in[:, :, 0:2], 0.0))
                if j == IN_UNITS - 1:
                    if g < 3:
                        take(G_EVEN + g, lambda t: qk[:, 4 * g + t, :] if 4 * g + t < 10 else vF[:, t - 2, :], rstd[:, :], done=done)
                    else:
                        h, part = divmod(g - 3, 3)
                        if part == 0:
                            take(G_EVEN + g, lambda t: gbuf[:, t, :], rstd[:, :], done=done)
                        elif part == 1:
                            take(G_EVEN + g, lambda t: ubuf[:, t, :], rstd[:, :], done=done)
                            dve.wait_ge(evac_g, G_EVEN + g + 1)
                            if h:
                                dve.wait_ge(ct_ps, 1)
                            dve.tensor_tensor(conv_in[:, :, 2:258], ubuf[:, :, 0:TP], gbuf[:, :, 0:TP], ALU.mult)
                            dve.tensor_tensor(conv_in[:, :, 274:282], ubuf[:, :, TP:T], gbuf[:, :, TP:T], ALU.mult)
                            dve.tensor_copy(conv_in[:, :, 258:274].rearrange("p t (j b) -> p t j b", j=2),
                                            conv_st[:, 4 * h:4 * h + 4, :].rearrange("p t (b j) -> p t j b", j=2)).then_inc(conv_u, 1)
                            dve.wait_ge(conv_u, h + 1)
                        else:
                            take(G_EVEN + g, lambda t: ubuf[:, t, :], rstd[:, :], done=done)
                            dve.wait_ge(evac_g, G_EVEN + g + 1)
                            dve.tensor_tensor(gbuf[:, :, :], ubuf[:, :, :], gbuf[:, :, :], ALU.mult).then_inc(conv_y, 1)
                            dve.wait_ge(conv_h, h + 1)
                            dve.tensor_tensor(yl[:, 8 + 4 * h:12 + 4 * h, :], gbuf[:, :, :], yh[:, 8 + 4 * h:12 + 4 * h, :].bitcast(F32),
                                              ALU.subtract).then_inc(conv_l, 1)
                if u in (40, 64):
                    conv((u - 40) // 24)
                for q, (c0, n) in enumerate(((0, 4), (4, 4), (8, 2))):
                    cs = slice(c0, c0 + n)
                    gain = vec[:, V_Q:V_Q + 1] if q < 2 else vec[:, V_K:V_K + 1]
                    if u == IN_UNITS * q + 9:
                        dve.wait_ge(qstd, q + 1)
                        own(dve.reciprocal(ubuf[:, 0:n, :], ubuf[:, 0:n, :]))
                        dve.scalar_tensor_tensor(qk[:, cs, :], qk[:, cs, :], gain, ubuf[:, 0:n, :], ALU.mult, ALU.mult).then_inc(qnorm, 1)
                    if u == IN_UNITS * q + 10:
                        cos = cst[:, C_COS:C_COS + T].unsqueeze(1).broadcast_to([P, n, T])
                        sin = cst[:, C_SIN:C_SIN + T].unsqueeze(1).broadcast_to([P, n, T])
                        dve.wait_ge(qrot, q + 1)
                        dve.tensor_tensor(gbuf[:, 0:n, :], ps[:, 4:4 + n, 0:T], sin, ALU.mult)
                        own(dve.tensor_tensor(qk[:, cs, :], qk[:, cs, :], cos, ALU.mult))
                        dve.tensor_tensor(qk[:, cs, :], qk[:, cs, :], gbuf[:, 0:n, :], ALU.add).then_inc(qk_ready, 1)
                        dve.wait_ge(qk_ready, q + 1)
                at, i = (u - 28) % 4, (u - 28) // 4
                if 0 <= i < 8:
                    if at == 0:
                        row_max(i)
                        denominators(i)
                    if at == 3:
                        out_lo(i)
                if u == 59:
                    for p in range(2):
                        k = qk[:, 8 + p, TP:T].unsqueeze(1).broadcast_to([P, 4, NB])
                        ins = dve.tensor_tensor(prod[:, 32 * p:32 * p + 32].rearrange("p (c b) -> p c b", c=4),
                                                qk[:, 4 * p:4 * p + 4, TP:T], k, ALU.mult)
                    ins.then_inc(prod_ok, 1)
                if u == 61:
                    dve.wait_ge(sR_done, 1)
                    own(dve.reduce_max(small[:, 48:49], ps[:, 5, 0:P + 1], AX))
                    own(dve.scalar_tensor_tensor(small[:, 49:50], small[:, 48:49], -HD ** -0.5, nsink_col[:, :], ALU.mult, ALU.min))
                    dve.tensor_tensor(small[:, 50:51], small[:, 49:50], sink_col[:, :], ALU.add).then_inc(nS_done, 1)
                    dve.wait_ge(eS_done, 1)
                    own(dve.tensor_tensor(small[:, 51:52], small[:, 51:52], small[:, 52:53], ALU.add))
                    own(dve.reciprocal(small[:, 53:54], small[:, 51:52]))
                    own(dve.tensor_scalar(pS[:, 0:P + 1], pS[:, 0:P + 1], small[:, 53:54], None, ALU.mult))
                    dve.tensor_scalar(dg[:, :], dg[:, :], pS[:, P:P + 1], None, ALU.mult).then_inc(pS_ok, 1)
                if u == 64:
                    dve.wait_ge(pvS, 1)
                    dve.wait_ge(pTS_ok, 1)
                    for p in range(2):
                        v = vF[:, p, TP:T].unsqueeze(1).broadcast_to([P, 4, NB])
                        ins = dve.tensor_tensor(prod[:, 32 * p:32 * p + 32].rearrange("p (c b) -> p c b", c=4),
                                                pTS[:, P + 32 * p:P + 32 * p + 32].rearrange("p (c b) -> p c b", c=4), v, ALU.mult)
                    own(ins)
                    dve.tensor_tensor(prod[:, :], ps[:, 7, 0:64], prod[:, :], ALU.add).then_inc(oS_ok, 1)
                if u == 65:
                    dve.wait_ge(oh_done, 9)
                    dve.wait_ge(oS_ok, 1)
                    dve.tensor_tensor(yl[:, 0:8, TP:T], prod[:, :].rearrange("p (c b) -> p c b", c=8),
                                      yh[:, 0:8, TP:T].bitcast(F32), ALU.subtract).then_inc(o_done, 1)

            def residual(G, U, c0, i):
                h = (c0 // 4) % 2
                c = dve.snap(i * 8 + c0)
                dve.wait_ge(units_done, at_turn(dve, i, residual.step, U + 1))
                at = bass.ds(c, 4)
                dve.tensor_tensor(x[:, at, :], ps[:, 4 * h:4 * h + 4, 0:T], x[:, at, :], ALU.add).then_inc(evac_g, 1)

            def out_proj(U, G, r0, base):
                residual.step = 2 * IN_UNITS
                with dve.Fori(0, 2, 1) as i:
                    for h in range(2):
                        for j in range(IN_UNITS):
                            split_lo(dve, U + IN_UNITS * h + j + AHEAD, i=i, step=2 * IN_UNITS)
                        residual(G + h, U + IN_UNITS * (h + 1) - 1, 4 * h, i)
                        norm_rest(r0 + h, 4 * h, base, i=i)

            def ffn(layer, U, G, m):
                scale = rstd[:, :].unsqueeze(1).broadcast_to([P, 4, T])
                it = 11 * layer

                def gate_up(i, peeled):
                    for k in range(2 * IN_UNITS):
                        split_lo(dve, U + k + AHEAD, i=i, step=2 * IN_UNITS)
                        if peeled and k == 5:
                            reciprocal_std(m)
                        if k == IN_UNITS - 1:
                            dve.wait_ge(units_done, at_turn(dve, i, 2 * IN_UNITS, U + IN_UNITS))
                            for t in range(2):
                                dve.tensor_tensor(gbuf[:, 2 * t:2 * t + 2, :], ps[:, 2 * t:2 * t + 2, 0:T], scale[:, 0:2], ALU.mult
                                                  ).then_inc((gate_half, evac_g)[t], 1)
                    dve.wait_ge(units_done, at_turn(dve, i, 2 * IN_UNITS, U + 2 * IN_UNITS))
                    dve.tensor_tensor(ubuf[:, :, :], ps[:, 4:8, 0:T], scale, ALU.mult).then_inc(evac_g, 1)
                    evac_g_then = at_turn(dve, i, 2, G + 2)
                    silu_done_then = at_turn(dve, i, 1, it + 1)
                    dve.wait_ge(evac_g, evac_g_then)
                    dve.wait_ge(silu_done, silu_done_then)
                    dve.tensor_tensor(ubuf[:, :, :], ubuf[:, :, :], gbuf[:, :, :], ALU.mult).then_inc(h_ready, 1)
                    at = slice(0, 4) if i is None else bass.ds(dve.snap(i * 4), 4)
                    dve.wait_ge(hh_done, at_turn(dve, i, 1, it + 1))
                    dve.tensor_tensor(hl[:, at, :], ubuf[:, :, :], hh[:, at, :].bitcast(F32), ALU.subtract).then_inc(hid_done, 1)

                gate_up(None, True)
                with dve.Fori(1, GU_ITERS, 1) as i:
                    gate_up(i, False)
                U2, G2 = U + 2 * IN_UNITS * GU_ITERS, G + 2 * GU_ITERS
                residual.step = 2 * DN_UNITS
                if layer == 0:
                    with dve.Fori(0, 2, 1) as i:
                        for h in range(2):
                            for j in range(DN_UNITS):
                                split_lo(dve, U2 + DN_UNITS * h + j + AHEAD, i=i, step=2 * DN_UNITS)
                            residual(G2 + h, U2 + DN_UNITS * (h + 1) - 1, 4 * h, i)
                            norm_rest(8 + h, 4 * h, V_MIX + KC, i=i)
                    return
                for i in range(2):
                    for h in range(2):
                        for j in range(DN_UNITS):
                            split_lo(dve, U2 + DN_UNITS * h + j + AHEAD, i=i, step=2 * DN_UNITS)
                        c = 8 * i + 4 * h
                        stage = (gbuf, ubuf)[h]
                        dve.wait_ge(units_done, U2 + DN_UNITS * (2 * i + h + 1))
                        if i:
                            dve.wait_ge(y_ps, 2)
                        dve.tensor_tensor(stage[:, :, :], ps[:, 4 * h:4 * h + 4, 0:T], x[:, c:c + 4, :],
                                          ALU.add).then_inc(evac_g, 1)

            out_proj(U_OUT_E, G_OUT_E, 4, V_FFN)
            ffn(0, U_FFN0, G_FFN0, 1)

            take.tiles = 3 * EVEN_GROUPS
            group_end = {s0 + (IN_UNITS if c is not None else 2) - 1: q for q, (c, s0) in enumerate(zip(ODD_COLS, ODD_FIRST))}

            def gla_states(h):
                dve.wait_ge(dl_ps, h + 1)
                if h >= 2:
                    dve.wait_ge(go_ps, h - 1)
                    dve.wait_ge(d_go[h % 2], 16)
                own(dve.tensor_copy(st[:, h % 2, 0, :], ps[:, 5, 0:GDV]))
                for n in range(1, NCH):
                    ins = dve.scalar_tensor_tensor(st[:, h % 2, n, :], st[:, h % 2, n - 1, :],
                                                   acc4[:, h, CH * n + CH - 1:CH * n + CH],
                                                   ps[:, 5 + n % 2, (n // 2) * GDV:(n // 2 + 1) * GDV], ALU.mult, ALU.add)
                    if n < NCH - 1:
                        own(ins)
                ins.then_inc(st_ok, 1)

            def dec_state(q):
                b, hp = divmod(q, 2)
                dve.wait_ge(kv_o, q + 1)
                dve.wait_ge(d_gs[q % 4], 16 * (q // 4 + 1))
                for k in range(2):
                    h = 2 * hp + k
                    ins = dve.scalar_tensor_tensor(sgl[:, q % 4, k, :], sgl[:, q % 4, k, :], acc4[:, h, TP + b:TP + b + 1],
                                                   ps[:, 5 + q % 2, k * GDV:(k + 1) * GDV], ALU.mult, ALU.add)
                ins.then_inc(sg_ok, 1)

            def window_means(g):
                w, cp = WIN[g], 2 * (g % 2)
                lvl = (w.bit_length() - 2) % 2
                u = ext[:, cp:cp + 2, PB:PB + TP]
                sm = tree[:, lvl, :, 16 - w:16 - w + TP]
                new = ext[:, cp:cp + 2, 286:399:16]
                cnt = cst[:, C_CNT + 16 * g:C_CNT + 16 * g + 16].unsqueeze(1).broadcast_to([P, 2, 16])
                dve.wait_ge(tree_ok, g + 1)
                dve.wait_ge(pst_ok, g // 2 + 1)
                if g:
                    dve.wait_ge(pm_ps, 2 * g)
                dve.scalar_tensor_tensor(dmix[:, :, 16:TP], sm[:, :, 16:TP], 1.0 / w, u[:, :, 16:TP], ALU.mult, ALU.subtract)
                dve.tensor_tensor(dmix[:, :, 0:16], sm[:, :, 0:16], cnt, ALU.mult)
                own(dve.reduce_sum(small[:, 0:16].rearrange("p (c b) -> p c b", c=2),
                                   ext[:, cp:cp + 2, 271:399].rearrange("p c (b j) -> p c b j", b=NB)[:, :, :, 16 - w:16], AX))
                dve.tensor_tensor(dmix[:, :, 0:16], dmix[:, :, 0:16], u[:, :, 0:16], ALU.subtract)
                dve.scalar_tensor_tensor(dmix[:, :, TP:T], small[:, 0:16].rearrange("p (c b) -> p c b", c=2), 1.0 / w, new,
                                         ALU.mult, ALU.subtract).then_inc(dmix_ok, 1)

            for s in range(U_OUT_O - U_ODD):
                split_lo(dve, U_ODD + s + AHEAD)
                done = U_ODD + s + 1
                q = group_end.get(s)
                if s == 5:
                    reciprocal_std(2)
                if q == 0:
                    take(G_ODD, lambda t: qg[:, t, :], rstd[:, :], done=done)
                if q == 1:
                    dve.wait_ge(units_done, done)
                    dve.tensor_tensor(zr[:, :], ps[0:16, 0, 0:T], rstd[0:16, :], ALU.mult).then_inc(evac_g, 1)
                if q == 2:
                    take(G_ODD + 2, lambda t: kg[:, t, :], rstd[:, :], done=done)
                if q in (3, 4):
                    if q == 4:
                        dve.wait_ge(vt_ps, 1)
                    take(G_ODD + q, lambda t: vf[:, t, :], rstd[:, :], done=done)
                if q in (5, 6):
                    if q == 6:
                        dve.wait_ge(dmix_ok, 2)
                        dve.wait_ge(po_ps, 2)
                    for t in range(4):
                        if t == 3:
                            dve.wait_ge(units_done, done)
                        else:
                            dve.wait_ge(tile_done, take.tiles + t + 1)
                        dve.tensor_tensor(ext[:, t, PB:PB + TP], ps[:, t, 0:TP], rstd[:, 0:TP], ALU.mult)
                        dve.tensor_tensor(ext[:, t, 286:399:16], ps[:, t, TP:T], rstd[:, TP:T], ALU.mult
                                          ).then_inc(evac_g if t == 3 else evac_t, 1)
                    take.tiles += 3
                if q in (7, 8):
                    take(G_ODD + q, lambda t: gbuf[:, t, :], rstd[:, :], done=done)
                if s == 10:
                    dve.wait_ge(gk_ps, 1)
                    for h in range(GH):
                        ins = dve.tensor_scalar(acc4[:, h, :], ps[:, 4 + h, 0:T], vec[:, V_BAL + h:V_BAL + h + 1], None, ALU.add)
                    ins.then_inc(zb_ok, 1)
                    dve.memset(attS[:, :, :], 0.0)
                    dve.wait_ge(ln_ok, 1)
                    dve.wait_ge(zb_ok, 1)
                    own(dve.scalar_tensor_tensor(acc4[:, :, :], acc4[:, :, :], 0.0, sq4[:, :, :], ALU.min, ALU.subtract))
                    dve.wait_ge(d0_ok, 3)
                    flat = [z[:, :, :].rearrange("p h t -> p (h t)") for z in (gbuf, d0, acc4)]
                    dve.tensor_tensor_scan(flat[0], flat[1], flat[2], 0.0, ALU.mult, ALU.add).then_inc(b_ok, 1)
                if s == 17:
                    scale = GDK ** -0.5
                    dve.wait_ge(eb_ok, 1)
                    dve.wait_ge(evac_g, G_ODD + 3)
                    dve.wait_ge(b_ok, 1)
                    own(dve.tensor_scalar(qsamp[:, :, :], qg[:, :, TP:T], scale, None, ALU.mult))
                    dve.scalar_tensor_tensor(qg[:, :, :], qg[:, :, :], scale, acc4[:, :, :], ALU.mult, ALU.mult)
                    dve.tensor_tensor(sq4[:, :, :], kg[:, :, :], sq4[:, :, :], ALU.mult).then_inc(kd_ok, 1)
                    bb = gbuf[:, :, 0:TP].rearrange("p h (n t) -> p h n t", n=NCH)
                    dve.tensor_tensor(ubuf[:, :, 0:TP].rearrange("p h (n t) -> p h n t", n=NCH),
                                      bb[:, :, :, CH - 1:CH].broadcast_to([P, GH, NCH, CH]), bb, ALU.subtract).then_inc(df_ok, 1)
                    dve.wait_ge(edf_ok, 1)
                    dve.tensor_tensor(ubuf[:, :, 0:TP], kg[:, :, 0:TP], ubuf[:, :, 0:TP], ALU.mult).then_inc(k2_ok, 1)
                if s == 19:
                    dve.wait_ge(att_ps, 1)
                    dve.wait_ge(k2_ok, 1)
                    mask = cst[:, C_TRI:C_TRI + CH].bitcast(I32).unsqueeze(1).broadcast_to([P, 8, CH])
                    dve.copy_predicated(attS[:, :, :], mask, ps[:, 4, :].rearrange("p (q c) -> p q c", q=8)).then_inc(att_ok, 1)
                for k, h in ((28, 0), (30, 1), (36, 2), (38, 3)):
                    if s == k:
                        gla_states(h)
                if s == 39:
                    dve.wait_ge(k2t_ps, 1)
                    dve.wait_ge(vt_ps, 2)
                    dve.wait_ge(k2_ok, 1)
                    dve.memset(ext[:, :, 0:PB], 0.0).then_inc(pad_ok, 1)
                if 0 <= s - 40 < 16:
                    dec_state(s - 40)
                for half in range(2):
                    if s == 42 + 8 * half:
                        window_means(2 * half)
                    if 44 + 8 * half <= s < 48 + 8 * half:
                        c = 4 * half + s - 44 - 8 * half
                        dve.wait_ge(pmh, c + 1)
                        dve.scalar_tensor_tensor(yl[:, 8 + c, :], ps[:, 4, 0:T], vec[:, V_PSC + c:V_PSC + c + 1],
                                                 yh[:, 8 + c, :].bitcast(F32), ALU.mult, ALU.subtract).then_inc(pml, 1)
                    if s == 45 + 8 * half:
                        window_means(2 * half + 1)
                    if s == 57 + 2 * half:
                        dve.wait_ge(ostd, half + 1)
                        dve.wait_ge(go_ok, 4)
                        own(dve.reciprocal(rst2[:, :, :], rst2[:, :, :]))
                        for t in range(4):
                            c = 4 * half + t
                            ins = dve.scalar_tensor_tensor(oF[:, c, :], oF[:, c, :], vec[:, V_GLA + c % 2:V_GLA + c % 2 + 1],
                                                           rst2[:, t // 2, :], ALU.mult, ALU.mult)
                        own(ins)
                    if s == 57 + 8 * half:
                        hs = slice(4 * half, 4 * half + 4)
                        dve.wait_ge(sg_silu, half + 1)
                        dve.tensor_tensor(oF[:, hs, :], oF[:, hs, :], gbuf[:, :, :], ALU.mult).then_inc(oc_ok, 1)
                        dve.wait_ge(och, half + 1)
                        dve.wait_ge(oc_ok, half + 1)
                        dve.tensor_tensor(yl[:, hs, :], oF[:, hs, :], yh[:, hs, :].bitcast(F32), ALU.subtract).then_inc(ocl, 1)

            out_proj(U_OUT_O, G_OUT_O, 12, V_FFN + KC)
            ffn(1, U_FFN1, G_FFN1, 3)

        @block.gpsimd
        def _(pool):
            steps = [0]

            def own(ins):
                steps[0] += 1
                ins.then_inc(pl, 1)
                pool.wait_ge(pl, steps[0])

            def add_squares(m):
                for g in range(4):
                    pool.wait_ge(sq_done, 4 * m + g + 1)
                    if g:
                        pool.wait_ge(acc_done, 4 * m + g)
                    if g == 0:
                        pool.tensor_copy(acc4[:, :, :], sq4[:, :, :]).then_inc(acc_done, 1)
                    else:
                        pool.tensor_tensor(acc4[:, :, :], acc4[:, :, :], sq4[:, :, :], ALU.add).then_inc(acc_done, 1)

            pool.memset(eps[:, :], EPS).then_inc(ms_done, 1)
            pool.memset(ones[:, :], 1.0).then_inc(ms_done, 1)
            pool.wait_ge(ms_done, 2)
            pool.memset(small[:, :], 0.0).then_inc(y_ok, 2)
            add_squares(0)
            for i in range(8):
                nk, b = P * (i // NKV + 1), 24 * (i % 2)
                pool.wait_ge(rec_done, i + 1)
                for g in range(GRP):
                    ins = pool.tensor_scalar(prob[:, i % 2, g, 0:nk], prob[:, i % 2, g, 0:nk],
                                             small[:, b + 20 + g:b + 21 + g], None, ALU.mult)
                ins.then_inc(pn_done, 1)
            add_squares(1)
            add_squares(2)
            pool.wait_ge(evac_g, G_ODD)
            pool.wait_ge(units_done, U_ODD)
            own(pool.memset(d0[:, :, :], 1.0))
            pool.wait_ge(ms_done, 2)
            pool.memset(d0[:, :, 0:TP:CH], 0.0).then_inc(d0_ok, 2)
            pool.memset(d0[:, :, TP:T], 0.0).then_inc(d0_ok, 1)

            def key_rows(b):
                pool.wait_ge(k2t_ok, 1)
                if b >= 2:
                    pool.wait_ge(kv_o, 2 * b - 2)
                pool.tensor_scalar(kdiag[:, b % 2, :], ktS[:, :], ident[0:NB, b:b + 1], None, ALU.mult).then_inc(kdg, 1)

            def window_sums(g):
                w, cp = WIN[g], 2 * (g % 2)
                pool.wait_ge(evac_g, G_ODD + 6 + g // 2)
                pool.wait_ge(pad_ok, 1)
                pool.wait_ge(b_ok, 1)
                if g:
                    pool.wait_ge(dmix_ok, g)
                src = ext[:, cp:cp + 2, 0:PB + TP]
                k, n, lvl = 1, PB + TP, 0
                while k < w:
                    n -= k
                    dst = tree[:, lvl, :, 0:n]
                    ins = pool.tensor_tensor(dst, src[:, :, 0:n], src[:, :, k:k + n], ALU.add)
                    k *= 2
                    if k < w:
                        own(ins)
                    src, lvl = dst, 1 - lvl
                ins.then_inc(tree_ok, 1)

            for b in range(NB):
                key_rows(b)
                if b in (0, 1):
                    window_sums(b)
                if b in (4, 5):
                    window_sums(b - 2)
            add_squares(3)


_INS = ["x_prompt", "x_sample", "cache_swa_k", "cache_swa_v", "state_conv", "state_gla", "state_pool",
        "norm_mix", "norm_ffn", "w_in_even", "w_out_even", "q_norm", "k_norm", "attn_sinks", "conv_w",
        "w_in_odd", "w_out_odd", "w_alpha_up", "b_alpha", "gla_out_norm", "w_pool", "pool_scale",
        "w_gate", "w_up", "w_down"]
_OUTS = [(1, TP, D), (NB, 1, D), (1, 1, P, NKV, HD), (1, 1, P, NKV, HD), (1, 1, 2, 1024), (1, 1, GH, GDK, GDV),
         (1, 1, PB, 1024), (1, NB, P, NKV, HD), (1, NB, P, NKV, HD), (1, NB, 2, 1024), (1, NB, GH, GDK, GDV),
         (1, NB, PB, 1024)]


def kernel(**inputs):
    import concourse.bacc as bacc
    from concourse.bass_utils import run_bass_kernel_spmd

    arrays = {n: np.ascontiguousarray(inputs[n]) for n in _INS}
    arrays["consts"] = constants()
    nc = bacc.Bacc("TRN2", target_bir_lowering=False, num_devices=1, dynamic_dma_scratch_size=256)
    a = {n: nc.dram_tensor(f"in_{n}", v.shape, F32, kind="ExternalInput").ap() for n, v in arrays.items()}
    o = [nc.dram_tensor(f"out_{i}", s, F32, kind="ExternalOutput").ap() for i, s in enumerate(_OUTS)]
    decoder_step(nc, a, o)
    r = run_bass_kernel_spmd(nc, [{f"in_{n}": v for n, v in arrays.items()}], core_ids=[0])
    return tuple(r.results[0][f"out_{i}"] for i in range(len(_OUTS)))
```

```python
from contextlib import ExitStack

import numpy as np

import concourse.bass as bass
from concourse import mybir

F32 = mybir.dt.float32
F32R = mybir.dt.float32r
BF16 = mybir.dt.bfloat16
I32 = mybir.dt.int32
ALU = mybir.AluOpType
ACT = mybir.ActivationFunctionType
AX = mybir.AxisListType.X

P = 128
D = 2048
TP, NB = 256, 8
T = TP + NB
KC = D // P
FF = 5632
FC = FF // P
HD, NH, NKV, GRP = 64, 16, 4, 4
PAST = 2048
EPS = 1e-6
GH, GDK, GDV = 4, 128, 256
CH = 64
NCH = TP // CH
WIN = (2, 4, 8, 16)
PB = 15
COLS = 512
RING = 4
AHEAD = 3

IN_UNITS = KC // 2
EVEN_GROUPS = 9
ATT = 31
U_EVEN = 0
U_OUT_E = U_EVEN + EVEN_GROUPS * IN_UNITS
U_FFN0 = U_OUT_E + 4 * IN_UNITS
GU_ITERS = FF // COLS
DN_UNITS = FC // 2
U_DN0 = U_FFN0 + GU_ITERS * 2 * IN_UNITS
U_ODD = U_DN0 + 4 * DN_UNITS
U_OUT_O = U_ODD + 8 * IN_UNITS + 2
U_FFN1 = U_OUT_O + 4 * IN_UNITS
U_DN1 = U_FFN1 + GU_ITERS * 2 * IN_UNITS
U_END = U_DN1 + 4 * DN_UNITS

G_EVEN = 4
G_OUT_E = G_EVEN + EVEN_GROUPS
G_FFN0 = G_OUT_E + 4
G_DN0 = G_FFN0 + 2 * GU_ITERS
G_ODD = G_DN0 + 4
G_OUT_O = G_ODD + 9
G_FFN1 = G_OUT_O + 4
G_DN1 = G_FFN1 + 2 * GU_ITERS

V_MIX, V_FFN, V_CONV, V_PSC, V_BAL, V_GLA, V_Q, V_K = 0, 32, 64, 88, 96, 100, 102, 103
NVEC = 104

C_ID, C_BLK, C_ROT, C_COS, C_SIN, C_MASK, C_TRI, C_CNT = 0, 128, 256, 384, 648, 912, 1168, 1232
C_ROW = C_CNT + 4 * 16
C_ALL = C_ROW + NB
K3 = 72

OUT_E_ORDER = (4, 5, 6, 0, 1, 2, 3, 7)
ATTN_UNITS = (3, 4, 5, 6)
OUT_O_ORDER = (4, 5, 6, 7, 0, 1, 2, 3)
ZR = 3072
ODD_COLS = (0, None, 512, 1024, 1536, 3088, 3600, 2048, 2560)
ODD_FIRST = (0, 8, 10, 18, 26, 34, 42, 50, 58)


def constants():
    c = np.zeros((P, C_ALL), np.float32)
    r = np.arange(P)
    c[:, C_ID:C_ID + P] = np.eye(P)
    c[:, C_BLK:C_BLK + P] = (r[:, None] // HD) == (r[None, :] // HD)
    half = HD // 2
    for m in range(P):
        if m % HD < half:
            c[m + half, C_ROT + m] = -1.0
        else:
            c[m - half, C_ROT + m] = 1.0
    inv = np.power(10000.0, -np.arange(half) / half).astype(np.float32)
    pos = np.concatenate([np.arange(TP), np.full(NB, PAST)]).astype(np.float32)
    ang = (pos[None, :] * inv[r % half][:, None]).astype(np.float32)
    c[:, C_COS:C_COS + T] = np.cos(ang)
    c[:, C_SIN:C_SIN + T] = np.sin(ang)
    k = np.arange(P)
    c[:, C_MASK:C_MASK + P] = np.where(k[None, :] >= r[:, None], 0.0, -1e30)
    c[:, C_MASK + P:C_MASK + 2 * P] = np.where(k[None, :] <= r[:, None], 0.0, -1e30)
    c[:, C_TRI:C_TRI + CH] = (r % CH)[:, None] <= np.arange(CH)[None, :]
    for k in (0, 32, 64):
        c[k:k + NB, C_ROW:C_ROW + NB] = np.eye(NB)
    for g, w in enumerate(WIN):
        c[:, C_CNT + 16 * g:C_CNT + 16 * g + 16] = np.float32(1.0) / np.minimum(w, np.arange(16) + 1).astype(np.float32)
    return c


def vectors(a):
    rows = [a[n].reshape(-1, P) for n in ("norm_mix", "norm_ffn", "conv_w", "pool_scale", "b_alpha", "gla_out_norm")]
    rows += [np.concatenate([a[n], a[n]], axis=1) for n in ("q_norm", "k_norm")]
    return np.ascontiguousarray(np.concatenate(rows, axis=0).T)


def decoder_step(nc, a, o):
    (y_prompt, y_sample, o_kp, o_vp, o_cp, o_gp, o_pp, o_ks, o_vs, o_cs, o_gs, o_ps) = o
    w_even, w_out_e = a["w_in_even"][0], a["w_out_even"][0]
    w_odd, w_out_o = a["w_in_odd"][0], a["w_out_odd"][0]

    ctx = ExitStack()
    with ctx:
        def sem(name):
            return ctx.enter_context(nc.semaphore(name))

        used = {}

        def put(name, shape, at, dt=F32):
            size = 1
            for s in shape[1:]:
                size *= s
            size *= 2 if dt == BF16 else 4
            used[name] = (at, at + size)
            return nc.alloc_sbuf_tensor_at(name, shape, dt, offset=at)

        def after(name):
            return (used[name][1] + 31) // 32 * 32

        x = put("x", [P, KC, T], 1024)
        xh = put("xh", [P, KC, T], after("x"), F32R)
        xl = put("xl", [P, KC, T], after("xh"), F32R)
        raw = put("raw", [P, RING, 2 * COLS], after("xl"))
        whi = put("whi", [P, RING, 2 * COLS], after("raw"), F32R)
        wlo = put("wlo", [P, RING, 2 * COLS], after("whi"), F32R)
        hh = put("hh", [P, FC, T], after("wlo"), F32R)
        hl = put("hl", [P, FC, T], after("hh"), F32R)
        sqs = put("sqs", [P, 2, 4, T], after("hl"))
        acc4, sq4 = sqs[:, 0, :, :], sqs[:, 1, :, :]
        gbuf = put("gbuf", [P, 4, T], after("sqs"))
        ubuf = put("ubuf", [P, 4, T], after("gbuf"))
        rstd = put("rstd", [P, T], after("ubuf"))
        seed = put("seed", [P, T], after("rstd"))
        ones = put("ones", [P, P], after("seed"))
        cst = put("cst", [P, C_ALL], after("ones"))
        vec = put("vec", [P, NVEC], after("cst"))
        maskb = put("maskb", [P, 2 * P], after("vec"), BF16)
        identb = put("identb", [P, P], after("maskb"), BF16)
        eps = put("eps", [P, 1], after("identb"))
        small = put("small", [P, 64], after("eps"))
        spare = after("small")
        assert spare <= 229344
        ident = cst[:, C_ID:C_ID + P]
        blk = cst[:, C_BLK:C_BLK + P]
        rot = cst[:, C_ROT:C_ROT + P]
        ya, yb = used["hh"][0], used["hl"][0]
        reg_a, end_a = ya + KC * T * 4, used["hh"][1]
        reg_b, end_b = yb + KC * T * 4, used["hl"][1]

        xtok = put("xtok", [P, 2, D], reg_a)
        xtok_s = put("xtok_s", [NB, D], after("xtok"))
        assert after("xtok_s") <= end_a

        kc = put("kc", [P, NB, 256], reg_b)
        prob = put("prob", [P, 2, 4, 256], reg_b)
        vc = put("vc", [P, NB, 256], after("kc"))
        kcT = put("kcT", [P, 2 * NB, P], after("vc"))
        cst_rows = put("cst_rows", [16, 1024], after("kcT"))
        assert after("cst_rows") <= end_b
        qk = put("qk", [P, 10, T], reg_a)
        vF = put("vF", [P, 2, T], after("qk"))
        kT1 = put("kT1", [P, 256], after("vF"))
        vT = put("vT", [P, 2, 256], after("kT1"))
        kvS = put("kvS", [NB, 512], after("vT"))
        pT = put("pT", [P, 2, 512], after("kvS"))
        conv_in = put("conv_in", [P, 4, 282], after("pT"))
        assert after("conv_in") <= end_a
        conv_tok = put("conv_tok", [NB, 2, COLS], spare)
        conv_st = put("conv_st", [P, 8, 16], after("conv_tok"))
        sT = put("sT", [P, P], after("conv_st"))
        pS = put("pS", [P, 132], after("sT"))
        pTS = put("pTS", [P, 192], after("pS"))
        prod = put("prod", [P, 64], after("pTS"))
        dg = put("dg", [P, 64], after("prod"))
        sink_row = put("sink_row", [P, 16], after("dg"))
        sink_col = put("sink_col", [P, 1], after("sink_row"))
        nsink_row = put("nsink_row", [P, 16], after("sink_col"))
        nsink_col = put("nsink_col", [P, 1], after("nsink_row"))
        qd = put("qd", [P, 2, NB, 2, 4], after("nsink_col"))
        assert after("qd") <= 229344, after("qd")

        yh, yl = hh, hl

        vtok = put("vtok", [P, 2, 1024], ya)
        oF = put("oF", [P, 8, T], yb)
        qg = put("qg", [P, 4, T], reg_a)
        kg = put("kg", [P, 4, T], after("qg"))
        vf = put("vf", [P, 4, T], after("kg"))
        ext = put("ext", [P, 4, 399], used["kg"][0])
        assert after("ext") <= after("vf")
        v3 = put("v3", [K3, 1024], after("vf"), F32R)
        k3 = put("k3", [K3, 512], after("v3"), F32R)
        kdiag = put("kdiag", [K3, 2, 512], after("k3"), F32R)
        attS = put("attS", [P, 8, CH], after("kdiag"))
        zr = put("zr", [16, T], after("attS"))
        qsamp = put("qsamp", [P, 4, NB], after("zr"))
        assert after("qsamp") <= end_a, (after("qsamp"), end_a)
        k2t = put("k2t", [P, 2, 512], reg_b)
        st = put("st", [P, 2, 4, 256], after("k2t"))
        wpool = put("wpool", [P, 8, 256], after("k2t"))
        sgl = put("sgl", [P, 4, 2, 256], after("st"))
        d0 = put("d0", [P, 4, T], after("sgl"))
        tree = put("tree", [P, 2, 2, 272], after("sgl"))
        dmix = put("dmix", [P, 2, T], after("tree"))
        wup = put("wup", [16, 512], after("dmix"))
        assert after("wup") <= end_b, (after("wup"), end_b)
        prow = put("prow", [120, 1024], spare)
        ptok = put("ptok", [16, 2, COLS], after("prow"))
        assert after("ptok") <= 229344, after("ptok")

        ps = ctx.enter_context(nc.psum_tensor("ps", [P, 8, 512], F32))
        psf = ps[:, :, :].rearrange("p b n -> p (b n)")

        raw_full = [sem(f"raw_full{s}") for s in range(RING)]
        raw_up = [sem(f"raw_up{s}") for s in range(RING)]
        hi_done = sem("hi_done")
        lo_done = sem("lo_done")
        units_done = sem("units_done")
        tile_done = sem("tile_done")
        evac_t = sem("evac_t")
        evac_g = sem("evac_g")
        head_done = sem("head_done")
        xh_done = sem("xh_done")
        xl_done = sem("xl_done")
        sq_done = sem("sq_done")
        acc_sum = sem("acc_sum")
        acc_done = sem("acc_done")
        ss_done = sem("ss_done")
        std_done = sem("std_done")
        rstd_done = sem("rstd_done")
        silu_done = sem("silu_done")
        h_ready = sem("h_ready")
        hh_done = sem("hh_done")
        hid_done = sem("hid_done")
        d_x = [sem(f"d_x{g}") for g in range(4)]
        d_xs = sem("d_xs")
        d_id = sem("d_id")
        d_cst = sem("d_cst")
        d_vec = sem("d_vec")
        d_even = sem("d_even")
        d_sink = sem("d_sink")
        d_odd = sem("d_odd")
        d_out = sem("d_out")
        ms_done = sem("ms_done")
        maskb_ok = sem("maskb_ok")
        dv = sem("dv")
        kcT_ps = sem("kcT_ps")
        kcT_ok = sem("kcT_ok")
        cst_ps = sem("cst_ps")
        cst_ok = sem("cst_ok")
        qsq = sem("qsq")
        qss = sem("qss")
        qstd = sem("qstd")
        qnorm = sem("qnorm")
        qrot = sem("qrot")
        qk_ready = sem("qk_ready")
        kv_ps = sem("kv_ps")
        kv_tok = sem("kv_tok")
        sc_done = sem("sc_done")
        negm_done = sem("negm_done")
        exp_done = sem("exp_done")
        pn_done = sem("pn_done")
        pt_done = sem("pt_done")
        pT_ok = sem("pT_ok")
        pv_done = sem("pv_done")
        oh_done = sem("oh_done")
        o_done = sem("o_done")
        qd_ok = sem("qd_ok")
        sS_done = sem("sS_done")
        sT_ok = sem("sT_ok")
        sR_done = sem("sR_done")
        nS_done = sem("nS_done")
        eS_done = sem("eS_done")
        pS_ok = sem("pS_ok")
        pTS_ps = sem("pTS_ps")
        pTS_ok = sem("pTS_ok")
        pvS = sem("pvS")
        prod_ok = sem("prod_ok")
        oS_ok = sem("oS_ok")
        conv_u = sem("conv_u")
        conv_y = sem("conv_y")
        conv_h = sem("conv_h")
        conv_l = sem("conv_l")
        ct_ps = sem("ct_ps")
        ct_ok = sem("ct_ok")
        gk_ps = sem("gk_ps")
        zb_ok = sem("zb_ok")
        ln_ok = sem("ln_ok")
        b_ok = sem("b_ok")
        eb_ok = sem("eb_ok")
        kd_ok = sem("kd_ok")
        df_ok = sem("df_ok")
        edf_ok = sem("edf_ok")
        k2_ok = sem("k2_ok")
        att_ps = sem("att_ps")
        att_ok = sem("att_ok")
        k2t_ps = sem("k2t_ps")
        k2t_ok = sem("k2t_ok")
        vt_ps = sem("vt_ps")
        vt_ok = sem("vt_ok")
        dl_ps = sem("dl_ps")
        st_ok = sem("st_ok")
        go_ps = sem("go_ps")
        go_ok = sem("go_ok")
        d_gs = [sem(f"d_gs{k}") for k in range(4)]
        d_gso = [sem(f"d_gso{k}") for k in range(4)]
        d_go = [sem("d_go0"), sem("d_go1")]
        kdg = sem("kdg")
        pad3_ok = sem("pad3_ok")
        lo3_ok = sem("lo3_ok")
        kv_o = sem("kv_o")
        sg_ok = sem("sg_ok")
        so_ps = sem("so_ps")
        osq = sem("osq")
        oss = sem("oss")
        ostd = sem("ostd")
        sg_silu = sem("sg_silu")
        oc_ok = sem("oc_ok")
        och = sem("och")
        ocl = sem("ocl")
        pst_ps = sem("pst_ps")
        pst_ok = sem("pst_ok")
        tree_ok = sem("tree_ok")
        dmix_ok = sem("dmix_ok")
        pm_ps = sem("pm_ps")
        pmh = sem("pmh")
        pml = sem("pml")
        po_ps = sem("po_ps")
        po_ok = sem("po_ok")
        d_wp = sem("d_wp")
        d_prow = sem("d_prow")
        d_pt = [sem("d_pt0"), sem("d_pt1")]
        d_ct = sem("d_ct")
        d_kc = sem("d_kc")
        ac = sem("ac")
        pl = sem("pl")
        d0_ok = sem("d0_ok")
        pad_ok = sem("pad_ok")
        y_ps = sem("y_ps")
        y_ok = sem("y_ok")
        d_y = sem("d_y")

        def at_turn(eng, i, step, first):
            if i is None:
                return first
            return i * step + first if isinstance(i, int) else eng.snap(i * step + first)

        def pieces(buf, n, split=False):
            slot = buf[:, n % RING, :]
            if n >= U_EVEN + 2 * IN_UNITS:
                return [slot]
            order = "p (q h d) -> p h q d" if split else "p (h q d) -> p h q d"
            return [slot[:, k * COLS:(k + 1) * COLS].rearrange(order, h=2, q=4) for k in range(2)]

        def beyond(n, i, step):
            return n + (i * step if isinstance(i, int) else 0) >= U_END

        def split_hi(act, n, i=None, step=0, up=None):
            if beyond(n, i, step):
                return
            landed = at_turn(act, i, 16 * step // RING, 16 * (n // RING + 1))
            if up is not None:
                up = at_turn(act, i, up[1], up[0])
            free = at_turn(act, i, step, n - RING + 1)
            act.wait_ge(raw_full[n % RING], landed)
            if up is not None:
                act.wait_ge(raw_up[n % RING], up)
            if n >= RING:
                act.wait_ge(units_done, free)
            for dst, src in zip(pieces(whi, n, True), pieces(raw, n)):
                ins = act.activation(dst, src, ACT.Copy)
            ins.then_inc(hi_done, 1)

        def split_lo(dve, n, i=None, step=0):
            if beyond(n, i, step):
                return
            dve.wait_ge(hi_done, at_turn(dve, i, step, n + 1))
            for dst, src, hi in zip(pieces(wlo, n, True), pieces(raw, n), pieces(whi, n, True)):
                ins = dve.tensor_tensor(dst, src, hi.bitcast(F32), ALU.subtract)
            ins.then_inc(lo_done, 1)

        block = ctx.enter_context(nc.Block())

        @block.sync
        def _(sp):
            def load(n, w, row, col, i=None, step=0, up=None):
                p = P if up is None else HD
                src = [w[r:r + 2 * p, :].rearrange("(k p) n -> p k n", p=p)[:, :, bass.ds(col, COLS)] for r in (row, up or row)]
                if n >= RING:
                    sp.wait_ge(lo_done, at_turn(sp, i, step, n - RING + 1))
                dst = raw[:, n % RING, :].rearrange("p (k n) -> p k n", k=2)
                sp.dma_start(dst[0:p], src[0]).then_inc(raw_full[n % RING], 16)
                if up is not None:
                    sp.dma_start(dst[p:P], src[1]).then_inc(raw_up[n % RING], 16)

            for g in range(3):
                for j in range(IN_UNITS):
                    if g == 0 and j < 4:
                        cs = slice(j * COLS, (j + 1) * COLS)
                        sp.dma_start(xtok[:, :, cs], a["x_prompt"][0].rearrange("(q p) d -> p q d", q=2)[:, :, cs]
                                     ).then_inc(d_x[j], 16)
                    load(U_EVEN + IN_UNITS * g + j, w_even, 2 * P * j, COLS * g)
            n0 = U_EVEN + 3 * IN_UNITS
            with sp.Fori(0, 2, 1) as i:
                for g, base in enumerate((2560, 3584, 1536)):
                    col = sp.snap(i * COLS + base)
                    for j in range(IN_UNITS):
                        load(n0 + IN_UNITS * g + j, w_even, 2 * P * j, col, i=i, step=3 * IN_UNITS)
            with sp.Fori(0, 2, 1) as i:
                for h in range(2):
                    col = i * (2 * COLS) + COLS * h
                    for j in range(IN_UNITS):
                        n = U_OUT_E + IN_UNITS * h + j
                        if j not in ATTN_UNITS:
                            load(n, w_out_e, 2 * P * OUT_E_ORDER[j], col, i=i, step=2 * IN_UNITS)
                            continue
                        c = 2 * OUT_E_ORDER[j]
                        lower = (8 * (c // 4) + c % 4) * HD
                        load(n, w_out_e, lower, col if lower else (i * 2 + h) * COLS, i=i, step=2 * IN_UNITS, up=lower + 4 * HD)

            def ffn(layer, n_gu, n_dn):
                with sp.Fori(0, GU_ITERS, 1) as i:
                    col = sp.snap(i * COLS)
                    for h, w in enumerate((a["w_gate"][layer], a["w_up"][layer])):
                        for j in range(IN_UNITS):
                            load(n_gu + IN_UNITS * h + j, w, 2 * P * j, col, i=i, step=2 * IN_UNITS)
                with sp.Fori(0, 2, 1) as i:
                    for h in range(2):
                        col = i * (2 * COLS) + COLS * h
                        for j in range(DN_UNITS):
                            load(n_dn + DN_UNITS * h + j, a["w_down"][layer], 2 * P * j, col, i=i, step=2 * DN_UNITS)

            ffn(0, U_FFN0, U_DN0)
            n = U_ODD
            for base in ODD_COLS:
                if base is None:
                    for j in range(2):
                        sp.wait_ge(lo_done, n - RING + 1)
                        sp.dma_start(raw[:, n % RING, :].rearrange("p (k n) -> p k n", k=8),
                                     w_odd[8 * P * j:8 * P * (j + 1), ZR:ZR + P].rearrange("(k p) n -> p k n", p=P)
                                     ).then_inc(raw_full[n % RING], 16)
                        n += 1
                else:
                    for j in range(IN_UNITS):
                        load(n, w_odd, 2 * P * j, base)
                        n += 1
            assert n == U_OUT_O
            with sp.Fori(0, 2, 1) as i:
                for h in range(2):
                    col = i * (2 * COLS) + COLS * h
                    for j in range(IN_UNITS):
                        row = 2 * P * OUT_O_ORDER[j]
                        load(U_OUT_O + IN_UNITS * h + j, w_out_o, row, col if row else (i * 2 + h) * COLS, i=i, step=2 * IN_UNITS)
            ffn(1, U_FFN1, U_DN1)

        @block.tensor
        def _(pe):
            def unit(n, yhi, ylo, k0, bank, first, last, i=None, step=0, taken=None, single=False):
                pe.wait_ge(lo_done, at_turn(pe, i, step, n + 1))
                s = n % RING
                for t in range(4):
                    if taken is not None and t < 3:
                        pe.wait_ge(evac_t, taken[0] + t)
                    if taken is not None and t == 3:
                        pe.wait_ge(evac_g, taken[1])
                    for kk in range(2):
                        c = kk * COLS + t * P
                        for m, (w, r) in enumerate(((whi, yhi), (whi, ylo), (wlo, yhi))):
                            mm = pe.matmul(ps[:, bank + t, 0:T], w[:, s, c:c + P], r[:, k0 + kk, :],
                                           start=first and kk == 0 and m == 0, stop=last and kk == 1 and m == 2)
                    if single and last and t < 3:
                        mm.then_inc(tile_done, 1)
                mm.then_inc(units_done, 1)

            def norm_sum(m):
                if m == 0:
                    pe.wait_ge(acc_done, 3)
                    chunks = 4
                else:
                    pe.wait_ge(acc_sum, m)
                    chunks = 1
                for t in range(chunks):
                    mm = pe.matmul(ps[:, 4, 0:T], ones[:, :], acc4[:, t, :], start=t == 0, stop=t == chunks - 1)
                mm.then_inc(ss_done, 1)

            def input_T(g):
                pe.wait_ge(d_x[g], 16)
                if g:
                    pe.wait_ge(evac_g, g)
                for t in range(4):
                    c = 4 * g + t
                    for q in range(2):
                        pe.transpose(ps[:, 4 + t, q * P:(q + 1) * P], xtok[:, q, c * P:(c + 1) * P], ident)
                    mm = pe.transpose(ps[:, 4 + t, TP:T], xtok_s[:, c * P:(c + 1) * P], ident[0:NB, 0:NB])
                mm.then_inc(head_done, 1)

            pe.wait_ge(d_id, 16)
            pe.wait_ge(d_xs, 16)
            input_T(0)
            input_T(1)
            pe.wait_ge(d_cst, 16)

            def cache_T():
                pe.wait_ge(d_kc, 16)
                pe.wait_ge(qk_ready, 1)
                for b in range(NB):
                    for p in range(2):
                        q = 2 * b + p
                        mm = pe.transpose(psf[:, 4 * 512 + q * P:4 * 512 + (q + 1) * P], kc[:, b, p * P:(p + 1) * P], ident)
                mm.then_inc(kcT_ps, 1)

            def conv_state_T():
                pe.wait_ge(d_even, 16 * 2)
                pe.wait_ge(kcT_ok, 1)
                for c in range(8):
                    mm = pe.transpose(ps[:, 4, c * 16:(c + 1) * 16], cst_rows[:, c * P:(c + 1) * P], ident[0:16, 0:16])
                mm.then_inc(cst_ps, 1)

            def qk_sum(q, n):
                pe.wait_ge(qsq, q + 1)
                if q == 0:
                    pe.wait_ge(std_done, 1)
                if q == 1:
                    pe.wait_ge(cst_ok, 1)
                if q == 2:
                    pe.wait_ge(qk_ready, q)
                for t in range(n):
                    mm = pe.matmul(ps[:, 4 + t, 0:T], blk, sq4[:, t, :], start=True, stop=True)
                mm.then_inc(qss, 1)

            def qk_rot(q, c0, n):
                pe.wait_ge(qnorm, q + 1)
                for t in range(n):
                    mm = pe.matmul(ps[:, 4 + t, 0:T], rot, qk[:, c0 + t, :], start=True, stop=True)
                mm.then_inc(qrot, 1)

            def kv_T():
                pe.wait_ge(qk_ready, 3)
                for p in range(2):
                    cs = slice(p * P, (p + 1) * P)
                    cs2 = slice(256 + p * P, 256 + (p + 1) * P)
                    pe.transpose(ps[:, 4, cs], qk[:, 8 + p, P:2 * P], ident)
                    pe.transpose(ps[:, 4, cs2], vF[:, p, 0:P], ident)
                    pe.transpose(ps[:, 5, cs], vF[:, p, P:2 * P], ident)
                    pe.matmul(ps[0:NB, 6, cs], qk[:, 8 + p, TP:T], ident, start=True, stop=True)
                    mm = pe.matmul(ps[0:NB, 6, cs2], vF[:, p, TP:T], ident, start=True, stop=True)
                mm.then_inc(kv_ps, 1)

            def item(i):
                q, kv = divmod(i, NKV)
                return q, kv, kv // 2, HD * (kv % 2), P * (q + 1)

            def scores(i):
                q, kv, p, r, nk = item(i)
                pe.wait_ge(kv_tok, 1)
                pe.wait_ge(maskb_ok, 2)
                if i:
                    pe.wait_ge(exp_done, i)
                if i == NKV:
                    pe.wait_ge(ct_ok, 1)
                for g in range(GRP):
                    out = psf[:, 4 * 512 + g * nk:4 * 512 + (g + 1) * nk]
                    pe.matmul(out, qk[r:r + HD, 4 * p + g, q * P:(q + 1) * P], qk[r:r + HD, 8 + p, 0:nk],
                              start=True, stop=False)
                    mm = pe.matmul(out, identb[:, :], maskb[:, 2 * P - nk:2 * P], start=False, stop=True)
                mm.then_inc(sc_done, 1)

            def probs_T(i):
                q, kv, p, r, nk = item(i)
                pe.wait_ge(pn_done, i + 1)
                if i:
                    pe.wait_ge(o_done, i)
                for kb in range(nk // P):
                    for g in range(GRP):
                        mm = pe.transpose(ps[:, 6 + kb, g * P:(g + 1) * P], prob[:, i % 2, g, kb * P:(kb + 1) * P], ident)
                mm.then_inc(pt_done, 1)

            def attend(i):
                q, kv, p, r, nk = item(i)
                pe.wait_ge(pT_ok, i + 1)
                for kb in range(nk // P):
                    mm = pe.matmul(ps[r:r + HD, 6, :], vT[:, kb, kv * HD:(kv + 1) * HD], pT[:, kb, :],
                                   start=kb == 0, stop=kb == nk // P - 1)
                mm.then_inc(pv_done, 1)

            def by_bc(flat):
                return flat.rearrange("p (r c b) -> p r c b", r=2, c=8)

            def dec_scores():
                pe.wait_ge(exp_done, 8)
                pe.wait_ge(kcT_ok, 1)
                pe.wait_ge(qd_ok, 1)
                for p in range(2):
                    for b in range(NB):
                        mm = pe.matmul(by_bc(ps[:, 4, 0:P])[:, :, 4 * p:4 * p + 4, b], kcT[:, 2 * b + p, :], qd[:, p, b, :, :],
                                       start=True, stop=True)
                mm.then_inc(sS_done, 1)

            def dec_rows():
                pe.wait_ge(sT_ok, 1)
                pe.wait_ge(prod_ok, 1)
                pe.transpose(ps[:, 5, 0:P], sT[:, :], ident)
                for r in (0, HD):
                    mm = pe.matmul(ps[r:r + HD, 5, P:P + 1], prod[r:r + HD, :], ones[r:r + HD, 0:1], start=True, stop=True)
                mm.then_inc(sR_done, 1)

            def dec_probs_T():
                pe.wait_ge(pS_ok, 1)
                pe.wait_ge(o_done, 8)
                pe.transpose(ps[:, 6, 0:P], pS[:, 0:P], ident)
                pe.matmul(ps[:, 6, P:P + HD], blk, dg[:, :], start=True, stop=True).then_inc(pTS_ps, 1)

            def dec_attend():
                pe.wait_ge(pTS_ok, 1)
                pe.wait_ge(d_even, 16 * 2)
                for p in range(2):
                    for b in range(NB):
                        c = (p * NB + b) * 8
                        mm = pe.matmul(ps[:, 7, c:c + 8].rearrange("p (r c) -> p r c", r=2), vc[:, b, p * P:(p + 1) * P],
                                       by_bc(pTS[:, 0:P])[:, :, 4 * p:4 * p + 4, b], start=True, stop=True)
                mm.then_inc(pvS, 1)

            def conv_T(h, b0, b1):
                pe.wait_ge(conv_u, h + 1)
                for t in range(4):
                    cs = slice(t * P, (t + 1) * P)
                    pe.matmul(ps[0:2, b0, cs], conv_in[:, t, TP:TP + 2], ident, start=True, stop=True)
                    mm = pe.matmul(ps[0:NB, b1, cs], conv_in[:, t, 274:282], ident, start=True, stop=True)
                mm.then_inc(ct_ps, 1)

            for u in range(EVEN_GROUPS * IN_UNITS):
                g, j = divmod(u, IN_UNITS)
                if g == 0:
                    pe.wait_ge(xl_done, j // 2 + 1)
                unit(U_EVEN + u, xh, xl, 2 * j, 0, j == 0, j == IN_UNITS - 1, single=True,
                     taken=(3 * g - 2, G_EVEN + g) if g and j == 0 else None)
                if u == 0:
                    input_T(2)
                if u == 2:
                    input_T(3)
                if u == 5:
                    pe.wait_ge(evac_g, 4)
                    norm_sum(0)
                if u == 14:
                    cache_T()
                if u == 15:
                    conv_state_T()
                for q, (c0, n) in enumerate(((0, 4), (4, 4), (8, 2))):
                    if u == IN_UNITS * q + 8:
                        qk_sum(q, n)
                    if u == IN_UNITS * q + 13:
                        qk_rot(q, c0, n)
                if u == 30:
                    kv_T()
                i, at = divmod(u - ATT, 4)
                if at == 0 and 1 <= i <= 8:
                    attend(i - 1)
                if at == 0 and 0 <= i < 8:
                    scores(i)
                if at == 3 and 0 <= i < 8:
                    probs_T(i)
                if u == 41:
                    conv_T(0, 5, 7)
                if u == 64:
                    dec_scores()
                if u == 65:
                    dec_rows()
                if u == 67:
                    dec_probs_T()
                if u == 68:
                    dec_attend()
                if u == 70:
                    pe.wait_ge(eS_done, 1)
                    conv_T(1, 4, 5)

            def out_proj(U, G, order, tiles, even):
                with pe.Fori(0, 2, 1) as i:
                    for h in range(2):
                        for j in range(IN_UNITS):
                            if j == 0:
                                pe.wait_ge(evac_g, at_turn(pe, i, 2, G - 1) if h == 0 else at_turn(pe, i, 2, G))
                            if h == 1 and j == 0:
                                if even:
                                    pe.wait_ge(ct_ok, 2)
                                else:
                                    pe.wait_ge(ostd, 1)
                            if even and h == 0 and j in (0, 2):
                                pe.wait_ge(conv_l, 1 + j // 2)
                            if even and h == 0 and j == 3:
                                pe.wait_ge(o_done, 9)
                            if not even and h == 0 and j in (0, 2):
                                pe.wait_ge(pml, 4 + 2 * j)
                            if not even and h == 0 and j in (4, 6):
                                pe.wait_ge(ocl, j // 2 - 1)
                            taken = None
                            if h == 0 and j == 0:
                                taken = (tiles - 2, at_turn(pe, i, 1, G))
                            unit(U + IN_UNITS * h + j, yh, yl, 2 * order[j], 4 * h, j == 0, j == IN_UNITS - 1,
                                 i=i, step=2 * IN_UNITS, taken=taken)

            def ffn(layer, U, G, m):
                def gate_up(i, peeled):
                    for h in range(2):
                        for j in range(IN_UNITS):
                            if j == 0:
                                pe.wait_ge(evac_g, at_turn(pe, i, 2, G - 1 + h))
                            if peeled and h == 0:
                                pe.wait_ge(xl_done, 4 * m + j // 2 + 1)
                            if peeled and h == 1 and j == 0:
                                pe.wait_ge(rstd_done, m + 1)
                            unit(U + IN_UNITS * h + j, xh, xl, 2 * j, 4 * h, j == 0, j == IN_UNITS - 1,
                                 i=i, step=2 * IN_UNITS)
                            if peeled and h == 0 and j == 5:
                                pe.wait_ge(evac_g, G)
                                norm_sum(m)

                gate_up(None, True)
                with pe.Fori(1, GU_ITERS, 1) as i:
                    gate_up(i, False)
                U2, G2 = U + 2 * IN_UNITS * GU_ITERS, G + 2 * GU_ITERS
                hid = GU_ITERS * (layer + 1)
                with pe.Fori(0, 2, 1) as i:
                    for h in range(2):
                        for j in range(DN_UNITS):
                            if j == 0:
                                pe.wait_ge(evac_g, at_turn(pe, i, 2, G2 - 1 + h))
                            if h == 0 and j == 0:
                                pe.wait_ge(hid_done, hid - 1)
                            if h == 0 and j == 20:
                                pe.wait_ge(hid_done, hid)
                            if layer == 1 and j == 0:
                                pe.wait_ge(y_ok, at_turn(pe, i, 2, 2))
                            unit(U2 + DN_UNITS * h + j, hh, hl, 2 * j, 4 * h, j == 0, j == DN_UNITS - 1,
                                 i=i, step=2 * DN_UNITS)
                            if layer == 1 and (h, j) in ((1, 2), (1, DN_UNITS - 1)):
                                k = 0 if j == 2 else 1
                                stage = (gbuf, ubuf)[k]
                                pe.wait_ge(evac_g, at_turn(pe, i, 2, G2 + k + 1))
                                for t in range(4):
                                    cs = slice(t * P, (t + 1) * P)
                                    for q in range(2):
                                        pe.transpose(ps[:, 4 * k + q, cs], stage[:, t, q * P:(q + 1) * P], ident)
                                    mm = pe.matmul(ps[0:NB, 4 * k + 2, cs], stage[:, t, TP:T], ident, start=True, stop=True)
                                mm.then_inc(y_ps, 1)

            out_proj(U_OUT_E, G_OUT_E, OUT_E_ORDER, 3 * EVEN_GROUPS, True)
            ffn(0, U_FFN0, G_FFN0, 1)

            def gate_rank():
                pe.wait_ge(evac_g, G_ODD + 2)
                pe.wait_ge(d_odd, 16)
                for h in range(GH):
                    mm = pe.matmul(ps[:, 4 + h, 0:T], wup[:, h * P:(h + 1) * P], zr[:, :], start=True, stop=True)
                mm.then_inc(gk_ps, 1)

            def att():
                pe.wait_ge(kd_ok, 1)
                pe.wait_ge(zb_ok, 1)
                for h in range(GH):
                    for n in range(NCH):
                        r = CH * (n % 2)
                        q = 2 * h + n // 2
                        mm = pe.matmul(ps[r:r + CH, 4, q * CH:(q + 1) * CH], sq4[:, h, n * CH:(n + 1) * CH],
                                       qg[:, h, n * CH:(n + 1) * CH], start=True, stop=True)
                mm.then_inc(att_ps, 1)

            def k2_T():
                pe.wait_ge(k2_ok, 1)
                for h in range(GH):
                    cs = slice(h * P, (h + 1) * P)
                    for q in range(2):
                        pe.transpose(ps[:, 5 + q, cs], ubuf[:, h, q * P:(q + 1) * P], ident)
                    mm = pe.matmul(ps[0:NB, 7, cs], kg[:, h, TP:T], ident, start=True, stop=True)
                mm.then_inc(k2t_ps, 1)

            def v_T(half):
                pe.wait_ge(evac_g, G_ODD + 4 + half)
                pe.wait_ge(k2t_ok, 1)
                if half:
                    pe.wait_ge(st_ok, 2)
                    pe.wait_ge(go_ok, 2)
                pe.wait_ge(lo3_ok, 1)
                for t in range(4):
                    cs = slice(t * P, (t + 1) * P)
                    for q in range(2):
                        pe.transpose(ps[:, 5 + q, cs], vf[:, t, q * P:(q + 1) * P], ident)
                    mm = pe.matmul(ps[0:NB, 7, cs], vf[:, t, TP:T], ident, start=True, stop=True)
                mm.then_inc(vt_ps, 1)

            def gla_delta(h):
                pe.wait_ge(vt_ok, h // 2 + 1)
                if h:
                    pe.wait_ge(st_ok, h)
                for n in range(NCH):
                    r, q = CH * (n % 2), n // 2
                    mm = pe.matmul(ps[:, 5 + n % 2, q * GDV:(q + 1) * GDV], k2t[r:r + CH, q, h * P:(h + 1) * P],
                                   vtok[r:r + CH, q, h * GDV:(h + 1) * GDV], start=True, stop=True)
                mm.then_inc(dl_ps, 1)

            def gla_out(h):
                pe.wait_ge(st_ok, h + 1)
                pe.wait_ge(att_ok, 1)
                if h:
                    pe.wait_ge(go_ok, h)
                if h % 2 == 0:
                    pe.wait_ge(lo3_ok, h // 2 + 2)
                for e in range(2):
                    for n in range(NCH):
                        r, q = CH * (n % 2), n // 2
                        out = ps[:, 4 if n % 2 == 0 else 7, e * P + q * CH:e * P + (q + 1) * CH]
                        c0 = h * GDV + e * P
                        mm = pe.matmul(out, vtok[r:r + CH, q, c0:c0 + P], attS[r:r + CH, 2 * h + q, :],
                                       start=True, stop=n == 0)
                        if n:
                            mm = pe.matmul(out, st[:, h % 2, n - 1, e * P:(e + 1) * P], qg[:, h, n * CH:(n + 1) * CH],
                                           start=False, stop=True)
                mm.then_inc(go_ps, 1)

            def dec_outer(q):
                b, hp = divmod(q, 2)
                pe.wait_ge(kdg, b + 1)
                pe.wait_ge(vt_ok, 2)
                pe.wait_ge(st_ok, 4)
                if q >= 2:
                    pe.wait_ge(sg_ok, q - 1)
                if q == 0:
                    pe.wait_ge(lo3_ok, 3)
                for k in range(2):
                    h = 2 * hp + k
                    mm = pe.matmul(ps[:, 5 + q % 2, k * GDV:(k + 1) * GDV], kdiag[:, b % 2, h * P:(h + 1) * P],
                                   v3[:, h * GDV:(h + 1) * GDV], start=True, stop=True)
                mm.then_inc(kv_o, 1)

            def dec_out(q):
                b, hp = divmod(q, 2)
                pe.wait_ge(sg_ok, q + 1)
                if q == 0:
                    pe.wait_ge(go_ok, 4)
                for k in range(2):
                    for e in range(2):
                        h = 2 * hp + k
                        c = (2 * h + e) * NB + b
                        mm = pe.matmul(ps[:, 7, c:c + 1], sgl[:, q % 4, k, e * P:(e + 1) * P], qsamp[:, h, b:b + 1],
                                       start=True, stop=True)
                mm.then_inc(so_ps, 1)

            def pool_state_T(half):
                pe.wait_ge(d_prow, 16)
                pe.wait_ge(go_ok, 4)
                if half:
                    pe.wait_ge(pml, 4)
                for t in range(4):
                    c = 4 * half + t
                    mm = pe.transpose(ps[:, 4, t * 120:(t + 1) * 120], prow[:, c * P:(c + 1) * P], ident[0:120, 0:120])
                mm.then_inc(pst_ps, 1)

            def pool_T(half, part):
                pe.wait_ge(evac_g, G_ODD + 6 + half)
                pe.wait_ge(pst_ok, half + 1)
                if half + part:
                    pe.wait_ge(po_ok, 2 * half + part)
                for t in range(4):
                    cs = slice(t * P, (t + 1) * P)
                    if part == 0:
                        mm = pe.matmul(ps[0:PB, 4, cs], ext[:, t, TP:TP + PB], ident, start=True, stop=True)
                    else:
                        mm = pe.matmul(ps[0:NB, 4, cs], ext[:, t, 286:399:16], ident, start=True, stop=True)
                mm.then_inc(po_ps, 1)

            def pool_mix(c):
                g, m = divmod(c, 2)
                pe.wait_ge(dmix_ok, g + 1)
                pe.wait_ge(d_wp, 16)
                pe.wait_ge(po_ok, 2 * (g // 2) + 2)
                if c:
                    pe.wait_ge(pml, c)
                for k in range(2):
                    mm = pe.matmul(ps[:, 4, 0:T], wpool[:, 2 * g + k, m * P:(m + 1) * P], dmix[:, k, :],
                                   start=k == 0, stop=k == 1)
                mm.then_inc(pm_ps, 1)

            def out_sum():
                pe.wait_ge(osq, 1)
                pe.wait_ge(pml, 8)
                pe.wait_ge(sg_ok, 16)
                for h in range(GH):
                    for e in range(2):
                        q = 2 * (h % 2) + e
                        mm = pe.matmul(ps[:, 4 + h, 0:T], ones[:, :], (sq4 if h < 2 else acc4)[:, q, :], start=e == 0, stop=e == 1)
                mm.then_inc(oss, 1)

            tiles_before = 3 * EVEN_GROUPS
            for q, (col, s0) in enumerate(zip(ODD_COLS, ODD_FIRST)):
                G = G_ODD + q
                units = IN_UNITS if col is not None else 2
                for j in range(units):
                    s = s0 + j
                    n = U_ODD + s
                    if col is None:
                        pe.wait_ge(lo_done, n + 1)
                        if j == 0:
                            pe.wait_ge(evac_t, tiles_before - 2)
                        for k in range(8):
                            for m, (w, r) in enumerate(((whi, xh), (whi, xl), (wlo, xh))):
                                mm = pe.matmul(ps[:, 0, 0:T], w[:, n % RING, k * P:(k + 1) * P], r[:, 8 * j + k, :],
                                               start=j == k == m == 0, stop=j == 1 and k == 7 and m == 2)
                        mm.then_inc(units_done, 1)
                    else:
                        if q == 0:
                            pe.wait_ge(xl_done, 8 + j // 2 + 1)
                        if q == 0 and j == 0:
                            pe.wait_ge(evac_g, G - 1)
                        if q == 2 and j == 0:
                            pe.wait_ge(evac_g, G)
                        unit(n, xh, xl, 2 * j, 0, j == 0, j == IN_UNITS - 1, single=True,
                             taken=(tiles_before - 2, G) if q > 2 and j == 0 else None)
                    if s == 5:
                        pe.wait_ge(evac_g, G_ODD)
                        norm_sum(2)
                    if s == 10:
                        pe.wait_ge(std_done, 3)
                        gate_rank()
                    if s == 20:
                        att()
                    if s == 21:
                        k2_T()
                    if s == 27:
                        v_T(0)
                    if s == 35:
                        v_T(1)
                    for k, h in ((28, 0), (30, 1), (36, 2), (38, 3)):
                        if s == k:
                            gla_delta(h)
                        if s == k + 1:
                            gla_out(h)
                    if 0 <= s - 40 < 16:
                        dec_outer(s - 40)
                    if 0 <= s - 41 < 16:
                        dec_out(s - 41)
                    if s == 58:
                        out_sum()
                    for half in range(2):
                        if s == 40 + 8 * half:
                            pool_state_T(half)
                        if s == 42 + 8 * half:
                            pool_T(half, 0)
                        if s == 43 + 8 * half:
                            pool_T(half, 1)
                        if 44 + 8 * half <= s < 48 + 8 * half:
                            pool_mix(4 * half + s - 44 - 8 * half)
                if col is not None:
                    tiles_before += 3

            out_proj(U_OUT_O, G_OUT_O, OUT_O_ORDER, tiles_before, False)
            ffn(1, U_FFN1, G_FFN1, 3)

        @block.scalar
        def _(act):
            steps = [0]

            def own(ins):
                steps[0] += 1
                ins.then_inc(ac, 1)
                act.wait_ge(ac, steps[0])

            act.dma_start(cst[:, C_ID:C_ID + P], a["consts"][:, C_ID:C_ID + P]).then_inc(d_id, 16)
            act.dma_start(xtok_s[:, :], a["x_sample"].rearrange("b s d -> (b s) d")).then_inc(d_xs, 16)
            act.dma_start(vec[:, :], a["vectors"]).then_inc(d_vec, 16)
            act.dma_start(cst[:, P:C_ALL], a["consts"][:, P:C_ALL]).then_inc(d_cst, 16)

            def norm_prep(m, g, G, base, i=None):
                taken = at_turn(act, i, 2, G + 1)
                added = 3 * m + max(g - 1, 0) if i is None else at_turn(act, i, 1 + g, 3 * m)
                c0 = 4 * g
                act.wait_ge(evac_g, taken)
                if i is not None or g > 1:
                    act.wait_ge(acc_done, added)
                c = c0 if i is None else act.snap(i * 8 + c0)
                for t in range(4):
                    ins = act.activation(xh[:, c0 + t, :] if i is None else xh[:, bass.ds(c + t, 1), :],
                                         x[:, c0 + t, :] if i is None else x[:, bass.ds(c + t, 1), :], ACT.Copy,
                                         scale=vec[:, base + c0 + t:base + c0 + t + 1] if i is None
                                         else vec[:, bass.ds(c + base + t, 1)])
                ins.then_inc(xh_done, 1)
                slot = slice(min(g, 1), min(g, 1) + 1) if i is None or g else bass.ds(i, 1)
                act.activation(sqs[:, slot, :, :].rearrange("p o c t -> p (o c t)"),
                               (x[:, c0:c0 + 4, :] if i is None else x[:, bass.ds(c, 4), :]).rearrange("p c t -> p (c t)"),
                               ACT.Square).then_inc(sq_done, 1)

            def inverse_root(r, v, sums, count):
                own(act.activation(r, sums, ACT.Ln, scale=1.0 / count, bias=eps[:, :]))
                act.activation(r, r, ACT.Exp, scale=-0.5)
                return act.activation(v, sums, ACT.Identity, scale=1.0 / count, bias=eps[:, :])

            def root(m):
                act.wait_ge(ss_done, m + 1)
                inverse_root(seed[:, :], acc4[:, 0, :], ps[:, 4, 0:T], D).then_inc(std_done, 1)

            split_hi(act, 0)
            act.wait_ge(d_vec, 16)
            norm_prep(0, 0, 0, V_MIX)
            split_hi(act, 1)
            norm_prep(0, 1, 1, V_MIX)
            split_hi(act, 2)
            act.dma_start(kc[:, :, :], a["cache_swa_k"][0].rearrange("b k h d -> k b (h d)")).then_inc(d_kc, 16)
            act.dma_start(vc[:, :, :], a["cache_swa_v"][0].rearrange("b k h d -> k b (h d)")).then_inc(d_even, 16)
            act.dma_start(cst_rows[:, :], a["state_conv"][0].rearrange("b j d -> (b j) d")).then_inc(d_even, 16)

            def item(i):
                q, kv = divmod(i, NKV)
                return q, kv, kv // 2, HD * (kv % 2), P * (q + 1)

            def exps(i):
                q, kv, p, r, nk = item(i)
                b = 24 * (i % 2)
                act.wait_ge(negm_done, i + 1)
                if i >= 2:
                    act.wait_ge(pt_done, i - 1)
                act.wait_ge(kcT_ps, 1)
                for g in range(GRP):
                    act.activation(prob[:, i % 2, g, 0:nk], psf[:, 4 * 512 + g * nk:4 * 512 + (g + 1) * nk], ACT.Exp,
                                   scale=HD ** -0.5, bias=small[:, b + 4 + g:b + 5 + g],
                                   accum_out=small[:, b + 12 + g:b + 13 + g])
                act.activation(small[:, b + 16:b + 20], small[:, b + 8:b + 12], ACT.Exp).then_inc(exp_done, 1)

            def take_pT(i):
                nkb = item(i)[4] // P
                act.wait_ge(pt_done, i + 1)
                if i:
                    act.wait_ge(pv_done, i)
                act.activation(pT[:, 0:nkb, :], ps[:, 6:6 + nkb, :], ACT.Copy).then_inc(pT_ok, 1)

            def out_hi(i):
                q, kv, p, r, nk = item(i)
                act.wait_ge(pv_done, i + 1)
                act.activation(yh[r:r + HD, 4 * p:4 * p + 4, q * P:(q + 1) * P],
                               ps[r:r + HD, 6, :].rearrange("p (g t) -> p g t", g=4), ACT.Copy).then_inc(oh_done, 1)

            def conv_rows(h):
                b0, b1 = ((5, 7), (4, 5))[h]
                act.wait_ge(ct_ps, h + 1)
                if h:
                    act.wait_ge(d_ct, 32)
                act.activation(conv_tok[0:2, 0, :], ps[0:2, b0, :], ACT.Copy)
                act.activation(conv_tok[:, 1, :], ps[0:NB, b1, :], ACT.Copy).then_inc(ct_ok, 1)
                act.wait_ge(ct_ok, h + 1)
                cs = slice(h * COLS, (h + 1) * COLS)
                act.dma_start(o_cp[0, 0, :, cs], conv_tok[0:2, 0, :]).then_inc(d_ct, 16)
                act.dma_start(o_cs[0, :, 1, cs], conv_tok[:, 1, :]).then_inc(d_ct, 16)

            for u in range(EVEN_GROUPS * IN_UNITS):
                n = U_EVEN + u + AHEAD
                split_hi(act, n)
                if u == 0:
                    norm_prep(0, 2, 2, V_MIX)
                    act.wait_ge(ms_done, 2)
                    act.wait_ge(d_cst, 16)
                    act.activation(maskb[:, :], cst[:, C_MASK:C_MASK + 2 * P], ACT.Copy).then_inc(maskb_ok, 1)
                    act.activation(identb[:, :], ident, ACT.Copy).then_inc(maskb_ok, 1)
                if u == 2:
                    norm_prep(0, 3, 3, V_MIX)
                if u == 14:
                    act.wait_ge(kcT_ps, 1)
                    act.activation(kcT[:, :, :].rearrange("p q k -> p (q k)"), psf[:, 4 * 512:8 * 512], ACT.Copy).then_inc(kcT_ok, 1)
                if u == 15:
                    act.wait_ge(cst_ps, 1)
                    act.activation(conv_st[:, :, :].rearrange("p c r -> p (c r)"), ps[:, 4, 0:P], ACT.Copy).then_inc(cst_ok, 1)
                if u == 5:
                    root(0)
                if u == 8:
                    act.dma_start(sink_row[:, :], a["attn_sinks"].broadcast_to([P, NH])).then_inc(d_sink, 16)
                if u in (10, 11, 12, 13):
                    r, p = divmod(u - 10, 2)
                    src = a["attn_sinks"][0, 8 * p + 4 * r:8 * p + 4 * r + 4].unsqueeze(1).unsqueeze(2)
                    at = HD * r + 32 * p
                    act.dma_start(sink_col[at:at + 32, :], src.broadcast_to([4, NB, 1])).then_inc(d_sink, 16)
                if u == 18:
                    act.dma_start(o_ks[0, :, 0:P - 1], a["cache_swa_k"][0, :, 1:P]).then_inc(d_out, 16)
                if u == 20:
                    act.dma_start(o_vs[0, :, 0:P - 1], a["cache_swa_v"][0, :, 1:P]).then_inc(d_out, 16)
                if u == 21:
                    act.dma_start(o_cs[0, :, 0, :], a["state_conv"][0, :, 1, :]).then_inc(d_out, 16)
                if u == 22:
                    act.dma_start(o_ps[0, :, 0:PB - 1, :], a["state_pool"][0, :, 1:PB, :]).then_inc(d_out, 16)
                for q, (c0, nq) in enumerate(((0, 4), (4, 4), (8, 2))):
                    if u == IN_UNITS * q + 7:
                        act.wait_ge(evac_g, G_EVEN + q + 1)
                        if q:
                            act.wait_ge(qnorm, q)
                        act.activation(sq4[:, 0:nq, :], qk[:, c0:c0 + nq, :], ACT.Square).then_inc(qsq, 1)
                    if u == IN_UNITS * q + 9:
                        act.wait_ge(qss, q + 1)
                        inverse_root(ubuf[:, 0:nq, :], sq4[:, 0:nq, :], ps[:, 4:4 + nq, 0:T], HD).then_inc(qstd, 1)
                if u == 30:
                    act.wait_ge(kv_ps, 1)
                    act.activation(vT[:, 0, :], ps[:, 4, 256:512], ACT.Copy)
                    act.activation(vT[:, 1, :], ps[:, 5, 0:256], ACT.Copy)
                    act.activation(kT1[:, :], ps[:, 4, 0:256], ACT.Copy)
                    act.activation(kvS[:, :], ps[0:NB, 6, :], ACT.Copy).then_inc(kv_tok, 1)
                if u == 33:
                    act.wait_ge(kv_tok, 1)
                    act.dma_start(o_kp[0, 0].rearrange("k h d -> k (h d)"), kT1[:, :]).then_inc(d_out, 16)
                    act.dma_start(o_vp[0, 0].rearrange("k h d -> k (h d)"), vT[:, 1, :]).then_inc(d_out, 16)
                    act.dma_start(o_ks[0, :, P - 1].rearrange("b h d -> b (h d)"), kvS[:, 0:256]).then_inc(d_out, 16)
                    act.dma_start(o_vs[0, :, P - 1].rearrange("b h d -> b (h d)"), kvS[:, 256:512]).then_inc(d_out, 16)
                for h in range(2):
                    if u == (48, 71)[h]:
                        act.wait_ge(conv_y, h + 1)
                        act.activation(yh[:, 8 + 4 * h:12 + 4 * h, :], gbuf[:, :, :], ACT.Copy).then_inc(conv_h, 1)
                i, at = divmod(u - ATT, 4)
                if at == 0 and 1 <= i <= 8:
                    out_hi(i - 1)
                if at == 0 and 0 <= i < 8:
                    exps(i)
                if at == 3 and 0 <= i < 8:
                    take_pT(i)
                if u == 41:
                    conv_rows(0)
                if u == 64:
                    act.wait_ge(sS_done, 1)
                    act.activation(sT[:, :], ps[:, 4, 0:P], ACT.Copy).then_inc(sT_ok, 1)
                if u == 65:
                    act.wait_ge(nS_done, 1)
                    act.activation(pS[:, 0:P + 1], ps[:, 5, 0:P + 1], ACT.Exp, scale=HD ** -0.5,
                                   bias=small[:, 49:50], accum_out=small[:, 51:52])
                    act.activation(small[:, 52:53], small[:, 50:51], ACT.Exp).then_inc(eS_done, 1)
                if u == 67:
                    act.wait_ge(pTS_ps, 1)
                    act.activation(pTS[:, :], ps[:, 6, 0:192], ACT.Copy).then_inc(pTS_ok, 1)
                if u == 69:
                    act.wait_ge(oS_ok, 1)
                    act.activation(yh[:, 0:8, TP:T], prod[:, :].rearrange("p (c b) -> p c b", c=8), ACT.Copy).then_inc(oh_done, 1)
                if u == 70:
                    conv_rows(1)

            def out_proj(U, G, m, base, split_rows):
                with act.Fori(0, 2, 1) as i:
                    for h in range(2):
                        for j in range(IN_UNITS):
                            n = U + IN_UNITS * h + j + AHEAD
                            up = (16 * (h + 1), 32) if split_rows and (j + AHEAD) in ATTN_UNITS else None
                            split_hi(act, n, i=i, step=2 * IN_UNITS, up=up)
                        norm_prep(m, h, G + h, base, i=i)

            def ffn(layer, U, G, m):
                def gate_up(i, peeled):
                    for k in range(2 * IN_UNITS):
                        split_hi(act, U + k + AHEAD, i=i, step=2 * IN_UNITS)
                        if peeled and k == 5:
                            root(m)
                        if k == IN_UNITS - 1:
                            act.wait_ge(evac_g, at_turn(act, i, 2, G + 1))
                            act.activation(gbuf[:, :, :], gbuf[:, :, :], ACT.Silu).then_inc(silu_done, 1)
                    act.wait_ge(h_ready, at_turn(act, i, 1, 11 * layer + 1))
                    dst = hh[:, 0:4, :] if i is None else hh[:, bass.ds(act.snap(i * 4), 4), :]
                    act.activation(dst, ubuf[:, :, :], ACT.Copy).then_inc(hh_done, 1)

                gate_up(None, True)
                with act.Fori(1, GU_ITERS, 1) as i:
                    gate_up(i, False)
                U2, G2 = U + 2 * IN_UNITS * GU_ITERS, G + 2 * GU_ITERS
                if layer == 0:
                    with act.Fori(0, 2, 1) as i:
                        for h in range(2):
                            for j in range(DN_UNITS):
                                split_hi(act, U2 + DN_UNITS * h + j + AHEAD, i=i, step=2 * DN_UNITS)
                            norm_prep(2, h, G2 + h, V_MIX + KC, i=i)
                    return

                def rows_out(i, k):
                    col = at_turn(act, i, 2 * COLS, COLS * k)
                    act.wait_ge(y_ps, 2 * i + k + 1)
                    if i or k:
                        act.wait_ge(d_y, 64 * i + 32 * k)
                    act.activation(sq4[:, :, :].rearrange("p a t -> p (a t)")[:, 0:2 * COLS], psf[:, 2048 * k:2048 * k + 2 * COLS], ACT.Copy)
                    act.activation(acc4[0:NB, :, :].rearrange("p a t -> p (a t)")[:, 0:COLS], ps[0:NB, 4 * k + 2, :], ACT.Copy).then_inc(y_ok, 1)
                    act.wait_ge(y_ok, 2 * i + k + 3)
                    act.dma_start(y_prompt[0].rearrange("(q p) d -> p q d", q=2)[:, :, bass.ds(col, COLS)],
                                  sq4[:, :, :].rearrange("p a t -> p (a t)")[:, 0:2 * COLS].rearrange("p (q d) -> p q d", q=2)
                                  ).then_inc(d_y, 16)
                    act.dma_start(y_sample.rearrange("b s d -> (b s) d")[:, bass.ds(col, COLS)],
                                  acc4[0:NB, :, :].rearrange("p a t -> p (a t)")[:, 0:COLS]).then_inc(d_y, 16)

                for i in range(2):
                    for k in range(2 * DN_UNITS):
                        split_hi(act, U2 + k + AHEAD, i=i, step=2 * DN_UNITS)
                        if k == DN_UNITS + 2:
                            rows_out(i, 0)
                    rows_out(i, 1)

            out_proj(U_OUT_E, G_OUT_E, 1, V_FFN, True)
            act.wait_ge(d_out, 16 * 8)
            act.wait_ge(d_ct, 64)
            ffn(0, U_FFN0, G_FFN0, 1)

            act.wait_ge(evac_g, G_ODD)
            act.wait_ge(units_done, U_ODD)
            act.wait_ge(d_ct, 64)
            act.dma_start(prow[:, :], a["state_pool"][0].rearrange("b j d -> (b j) d")).then_inc(d_prow, 16)
            act.dma_start(wup[:, :], a["w_alpha_up"][0]).then_inc(d_odd, 16)
            gla_in = a["state_gla"][0].rearrange("b h k v -> k b h v")
            gla_o = o_gs[0].rearrange("b h k v -> k b h v")

            def dec_load(q):
                b, hp = divmod(q, 2)
                if q >= 4:
                    act.wait_ge(d_gso[q % 4], 16 * (q // 4))
                    act.wait_ge(so_ps, q - 3)
                act.dma_start(sgl[:, q % 4, :, :], gla_in[:, b, 2 * hp:2 * hp + 2, :]).then_inc(d_gs[q % 4], 16)

            for q in range(4):
                dec_load(q)

            def key_rows(b):
                if b == 0:
                    act.wait_ge(lo3_ok, 1)
                if b >= 2:
                    act.wait_ge(kv_o, 2 * b - 2)
                act.activation(kdiag[:, b % 2, :], k3[:, :].bitcast(F32), ACT.Copy, scale=cst[0:K3, C_ROW + b:C_ROW + b + 1]
                               ).then_inc(kdg, 1)

            def pool_rows(half, part):
                n = PB if part == 0 else NB
                act.wait_ge(po_ps, 2 * half + part + 1)
                if half:
                    act.wait_ge(d_pt[part], 16)
                act.activation(ptok[0:n, part, :], ps[0:n, 4, :], ACT.Copy).then_inc(po_ok, 1)
                act.wait_ge(po_ok, 2 * half + part + 1)
                cs = slice(half * COLS, (half + 1) * COLS)
                dst = o_pp[0, 0, :, cs] if part == 0 else o_ps[0, :, PB - 1, cs]
                act.dma_start(dst, ptok[0:n, part, :]).then_inc(d_pt[part], 16)

            for s in range(U_OUT_O - U_ODD):
                split_hi(act, U_ODD + s + AHEAD)
                if s == 5:
                    root(2)
                if s == 11:
                    act.wait_ge(zb_ok, 1)
                    own(act.activation(sq4[:, :, :], acc4[:, :, :], ACT.Abs))
                if s == 12:
                    own(act.activation(sq4[:, :, :], sq4[:, :, :], ACT.Exp, scale=-1.0))
                    act.activation(sq4[:, :, :], sq4[:, :, :], ACT.Ln, bias=ones[:, 0:1]).then_inc(ln_ok, 1)
                if s == 15:
                    act.wait_ge(b_ok, 1)
                    act.activation(acc4[:, :, :], gbuf[:, :, :], ACT.Exp, scale=1.0 / 16)
                    act.activation(sq4[:, :, :], gbuf[:, :, :], ACT.Exp, scale=-1.0 / 16).then_inc(eb_ok, 1)
                if s == 18:
                    act.wait_ge(df_ok, 1)
                    act.activation(ubuf[:, :, 0:TP], ubuf[:, :, 0:TP], ACT.Exp, scale=1.0 / 16).then_inc(edf_ok, 1)
                if s == 21:
                    act.wait_ge(k2t_ps, 1)
                    act.activation(k2t[:, :, :], ps[:, 5:7, :], ACT.Copy)
                    act.wait_ge(pad3_ok, 1)
                    for k in (0, 32):
                        ins = act.activation(k3[k:k + NB, :], ps[0:NB, 7, :], ACT.Copy)
                    ins.then_inc(k2t_ok, 1)
                for half in range(2):
                    if s == 27 + 8 * half:
                        act.wait_ge(vt_ps, half + 1)
                        cs = slice(half * COLS, (half + 1) * COLS)
                        act.activation(vtok[:, :, cs], ps[:, 5:7, :], ACT.Copy)
                        for k in (0, 64):
                            ins = act.activation(v3[k:k + NB, cs], ps[0:NB, 7, :], ACT.Copy)
                        ins.then_inc(vt_ok, 1)
                for k, h in ((29, 0), (31, 1), (37, 2), (39, 3)):
                    if s == k:
                        act.wait_ge(go_ps, h + 1)
                        to = oF[:, 2 * h:2 * h + 2, 0:TP].rearrange("p e (q r c) -> p e q r c", q=2, r=2)
                        for r, bank in ((0, 4), (1, 7)):
                            ins = act.activation(to[:, :, :, r, :], ps[:, bank, 0:TP].rearrange("p (e q c) -> p e q c", e=2, q=2), ACT.Copy)
                        ins.then_inc(go_ok, 1)
                        act.wait_ge(st_ok, h + 1)
                        act.dma_start(o_gp[0, 0, h], st[:, h % 2, 3, :]).then_inc(d_go[h % 2], 16)
                if s == 40:
                    act.wait_ge(d_go[0], 32)
                    act.wait_ge(d_go[1], 32)
                    act.wait_ge(go_ps, 4)
                    act.dma_start(wpool[:, :, :], a["w_pool"][0].rearrange("g (k p) n -> p (g k) n", p=P)).then_inc(d_wp, 16)
                if s >= 38 and s % 2 == 0 and (s - 38) // 2 < NB:
                    key_rows((s - 38) // 2)
                if 0 <= s - 41 < 16:
                    q = s - 41
                    act.wait_ge(sg_ok, q + 1)
                    act.dma_start(gla_o[:, q // 2, 2 * (q % 2):2 * (q % 2) + 2, :], sgl[:, q % 4, :, :]).then_inc(d_gso[q % 4], 16)
                if 0 <= s - 42 < 12:
                    dec_load(s - 42 + 4)
                for half in range(2):
                    if s == 40 + 8 * half:
                        act.wait_ge(pst_ps, half + 1)
                        act.wait_ge(pad_ok, 1)
                        if half:
                            act.wait_ge(dmix_ok, 2)
                            act.wait_ge(po_ps, 2)
                        act.activation(ext[:, :, 271:399].rearrange("p t (b j) -> p t b j", b=NB)[:, :, :, 0:PB],
                                       ps[:, 4, 0:480].rearrange("p (t b j) -> p t b j", t=4, b=NB), ACT.Copy).then_inc(pst_ok, 1)
                    if s == 42 + 8 * half:
                        pool_rows(half, 0)
                    if s == 43 + 8 * half:
                        pool_rows(half, 1)
                    if 44 + 8 * half <= s < 48 + 8 * half:
                        c = 4 * half + s - 44 - 8 * half
                        act.wait_ge(pm_ps, c + 1)
                        act.activation(yh[:, 8 + c, :], ps[:, 4, 0:T], ACT.Copy,
                                       scale=vec[:, V_PSC + c:V_PSC + c + 1]).then_inc(pmh, 1)
                    if s == 57 + 8 * half:
                        act.wait_ge(evac_g, G_ODD + 8 + half)
                        act.activation(gbuf[:, :, :], gbuf[:, :, :], ACT.Silu).then_inc(sg_silu, 1)
                    if s == (62, 65)[half]:
                        act.wait_ge(oc_ok, half + 1)
                        act.activation(yh[:, 4 * half:4 * half + 4, :], oF[:, 4 * half:4 * half + 4, :], ACT.Copy).then_inc(och, 1)
                if s == 56:
                    act.wait_ge(so_ps, 16)
                    own(act.activation(oF[:, :, TP:T], ps[:, 7, 0:64].rearrange("p (c b) -> p c b", c=8), ACT.Copy))
                if s == 57:
                    act.wait_ge(kd_ok, 1)
                    act.activation(sq4, oF[:, 0:4, :], ACT.Square)
                    act.activation(acc4, oF[:, 4:8, :], ACT.Square).then_inc(osq, 1)
                if s == 58:
                    act.wait_ge(oss, 1)
                    inverse_root(vf[:, :, :], ubuf[:, :, :], ps[:, 4:8, 0:T], GDV).then_inc(ostd, 1)

            out_proj(U_OUT_O, G_OUT_O, 3, V_FFN + KC, False)
            act.wait_ge(d_go[0], 32)
            act.wait_ge(d_go[1], 32)
            act.wait_ge(d_gso[0], 64)
            act.wait_ge(d_gso[1], 64)
            act.wait_ge(d_gso[2], 64)
            act.wait_ge(d_gso[3], 64)
            ffn(1, U_FFN1, G_FFN1, 3)
            act.wait_ge(d_out, 16 * 8)
            act.wait_ge(d_ct, 64)
            act.wait_ge(d_go[0], 32)
            act.wait_ge(d_go[1], 32)
            act.wait_ge(d_pt[0], 32)
            act.wait_ge(d_pt[1], 32)
            act.wait_ge(d_y, 128)
            act.wait_ge(d_gso[0], 64)
            act.wait_ge(d_gso[1], 64)
            act.wait_ge(d_gso[2], 64)
            act.wait_ge(d_gso[3], 64)

        @block.vector
        def _(dve):
            steps = [0]

            def own(ins):
                steps[0] += 1
                ins.then_inc(dv, 1)
                dve.wait_ge(dv, steps[0])

            def norm_rest(r, c0, base, i=None):
                dve.wait_ge(xh_done, at_turn(dve, i, 2, r + 1))
                c = c0 if i is None else dve.snap(i * 8 + c0)
                for t in range(4):
                    at = slice(c0 + t, c0 + t + 1) if i is None else bass.ds(c + t, 1)
                    g = vec[:, base + c0 + t:base + c0 + t + 1] if i is None else vec[:, bass.ds(c + base + t, 1)]
                    ins = dve.scalar_tensor_tensor(xl[:, at, :], x[:, at, :], g, xh[:, at, :].bitcast(F32), ALU.mult, ALU.subtract)
                ins.then_inc(xl_done, 1)

            def refine(r, v, scratch, out):
                own(dve.tensor_tensor(scratch, r, r, ALU.mult))
                own(dve.scalar_tensor_tensor(scratch, scratch, -0.5, v, ALU.mult, ALU.mult))
                return dve.scalar_tensor_tensor(out, scratch, 1.5, r, ALU.add, ALU.mult)

            def norm_factor(m):
                dve.wait_ge(std_done, m + 1)
                refine(seed[:, :], acc4[:, 0, :], acc4[:, 1, :], rstd[:, :]).then_inc(rstd_done, 1)
                dve.wait_ge(rstd_done, m + 1)

            def take(G, dst, scale, tiles=4, done=None):
                for t in range(tiles):
                    if t == 3:
                        dve.wait_ge(units_done, done)
                    else:
                        dve.wait_ge(tile_done, take.tiles + t + 1)
                    ins = dve.tensor_tensor(dst(t), ps[:, t, 0:T], scale, ALU.mult)
                    ins.then_inc(evac_g if t == tiles - 1 else evac_t, 1)
                if tiles == 4:
                    take.tiles += 3

            take.tiles = 0

            def take_input(g):
                dve.wait_ge(head_done, g + 1)
                dve.tensor_copy(x[:, 4 * g:4 * g + 4, :], ps[:, 4:8, 0:T]).then_inc(evac_g, 1)

            take_input(0)
            split_lo(dve, 0)
            norm_rest(0, 0, V_MIX)
            take_input(1)
            split_lo(dve, 1)
            norm_rest(1, 4, V_MIX)
            split_lo(dve, 2)

            def item(i):
                q, kv = divmod(i, NKV)
                return q, kv, kv // 2, HD * (kv % 2), P * (q + 1)

            def row_max(i):
                q, kv, p, r, nk = item(i)
                b = 24 * (i % 2)
                dve.wait_ge(sc_done, i + 1)
                own(dve.reduce_max(small[:, b:b + 4], psf[:, 4 * 512:4 * 512 + 4 * nk].rearrange("p (g k) -> p g k", g=4), AX))
                own(dve.scalar_tensor_tensor(small[:, b + 4:b + 8], small[:, b:b + 4], -HD ** -0.5,
                                             nsink_row[:, 4 * kv:4 * kv + 4], ALU.mult, ALU.min))
                dve.tensor_tensor(small[:, b + 8:b + 12], small[:, b + 4:b + 8], sink_row[:, 4 * kv:4 * kv + 4],
                                  ALU.add).then_inc(negm_done, 1)

            def normalise(i):
                nk = item(i)[4]
                b = 24 * (i % 2)
                dve.wait_ge(exp_done, i + 1)
                own(dve.tensor_tensor(small[:, b + 12:b + 16], small[:, b + 12:b + 16], small[:, b + 16:b + 20], ALU.add))
                own(dve.reciprocal(small[:, b + 20:b + 24], small[:, b + 12:b + 16]))
                dve.tensor_tensor(prob[:, i % 2, :, 0:nk], prob[:, i % 2, :, 0:nk],
                                  small[:, b + 20:b + 24].unsqueeze(2).broadcast_to([P, GRP, nk]), ALU.mult).then_inc(pn_done, 1)

            def out_lo(i):
                q, kv, p, r, nk = item(i)
                dve.wait_ge(oh_done, i + 1)
                at = (slice(r, r + HD), slice(4 * p, 4 * p + 4), slice(q * P, (q + 1) * P))
                dve.tensor_tensor(yl[at], ps[r:r + HD, 6, :].rearrange("p (g t) -> p g t", g=4), yh[at].bitcast(F32),
                                  ALU.subtract).then_inc(o_done, 1)

            def conv(h, j):
                for t in range(4):
                    w = vec[:, V_CONV + 8 * j + 4 * h + t:V_CONV + 8 * j + 4 * h + t + 1]
                    for dst, src in ((gbuf[:, t, 0:TP], conv_in[:, t, j:j + TP]),
                                     (gbuf[:, t, TP:T], conv_in[:, t, 258 + NB * j:266 + NB * j])):
                        if j == 0:
                            ins = dve.tensor_scalar(dst, src, w, None, ALU.mult)
                        else:
                            ins = dve.scalar_tensor_tensor(dst, src, w, dst, ALU.mult, ALU.add)
                own(ins)

            for u in range(EVEN_GROUPS * IN_UNITS):
                done = U_EVEN + u + 1
                g, j = divmod(u, IN_UNITS)
                if j < IN_UNITS - 1:
                    split_lo(dve, U_EVEN + u + AHEAD)
                if u == 5:
                    norm_factor(0)
                if u == 0:
                    take_input(2)
                    norm_rest(2, 8, V_MIX)
                if u == 2:
                    take_input(3)
                    norm_rest(3, 12, V_MIX)
                if u == 16:
                    dve.wait_ge(d_sink, 16 * 5)
                    dve.wait_ge(d_vec, 16)
                    dve.wait_ge(evac_g, 4)
                    dve.wait_ge(cst_ok, 1)
                    dve.tensor_scalar(nsink_row[:, :], sink_row[:, :], -1.0, None, ALU.mult)
                    dve.tensor_scalar(nsink_col[:, :], sink_col[:, :], -1.0, None, ALU.mult)
                    dve.tensor_tensor(dg[:, :], ident[:, 0:HD], ident[:, HD:P], ALU.add)
                    own(dve.memset(conv_in[:, :, 0:2], 0.0))
                    own(dve.memset(qd[:, :, :, :, :], 0.0))
                if j == IN_UNITS - 1:
                    if g < 3:
                        take(G_EVEN + g, lambda t: qk[:, 4 * g + t, :] if 4 * g + t < 10 else vF[:, t - 2, :], rstd[:, :], done=done)
                    else:
                        h, part = divmod(g - 3, 3)
                        if part == 0:
                            take(G_EVEN + g, lambda t: gbuf[:, t, :], rstd[:, :], done=done)
                        elif part == 1:
                            take(G_EVEN + g, lambda t: ubuf[:, t, :], rstd[:, :], done=done)
                            dve.wait_ge(evac_g, G_EVEN + g + 1)
                            if h:
                                dve.wait_ge(ct_ps, 1)
                            dve.tensor_tensor(conv_in[:, :, 2:258], ubuf[:, :, 0:TP], gbuf[:, :, 0:TP], ALU.mult)
                            dve.tensor_tensor(conv_in[:, :, 274:282], ubuf[:, :, TP:T], gbuf[:, :, TP:T], ALU.mult)
                            dve.tensor_copy(conv_in[:, :, 258:274].rearrange("p t (j b) -> p t j b", j=2),
                                            conv_st[:, 4 * h:4 * h + 4, :].rearrange("p t (b j) -> p t j b", j=2)).then_inc(conv_u, 1)
                            dve.wait_ge(conv_u, h + 1)
                        else:
                            take(G_EVEN + g, lambda t: ubuf[:, t, :], rstd[:, :], done=done)
                if j == IN_UNITS - 1:
                    split_lo(dve, U_EVEN + u + AHEAD)
                for h in range(2):
                    if u == (48, 71)[h]:
                        dve.wait_ge(evac_g, G_EVEN + 6 + 3 * h)
                        dve.tensor_tensor(gbuf[:, :, :], ubuf[:, :, :], gbuf[:, :, :], ALU.mult).then_inc(conv_y, 1)
                    if u == (50, 71)[h]:
                        dve.wait_ge(conv_h, h + 1)
                        dve.tensor_tensor(yl[:, 8 + 4 * h:12 + 4 * h, :], gbuf[:, :, :],
                                          yh[:, 8 + 4 * h:12 + 4 * h, :].bitcast(F32), ALU.subtract).then_inc(conv_l, 1)
                for h, first in enumerate((40, 64)):
                    if 0 <= u - first < 3:
                        conv(h, u - first)
                for q, (c0, n) in enumerate(((0, 4), (4, 4), (8, 2))):
                    cs = slice(c0, c0 + n)
                    gain = vec[:, V_Q:V_Q + 1] if q < 2 else vec[:, V_K:V_K + 1]
                    if u == IN_UNITS * q + 10:
                        dve.wait_ge(qstd, q + 1)
                        own(refine(ubuf[:, 0:n, :], sq4[:, 0:n, :], gbuf[:, 0:n, :], ubuf[:, 0:n, :]))
                        dve.scalar_tensor_tensor(qk[:, cs, :], qk[:, cs, :], gain, ubuf[:, 0:n, :], ALU.mult, ALU.mult).then_inc(qnorm, 1)
                    if u == IN_UNITS * q + 13:
                        cos = cst[:, C_COS:C_COS + T].unsqueeze(1).broadcast_to([P, n, T])
                        sin = cst[:, C_SIN:C_SIN + T].unsqueeze(1).broadcast_to([P, n, T])
                        dve.wait_ge(qrot, q + 1)
                        dve.tensor_tensor(gbuf[:, 0:n, :], ps[:, 4:4 + n, 0:T], sin, ALU.mult)
                        own(dve.tensor_tensor(qk[:, cs, :], qk[:, cs, :], cos, ALU.mult))
                        dve.tensor_tensor(qk[:, cs, :], qk[:, cs, :], gbuf[:, 0:n, :], ALU.add).then_inc(qk_ready, 1)
                        dve.wait_ge(qk_ready, q + 1)
                i, at = divmod(u - ATT, 4)
                if at == 0 and 1 <= i <= 8:
                    out_lo(i - 1)
                if at == 0 and 0 <= i < 8:
                    row_max(i)
                if at == 1 and 0 <= i < 8:
                    normalise(i)
                if u == 62:
                    for r in range(2):
                        rows = slice(HD * r, HD * (r + 1))
                        ins = dve.tensor_copy(qd[rows, :, :, r, :],
                                              qk[rows, 0:8, TP:T].rearrange("p (q c) b -> p q b c", q=2))
                    ins.then_inc(qd_ok, 1)
                if u == 63:
                    for p in range(2):
                        k = qk[:, 8 + p, TP:T].unsqueeze(1).broadcast_to([P, 4, NB])
                        ins = dve.tensor_tensor(prod[:, 32 * p:32 * p + 32].rearrange("p (c b) -> p c b", c=4),
                                                qk[:, 4 * p:4 * p + 4, TP:T], k, ALU.mult)
                    ins.then_inc(prod_ok, 1)
                if u == 65:
                    dve.wait_ge(sR_done, 1)
                    own(dve.reduce_max(small[:, 48:49], ps[:, 5, 0:P + 1], AX))
                    own(dve.scalar_tensor_tensor(small[:, 49:50], small[:, 48:49], -HD ** -0.5, nsink_col[:, :], ALU.mult, ALU.min))
                    dve.tensor_tensor(small[:, 50:51], small[:, 49:50], sink_col[:, :], ALU.add).then_inc(nS_done, 1)
                if u == 66:
                    dve.wait_ge(eS_done, 1)
                    own(dve.tensor_tensor(small[:, 51:52], small[:, 51:52], small[:, 52:53], ALU.add))
                    own(dve.reciprocal(small[:, 53:54], small[:, 51:52]))
                    own(dve.tensor_scalar(pS[:, 0:P + 1], pS[:, 0:P + 1], small[:, 53:54], None, ALU.mult))
                    dve.tensor_scalar(dg[:, :], dg[:, :], pS[:, P:P + 1], None, ALU.mult).then_inc(pS_ok, 1)
                if u == 68:
                    dve.wait_ge(pvS, 1)
                    dve.wait_ge(pTS_ok, 1)
                    for p in range(2):
                        v = vF[:, p, TP:T].unsqueeze(1).broadcast_to([P, 4, NB])
                        ins = dve.tensor_tensor(prod[:, 32 * p:32 * p + 32].rearrange("p (c b) -> p c b", c=4),
                                                pTS[:, P + 32 * p:P + 32 * p + 32].rearrange("p (c b) -> p c b", c=4), v, ALU.mult)
                    own(ins)
                    for r in range(2):
                        rows = slice(HD * r, HD * (r + 1))
                        mine = ps[rows, 7, 0:P].rearrange("p (q b r c) -> p q r c b", q=2, b=NB, r=2)[:, :, r, :, :]
                        sums = prod[rows, :].rearrange("p (q c b) -> p q c b", q=2, c=4)
                        ins = dve.tensor_tensor(sums, mine, sums, ALU.add)
                    ins.then_inc(oS_ok, 1)
                if u == 69:
                    dve.wait_ge(oh_done, 9)
                    dve.wait_ge(oS_ok, 1)
                    dve.tensor_tensor(yl[:, 0:8, TP:T], prod[:, :].rearrange("p (c b) -> p c b", c=8),
                                      yh[:, 0:8, TP:T].bitcast(F32), ALU.subtract).then_inc(o_done, 1)

            def residual(G, U, c0, i):
                h = (c0 // 4) % 2
                c = dve.snap(i * 8 + c0)
                dve.wait_ge(units_done, at_turn(dve, i, residual.step, U + 1))
                at = bass.ds(c, 4)
                dve.tensor_tensor(x[:, at, :], ps[:, 4 * h:4 * h + 4, 0:T], x[:, at, :], ALU.add).then_inc(evac_g, 1)

            def out_proj(U, G, r0, base):
                residual.step = 2 * IN_UNITS
                with dve.Fori(0, 2, 1) as i:
                    for h in range(2):
                        for j in range(IN_UNITS):
                            split_lo(dve, U + IN_UNITS * h + j + AHEAD, i=i, step=2 * IN_UNITS)
                        residual(G + h, U + IN_UNITS * (h + 1) - 1, 4 * h, i)
                        norm_rest(r0 + h, 4 * h, base, i=i)

            def ffn(layer, U, G, m):
                scale = rstd[:, :].unsqueeze(1).broadcast_to([P, 4, T])
                it = 11 * layer

                def gate_up(i, peeled):
                    for k in range(2 * IN_UNITS):
                        split_lo(dve, U + k + AHEAD, i=i, step=2 * IN_UNITS)
                        if peeled and k == 5:
                            norm_factor(m)
                        if k == IN_UNITS - 1:
                            dve.wait_ge(units_done, at_turn(dve, i, 2 * IN_UNITS, U + IN_UNITS))
                            dve.tensor_tensor(gbuf[:, :, :], ps[:, 0:4, 0:T], scale, ALU.mult).then_inc(evac_g, 1)
                    dve.wait_ge(units_done, at_turn(dve, i, 2 * IN_UNITS, U + 2 * IN_UNITS))
                    dve.tensor_tensor(ubuf[:, :, :], ps[:, 4:8, 0:T], scale, ALU.mult).then_inc(evac_g, 1)
                    evac_g_then = at_turn(dve, i, 2, G + 2)
                    silu_done_then = at_turn(dve, i, 1, it + 1)
                    dve.wait_ge(evac_g, evac_g_then)
                    dve.wait_ge(silu_done, silu_done_then)
                    dve.tensor_tensor(ubuf[:, :, :], ubuf[:, :, :], gbuf[:, :, :], ALU.mult).then_inc(h_ready, 1)
                    at = slice(0, 4) if i is None else bass.ds(dve.snap(i * 4), 4)
                    dve.wait_ge(hh_done, at_turn(dve, i, 1, it + 1))
                    dve.tensor_tensor(hl[:, at, :], ubuf[:, :, :], hh[:, at, :].bitcast(F32), ALU.subtract).then_inc(hid_done, 1)

                gate_up(None, True)
                with dve.Fori(1, GU_ITERS, 1) as i:
                    gate_up(i, False)
                U2, G2 = U + 2 * IN_UNITS * GU_ITERS, G + 2 * GU_ITERS
                residual.step = 2 * DN_UNITS
                if layer == 0:
                    with dve.Fori(0, 2, 1) as i:
                        for h in range(2):
                            for j in range(DN_UNITS):
                                split_lo(dve, U2 + DN_UNITS * h + j + AHEAD, i=i, step=2 * DN_UNITS)
                            residual(G2 + h, U2 + DN_UNITS * (h + 1) - 1, 4 * h, i)
                            norm_rest(8 + h, 4 * h, V_MIX + KC, i=i)
                    return
                for i in range(2):
                    for h in range(2):
                        for j in range(DN_UNITS):
                            split_lo(dve, U2 + DN_UNITS * h + j + AHEAD, i=i, step=2 * DN_UNITS)
                        c = 8 * i + 4 * h
                        stage = (gbuf, ubuf)[h]
                        dve.wait_ge(units_done, U2 + DN_UNITS * (2 * i + h + 1))
                        if i:
                            dve.wait_ge(y_ps, 2)
                        dve.tensor_tensor(stage[:, :, :], ps[:, 4 * h:4 * h + 4, 0:T], x[:, c:c + 4, :],
                                          ALU.add).then_inc(evac_g, 1)

            out_proj(U_OUT_E, G_OUT_E, 4, V_FFN)
            ffn(0, U_FFN0, G_FFN0, 1)

            take.tiles = 3 * EVEN_GROUPS
            group_end = {s0 + (IN_UNITS if c is not None else 2) - 1: q for q, (c, s0) in enumerate(zip(ODD_COLS, ODD_FIRST))}

            def gla_states(h):
                dve.wait_ge(dl_ps, h + 1)
                if h >= 2:
                    dve.wait_ge(go_ps, h - 1)
                    dve.wait_ge(d_go[h % 2], 16)
                own(dve.tensor_copy(st[:, h % 2, 0, :], ps[:, 5, 0:GDV]))
                for n in range(1, NCH):
                    ins = dve.scalar_tensor_tensor(st[:, h % 2, n, :], st[:, h % 2, n - 1, :],
                                                   acc4[:, h, CH * n + CH - 1:CH * n + CH],
                                                   ps[:, 5 + n % 2, (n // 2) * GDV:(n // 2 + 1) * GDV], ALU.mult, ALU.add)
                    if n < NCH - 1:
                        own(ins)
                ins.then_inc(st_ok, 1)

            def dec_state(q):
                b, hp = divmod(q, 2)
                dve.wait_ge(kv_o, q + 1)
                dve.wait_ge(d_gs[q % 4], 16 * (q // 4 + 1))
                for k in range(2):
                    h = 2 * hp + k
                    ins = dve.scalar_tensor_tensor(sgl[:, q % 4, k, :], sgl[:, q % 4, k, :], acc4[:, h, TP + b:TP + b + 1],
                                                   ps[:, 5 + q % 2, k * GDV:(k + 1) * GDV], ALU.mult, ALU.add)
                ins.then_inc(sg_ok, 1)

            def window_means(g):
                w, cp = WIN[g], 2 * (g % 2)
                lvl = (w.bit_length() - 2) % 2
                u = ext[:, cp:cp + 2, PB:PB + TP]
                sm = tree[:, lvl, :, 16 - w:16 - w + TP]
                new = ext[:, cp:cp + 2, 286:399:16]
                cnt = cst[:, C_CNT + 16 * g:C_CNT + 16 * g + 16].unsqueeze(1).broadcast_to([P, 2, 16])
                dve.wait_ge(tree_ok, g + 1)
                dve.wait_ge(pst_ok, g // 2 + 1)
                if g:
                    dve.wait_ge(pm_ps, 2 * g)
                dve.scalar_tensor_tensor(dmix[:, :, 16:TP], sm[:, :, 16:TP], 1.0 / w, u[:, :, 16:TP], ALU.mult, ALU.subtract)
                dve.tensor_tensor(dmix[:, :, 0:16], sm[:, :, 0:16], cnt, ALU.mult)
                own(dve.reduce_sum(small[:, 0:16].rearrange("p (c b) -> p c b", c=2),
                                   ext[:, cp:cp + 2, 271:399].rearrange("p c (b j) -> p c b j", b=NB)[:, :, :, 16 - w:16], AX))
                dve.tensor_tensor(dmix[:, :, 0:16], dmix[:, :, 0:16], u[:, :, 0:16], ALU.subtract)
                dve.scalar_tensor_tensor(dmix[:, :, TP:T], small[:, 0:16].rearrange("p (c b) -> p c b", c=2), 1.0 / w, new,
                                         ALU.mult, ALU.subtract).then_inc(dmix_ok, 1)

            for s in range(U_OUT_O - U_ODD):
                done = U_ODD + s + 1
                q = group_end.get(s)
                if q is None:
                    split_lo(dve, U_ODD + s + AHEAD)
                if s == 5:
                    norm_factor(2)
                if q == 0:
                    take(G_ODD, lambda t: qg[:, t, :], rstd[:, :], done=done)
                if q == 1:
                    dve.wait_ge(units_done, done)
                    dve.tensor_tensor(zr[:, :], ps[0:16, 0, 0:T], rstd[0:16, :], ALU.mult).then_inc(evac_g, 1)
                if q == 2:
                    take(G_ODD + 2, lambda t: kg[:, t, :], rstd[:, :], done=done)
                if q in (3, 4):
                    if q == 4:
                        dve.wait_ge(vt_ps, 1)
                    take(G_ODD + q, lambda t: vf[:, t, :], rstd[:, :], done=done)
                if q in (5, 6):
                    if q == 6:
                        dve.wait_ge(dmix_ok, 2)
                        dve.wait_ge(po_ps, 2)
                    for t in range(4):
                        if t == 3:
                            dve.wait_ge(units_done, done)
                        else:
                            dve.wait_ge(tile_done, take.tiles + t + 1)
                        dve.tensor_tensor(ext[:, t, PB:PB + TP], ps[:, t, 0:TP], rstd[:, 0:TP], ALU.mult)
                        dve.tensor_tensor(ext[:, t, 286:399:16], ps[:, t, TP:T], rstd[:, TP:T], ALU.mult
                                          ).then_inc(evac_g if t == 3 else evac_t, 1)
                    take.tiles += 3
                if q in (7, 8):
                    take(G_ODD + q, lambda t: gbuf[:, t, :], rstd[:, :], done=done)
                if q is not None:
                    split_lo(dve, U_ODD + s + AHEAD)
                if s == 10:
                    dve.wait_ge(gk_ps, 1)
                    for h in range(GH):
                        ins = dve.tensor_scalar(acc4[:, h, :], ps[:, 4 + h, 0:T], vec[:, V_BAL + h:V_BAL + h + 1], None, ALU.add)
                    ins.then_inc(zb_ok, 1)
                    dve.memset(attS[:, :, :], 0.0)
                    dve.memset(v3[:, :].bitcast(F32), 0.0)
                    dve.memset(k3[:, :].bitcast(F32), 0.0).then_inc(pad3_ok, 1)
                if s == 13:
                    dve.wait_ge(ln_ok, 1)
                    dve.wait_ge(zb_ok, 1)
                    own(dve.scalar_tensor_tensor(acc4[:, :, :], acc4[:, :, :], 0.0, sq4[:, :, :], ALU.min, ALU.subtract))
                if s == 14:
                    dve.wait_ge(d0_ok, 3)
                    flat = [z[:, :, :].rearrange("p h t -> p (h t)") for z in (gbuf, d0, acc4)]
                    dve.tensor_tensor_scan(flat[0], flat[1], flat[2], 0.0, ALU.mult, ALU.add).then_inc(b_ok, 1)
                if s == 17:
                    scale = GDK ** -0.5
                    dve.wait_ge(eb_ok, 1)
                    dve.wait_ge(evac_g, G_ODD + 3)
                    dve.wait_ge(b_ok, 1)
                    own(dve.tensor_scalar(qsamp[:, :, :], qg[:, :, TP:T], scale, None, ALU.mult))
                    dve.scalar_tensor_tensor(qg[:, :, :], qg[:, :, :], scale, acc4[:, :, :], ALU.mult, ALU.mult)
                    dve.tensor_tensor(sq4[:, :, :], kg[:, :, :], sq4[:, :, :], ALU.mult).then_inc(kd_ok, 1)
                if s == 18:
                    bb = gbuf[:, :, 0:TP].rearrange("p h (n t) -> p h n t", n=NCH)
                    dve.tensor_tensor(ubuf[:, :, 0:TP].rearrange("p h (n t) -> p h n t", n=NCH),
                                      bb[:, :, :, CH - 1:CH].broadcast_to([P, GH, NCH, CH]), bb, ALU.subtract).then_inc(df_ok, 1)
                if s == 19:
                    dve.wait_ge(edf_ok, 1)
                    dve.tensor_tensor(ubuf[:, :, 0:TP], kg[:, :, 0:TP], ubuf[:, :, 0:TP], ALU.mult).then_inc(k2_ok, 1)
                if s == 20:
                    dve.wait_ge(att_ps, 1)
                    dve.wait_ge(k2_ok, 1)
                    mask = cst[:, C_TRI:C_TRI + CH].bitcast(I32).unsqueeze(1).broadcast_to([P, 8, CH])
                    dve.copy_predicated(attS[:, :, :], mask, ps[:, 4, :].rearrange("p (q c) -> p q c", q=8)).then_inc(att_ok, 1)
                if s == 21:
                    dve.wait_ge(k2t_ok, 1)
                    dve.tensor_tensor(k3[64:K3, :], ps[0:NB, 7, :], k3[0:NB, :].bitcast(F32), ALU.subtract).then_inc(lo3_ok, 1)
                if s in (27, 35):
                    half = (s - 27) // 8
                    cs = slice(half * COLS, (half + 1) * COLS)
                    dve.wait_ge(vt_ok, half + 1)
                    dve.tensor_tensor(v3[32:32 + NB, cs], ps[0:NB, 7, :], v3[0:NB, cs].bitcast(F32), ALU.subtract).then_inc(lo3_ok, 1)
                for k, h in ((28, 0), (30, 1), (36, 2), (38, 3)):
                    if s == k:
                        gla_states(h)
                if s == 39:
                    dve.wait_ge(k2t_ps, 1)
                    dve.wait_ge(vt_ps, 2)
                    dve.wait_ge(k2_ok, 1)
                    dve.memset(ext[:, :, 0:PB], 0.0).then_inc(pad_ok, 1)
                if s == 59:
                    dve.wait_ge(ostd, 1)
                    dve.wait_ge(go_ok, 4)
                    own(refine(vf[:, :, :], ubuf[:, :, :], sq4, vf[:, :, :]))
                if 0 <= s - 40 < 16:
                    dec_state(s - 40)
                for half in range(2):
                    if s == 42 + 8 * half:
                        window_means(2 * half)
                    if 44 + 8 * half <= s < 48 + 8 * half:
                        c = 4 * half + s - 44 - 8 * half
                        dve.wait_ge(pmh, c + 1)
                        dve.scalar_tensor_tensor(yl[:, 8 + c, :], ps[:, 4, 0:T], vec[:, V_PSC + c:V_PSC + c + 1],
                                                 yh[:, 8 + c, :].bitcast(F32), ALU.mult, ALU.subtract).then_inc(pml, 1)
                    if s == 45 + 8 * half:
                        window_means(2 * half + 1)
                    if s == 60 + 2 * half:
                        for t in range(4):
                            c = 4 * half + t
                            ins = dve.scalar_tensor_tensor(oF[:, c, :], oF[:, c, :], vec[:, V_GLA + c % 2:V_GLA + c % 2 + 1],
                                                           vf[:, c // 2, :], ALU.mult, ALU.mult)
                        own(ins)
                    hs = slice(4 * half, 4 * half + 4)
                    if s == (61, 65)[half]:
                        dve.wait_ge(sg_silu, half + 1)
                        dve.tensor_tensor(oF[:, hs, :], oF[:, hs, :], gbuf[:, :, :], ALU.mult).then_inc(oc_ok, 1)
                    if s == (63, 65)[half]:
                        dve.wait_ge(och, half + 1)
                        dve.wait_ge(oc_ok, half + 1)
                        dve.tensor_tensor(yl[:, hs, :], oF[:, hs, :], yh[:, hs, :].bitcast(F32), ALU.subtract).then_inc(ocl, 1)

            out_proj(U_OUT_O, G_OUT_O, 12, V_FFN + KC)
            ffn(1, U_FFN1, G_FFN1, 3)

        @block.gpsimd
        def _(pool):
            steps = [0]

            def own(ins):
                steps[0] += 1
                ins.then_inc(pl, 1)
                pool.wait_ge(pl, steps[0])

            def add_squares(m):
                for g in range(1, 4):
                    pool.wait_ge(sq_done, 4 * m + g + 1)
                    if g > 1:
                        pool.wait_ge(acc_done, 3 * m + g - 1)
                    pool.tensor_tensor(acc4, acc4, sq4, ALU.add).then_inc(acc_done, 1)
                if m == 0:
                    return
                pool.wait_ge(acc_done, 3 * m + 3)
                own(pool.tensor_tensor(acc4[:, 0:2, :], acc4[:, 0:2, :], acc4[:, 2:4, :], ALU.add))
                pool.tensor_tensor(acc4[:, 0, :], acc4[:, 0, :], acc4[:, 1, :], ALU.add).then_inc(acc_sum, 1)

            pool.memset(eps[:, :], EPS).then_inc(ms_done, 1)
            pool.memset(ones[:, :], 1.0).then_inc(ms_done, 1)
            pool.wait_ge(ms_done, 2)
            pool.memset(small[:, :], 0.0).then_inc(y_ok, 2)
            add_squares(0)
            add_squares(1)
            add_squares(2)
            pool.wait_ge(evac_g, G_ODD)
            pool.wait_ge(units_done, U_ODD)
            own(pool.memset(d0[:, :, :], 1.0))
            pool.wait_ge(ms_done, 2)
            pool.memset(d0[:, :, 0:TP:CH], 0.0).then_inc(d0_ok, 2)
            pool.memset(d0[:, :, TP:T], 0.0).then_inc(d0_ok, 1)

            def window_sums(g):
                w, cp = WIN[g], 2 * (g % 2)
                pool.wait_ge(evac_g, G_ODD + 6 + g // 2)
                pool.wait_ge(pad_ok, 1)
                pool.wait_ge(b_ok, 1)
                if g:
                    pool.wait_ge(dmix_ok, g)
                src = ext[:, cp:cp + 2, 0:PB + TP]
                k, n, lvl = 1, PB + TP, 0
                while k < w:
                    n -= k
                    dst = tree[:, lvl, :, 0:n]
                    ins = pool.tensor_tensor(dst, src[:, :, 0:n], src[:, :, k:k + n], ALU.add)
                    k *= 2
                    if k < w:
                        own(ins)
                    src, lvl = dst, 1 - lvl
                ins.then_inc(tree_ok, 1)

            for g in range(4):
                window_sums(g)
            add_squares(3)


_INS = ["x_prompt", "x_sample", "cache_swa_k", "cache_swa_v", "state_conv", "state_gla", "state_pool",
        "norm_mix", "norm_ffn", "w_in_even", "w_out_even", "q_norm", "k_norm", "attn_sinks", "conv_w",
        "w_in_odd", "w_out_odd", "w_alpha_up", "b_alpha", "gla_out_norm", "w_pool", "pool_scale",
        "w_gate", "w_up", "w_down"]
_OUTS = [(1, TP, D), (NB, 1, D), (1, 1, P, NKV, HD), (1, 1, P, NKV, HD), (1, 1, 2, 1024), (1, 1, GH, GDK, GDV),
         (1, 1, PB, 1024), (1, NB, P, NKV, HD), (1, NB, P, NKV, HD), (1, NB, 2, 1024), (1, NB, GH, GDK, GDV),
         (1, NB, PB, 1024)]


def kernel(**inputs):
    import concourse.bacc as bacc
    from concourse.bass_utils import run_bass_kernel_spmd

    arrays = {n: np.ascontiguousarray(inputs[n]) for n in _INS}
    arrays["consts"] = constants()
    arrays["vectors"] = vectors(arrays)
    nc = bacc.Bacc("TRN2", target_bir_lowering=False, num_devices=1, dynamic_dma_scratch_size=256)
    a = {n: nc.dram_tensor(f"in_{n}", v.shape, F32, kind="ExternalInput").ap() for n, v in arrays.items()}
    o = [nc.dram_tensor(f"out_{i}", s, F32, kind="ExternalOutput").ap() for i, s in enumerate(_OUTS)]
    decoder_step(nc, a, o)
    r = run_bass_kernel_spmd(nc, [{f"in_{n}": v for n, v in arrays.items()}], core_ids=[0])
    return tuple(r.results[0][f"out_{i}"] for i in range(len(_OUTS)))
```
